# Optimizing a Trainium2 kernel written in Bass

```python
import jax, jax.numpy as jnp
from jax import lax
import numpy as np

D_MODEL = 1024
BATCH = 1
SEQ = 2048
DEPTH = 1

MEM_LEN = 256
HEAD_DIM = 64
CHUNK = 128
A_GROUPS = 4
A_WIDTH = D_MODEL // 2
A_GROUP_W = A_WIDTH // A_GROUPS
SWA_HEADS = 4
SWA_KV_HEADS = 2
SWA_WIDTH = SWA_HEADS * HEAD_DIM
SWA_KV_WIDTH = SWA_KV_HEADS * HEAD_DIM
WINDOW = 128
MEM_HEADS = 4
MEM_WIDTH = MEM_HEADS * HEAD_DIM
MIX_WIDTH = A_WIDTH + SWA_WIDTH + MEM_WIDTH
IN_WIDTH = 2 * A_WIDTH + SWA_WIDTH + 2 * SWA_KV_WIDTH + MEM_WIDTH + MIX_WIDTH
N_BUCKETS = 32
MAX_DISTANCE = 128
EPS = 1e-6
NEG = -1e30


def rms_norm(x, g):
    xf = x.astype(jnp.float32)
    y = xf * lax.rsqrt(jnp.mean(xf * xf, axis=-1, keepdims=True) + EPS)
    return (y * g.astype(jnp.float32)).astype(x.dtype)

def t5_causal_buckets(dist):
    n = np.maximum(dist, 0)
    max_exact = N_BUCKETS // 2
    large = max_exact + (np.log(np.maximum(n, 1) / max_exact) / np.log(MAX_DISTANCE / max_exact)
                         * (N_BUCKETS - max_exact)).astype(np.int32)
    large = np.minimum(large, N_BUCKETS - 1)
    return np.where(n < max_exact, n, large).astype(np.int32)

def chunked_spatial_gating(u, v, v_g, v_b, w_s, b_s):
    b, s, _ = u.shape
    nc = s // CHUNK
    vg = v.reshape(b, s, A_GROUPS, A_GROUP_W).astype(jnp.float32)
    mu = jnp.mean(vg, axis=-1, keepdims=True)
    var = jnp.mean(jnp.square(vg - mu), axis=-1, keepdims=True)
    vg = (vg - mu) * lax.rsqrt(var + EPS)
    vg = vg * v_g.reshape(A_GROUPS, A_GROUP_W).astype(jnp.float32) + v_b.reshape(A_GROUPS, A_GROUP_W).astype(jnp.float32)
    vc = vg.astype(v.dtype).reshape(b, nc, CHUNK, A_GROUPS, A_GROUP_W)
    causal = jnp.tril(jnp.ones((CHUNK, CHUNK), dtype=w_s.dtype))
    w = w_s * causal[None]
    sv = jnp.einsum('gts,bnsgc->bntgc', w, vc) + b_s.T[None, None, :, :, None]
    return u * sv.reshape(b, s, A_WIDTH)

def sliding_window_attention(q, k, v, sinks, rel_bias):
    b, s, hq, dh = q.shape
    nb = s // CHUNK
    g = hq // SWA_KV_HEADS
    qb = q.reshape(b, nb, CHUNK, SWA_KV_HEADS, g, dh)

    def band(t):
        tb = t.reshape(b, nb, CHUNK, SWA_KV_HEADS, dh)
        prev = jnp.pad(tb, ((0, 0), (1, 0), (0, 0), (0, 0), (0, 0)))[:, :-1]
        return jnp.concatenate([prev, tb], axis=2)

    kb, vb = band(k), band(v)
    logits = jnp.einsum('bnqhgd,bnjhd->bnhgqj', qb, kb).astype(jnp.float32) * (dh ** -0.5)

    qi = np.arange(CHUNK)[:, None]
    kj = np.arange(2 * CHUNK)[None, :]
    dist = qi + CHUNK - kj
    blk = np.arange(nb)[:, None, None]
    valid = (dist >= 0) & (dist < WINDOW) & (blk * CHUNK + kj - CHUNK >= 0)
    buckets = t5_causal_buckets(dist)
    bias = rel_bias.astype(jnp.float32)[buckets]
    bias = jnp.transpose(bias, (2, 0, 1)).reshape(SWA_KV_HEADS, g, CHUNK, 2 * CHUNK)

    logits = jnp.where(valid[None, :, None, None], logits + bias[None, None], NEG)
    sink = sinks.astype(jnp.float32).reshape(1, 1, SWA_KV_HEADS, g, 1, 1)
    m = jnp.maximum(jnp.max(logits, axis=-1, keepdims=True), sink)
    p = jnp.exp(logits - m)
    probs = p / (jnp.sum(p, axis=-1, keepdims=True) + jnp.exp(sink - m))
    out = jnp.einsum('bnhgqj,bnjhd->bnqhgd', probs.astype(v.dtype), vb)
    return out.reshape(b, s, hq * dh)

def memory_cross_attention(q, mem_k, mem_v):
    b, s, h, dh = q.shape
    logits = jnp.einsum('bshd,bmhd->bhsm', q, mem_k).astype(jnp.float32) * (dh ** -0.5)
    probs = jax.nn.softmax(logits, axis=-1)
    out = jnp.einsum('bhsm,bmhd->bshd', probs.astype(mem_v.dtype), mem_v)
    return out.reshape(b, s, h * dh)

def first_inputs(seed: int = 0) -> dict:
    key = jax.random.key(seed)
    ks = jax.random.split(key, 16)
    f32 = jnp.float32
    x = jax.random.normal(ks[0], (BATCH, SEQ, D_MODEL), f32)
    mem = jax.random.normal(ks[1], (BATCH, MEM_LEN, D_MODEL), f32)
    pre_norm_g = 1.0 + 0.05 * jax.random.normal(ks[2], (DEPTH, D_MODEL), f32)
    post_norm_g = 1.0 + 0.05 * jax.random.normal(ks[3], (DEPTH, D_MODEL), f32)
    mem_norm_g = 1.0 + 0.05 * jax.random.normal(ks[4], (DEPTH, D_MODEL), f32)
    w_in = jax.random.normal(ks[5], (DEPTH, D_MODEL, IN_WIDTH), f32) * D_MODEL ** -0.5
    w_mem_kv = jax.random.normal(ks[6], (DEPTH, D_MODEL, 2 * MEM_WIDTH), f32) * D_MODEL ** -0.5
    v_norm_g = 1.0 + 0.05 * jax.random.normal(ks[7], (DEPTH, A_WIDTH), f32)
    v_norm_b = 0.02 * jax.random.normal(ks[8], (DEPTH, A_WIDTH), f32)
    w_spatial = jax.random.normal(ks[9], (DEPTH, A_GROUPS, CHUNK, CHUNK), f32) * CHUNK ** -0.5
    b_spatial = 1.0 + 0.1 * jax.random.normal(ks[10], (DEPTH, A_GROUPS, CHUNK), f32)
    attn_sinks = 0.5 * jax.random.normal(ks[11], (DEPTH, SWA_HEADS), f32)
    rel_bias = 0.5 * jax.random.normal(ks[12], (N_BUCKETS, SWA_HEADS), f32)
    w_out = jax.random.normal(ks[13], (DEPTH, MIX_WIDTH, D_MODEL), f32) * MIX_WIDTH ** -0.5
    return {"x": x, "mem": mem, "pre_norm_g": pre_norm_g, "post_norm_g": post_norm_g,
            "mem_norm_g": mem_norm_g, "w_in": w_in, "w_mem_kv": w_mem_kv,
            "v_norm_g": v_norm_g, "v_norm_b": v_norm_b, "w_spatial": w_spatial,
            "b_spatial": b_spatial, "attn_sinks": attn_sinks, "rel_bias": rel_bias,
            "w_out": w_out}

def first_block(x, mem, pre_norm_g, post_norm_g, mem_norm_g, w_in, w_mem_kv, v_norm_g, v_norm_b,
              w_spatial, b_spatial, attn_sinks, rel_bias, w_out):
    b, s, _ = x.shape
    m_len = mem.shape[1]
    split_at = np.cumsum([A_WIDTH, A_WIDTH, SWA_WIDTH, SWA_KV_WIDTH, SWA_KV_WIDTH, MEM_WIDTH]).tolist()
    for layer in range(DEPTH):
        h = rms_norm(x, pre_norm_g[layer])
        proj = h @ w_in[layer]
        a_u, a_v, sq, sk, sv, mq, z = jnp.split(proj, split_at, axis=-1)

        y_a = chunked_spatial_gating(jax.nn.gelu(a_u), jax.nn.gelu(a_v), v_norm_g[layer],
                                     v_norm_b[layer], w_spatial[layer], b_spatial[layer])

        y_b = sliding_window_attention(sq.reshape(b, s, SWA_HEADS, HEAD_DIM),
                                       sk.reshape(b, s, SWA_KV_HEADS, HEAD_DIM),
                                       sv.reshape(b, s, SWA_KV_HEADS, HEAD_DIM),
                                       attn_sinks[layer], rel_bias)

        mkv = rms_norm(mem, mem_norm_g[layer]) @ w_mem_kv[layer]
        mk, mv = jnp.split(mkv, 2, axis=-1)
        y_c = memory_cross_attention(mq.reshape(b, s, MEM_HEADS, HEAD_DIM),
                                     mk.reshape(b, m_len, MEM_HEADS, HEAD_DIM),
                                     mv.reshape(b, m_len, MEM_HEADS, HEAD_DIM))

        y = jnp.concatenate([y_a, y_b, y_c], axis=-1) * jax.nn.silu(z)
        x = x + rms_norm(y @ w_out[layer], post_norm_g[layer])
    return x


MIX_WIDTH_2 = D_MODEL
MLSTM_WIDTH = D_MODEL // 2
MLSTM_HEADS = 4
MLSTM_HEAD_DIM = MLSTM_WIDTH // MLSTM_HEADS
CHUNK_2 = 64
CONV_WIDTH = 4
POOL_WIDTH = MIX_WIDTH_2 - MLSTM_WIDTH
POOL_WINDOWS = (2, 4, 8, 16)
POOL_GROUP = POOL_WIDTH // len(POOL_WINDOWS)
N_IN = 4 * MLSTM_WIDTH + 2 * MLSTM_HEADS + POOL_WIDTH
XATTN_HEADS = 4
XATTN_HEAD_DIM = D_MODEL // XATTN_HEADS
N_EXPERTS = 16
N_GROUPS = 4
EXPERTS_PER_GROUP = N_EXPERTS // N_GROUPS
TOP_K = 2
D_EXPERT = D_MODEL // 4
MOE_BLOCK = 128
DEEPNORM_ALPHA = (2 * DEPTH) ** 0.25
DEEPNORM_BETA = (8 * DEPTH) ** -0.25
LN_EPS = 1e-5


def layer_norm(x, g, b):
    xf = x.astype(jnp.float32)
    mu = xf.mean(-1, keepdims=True)
    var = jnp.square(xf - mu).mean(-1, keepdims=True)
    return ((xf - mu) * lax.rsqrt(var + LN_EPS) * g + b).astype(x.dtype)

def causal_depthwise_conv(u, w):
    S = u.shape[1]
    K = w.shape[0]
    up = jnp.pad(u, ((0, 0), (K - 1, 0), (0, 0)))
    return sum(up[:, j:j + S] * w[j] for j in range(K))

def mlstm_chunkwise(q, k, v, i_pre, f_pre):
    B, S, H, dh = q.shape
    L = CHUNK_2
    NC = S // L

    def chunk(t):
        t = t.reshape((B, NC, L, H) + t.shape[3:])
        return jnp.moveaxis(t, 3, 1)

    q = chunk(q.astype(jnp.float32)) * dh ** -0.5
    k = chunk(k.astype(jnp.float32))
    v = chunk(v.astype(jnp.float32))
    ig = chunk(i_pre.astype(jnp.float32))
    b = jnp.cumsum(jax.nn.log_sigmoid(chunk(f_pre.astype(jnp.float32))), axis=-1)
    b_last = b[..., -1]

    w_state = b_last[..., None] - b + ig
    m_loc = w_state.max(-1)
    a = jnp.exp(w_state - m_loc[..., None])
    C_loc = jnp.einsum('bhcl,bhcld,bhcle->bhcde', a, k, v)
    n_loc = jnp.einsum('bhcl,bhcld->bhcd', a, k)

    def step(carry, inp):
        C, n, m = carry
        Cl, nl, ml, bl = inp
        m_new = jnp.maximum(bl + m, ml)
        s_old = jnp.exp(bl + m - m_new)
        s_new = jnp.exp(ml - m_new)
        C_new = s_old[..., None, None] * C + s_new[..., None, None] * Cl
        n_new = s_old[..., None] * n + s_new[..., None] * nl
        return (C_new, n_new, m_new), (C, n, m)

    init = (jnp.zeros((B, H, dh, dh), jnp.float32),
            jnp.zeros((B, H, dh), jnp.float32),
            jnp.zeros((B, H), jnp.float32))
    xs = tuple(jnp.moveaxis(t, 2, 0) for t in (C_loc, n_loc, m_loc, b_last))
    _, (C_prev, n_prev, m_prev) = lax.scan(step, init, xs)
    C_prev = jnp.moveaxis(C_prev, 0, 2)
    n_prev = jnp.moveaxis(n_prev, 0, 2)
    m_prev = jnp.moveaxis(m_prev, 0, 2)

    causal = jnp.tril(jnp.ones((L, L), dtype=bool))
    log_d = jnp.where(causal, b[..., :, None] - b[..., None, :] + ig[..., None, :], -jnp.inf)
    log_inter = b + m_prev[..., None]
    m_t = jnp.maximum(log_d.max(-1), log_inter)
    p = jnp.exp(log_d - m_t[..., None]) * jnp.einsum('bhcld,bhcsd->bhcls', q, k)
    inter = jnp.exp(log_inter - m_t)
    num = (jnp.einsum('bhcls,bhcse->bhcle', p, v)
           + inter[..., None] * jnp.einsum('bhcld,bhcde->bhcle', q, C_prev))
    den = p.sum(-1) + inter * jnp.einsum('bhcld,bhcd->bhcl', q, n_prev)
    h = num / jnp.maximum(jnp.abs(den), jnp.exp(-m_t))[..., None]
    return jnp.moveaxis(h, 1, 3).reshape(B, S, H, dh)

def multiscale_pool(u):
    S = u.shape[1]
    pos = jnp.arange(1, S + 1, dtype=jnp.float32)[:, None]
    outs = []
    for g, w in enumerate(POOL_WINDOWS):
        ug = u[..., g * POOL_GROUP:(g + 1) * POOL_GROUP].astype(jnp.float32)
        cs = jnp.cumsum(ug, axis=1)
        lagged = jnp.pad(cs, ((0, 0), (w, 0), (0, 0)))[:, :S]
        outs.append((cs - lagged) / jnp.minimum(pos, w) - ug)
    return jnp.stack(outs, axis=2)

def hybrid_mixer(x, w_in, b_i, b_f, conv_qk, head_norm_g, pool_w, pool_scale, w_out):
    B, S, _ = x.shape
    M, H, dh = MLSTM_WIDTH, MLSTM_HEADS, MLSTM_HEAD_DIM
    z = x @ w_in
    qk = jax.nn.silu(causal_depthwise_conv(z[..., :2 * M], conv_qk))
    q = qk[..., :M].reshape(B, S, H, dh)
    k = qk[..., M:].reshape(B, S, H, dh)
    v = z[..., 2 * M:3 * M].reshape(B, S, H, dh)
    o_pre = z[..., 3 * M:4 * M]
    i_pre = z[..., 4 * M:4 * M + H] + b_i
    f_pre = z[..., 4 * M + H:4 * M + 2 * H] + b_f
    u = z[..., 4 * M + 2 * H:]

    h = mlstm_chunkwise(q, k, v, i_pre, f_pre)
    mu = h.mean(-1, keepdims=True)
    var = jnp.square(h - mu).mean(-1, keepdims=True)
    h = (h - mu) * lax.rsqrt(var + LN_EPS) * head_norm_g.reshape(H, dh).astype(jnp.float32)
    h = h.reshape(B, S, M) * jax.nn.sigmoid(o_pre.astype(jnp.float32))

    pooled = multiscale_pool(u)
    pm = jnp.einsum('bsgc,gcd->bsgd', pooled, pool_w.astype(jnp.float32))
    pm = pm.reshape(B, S, POOL_WIDTH) * pool_scale.astype(jnp.float32)

    mixed = jnp.concatenate([h, pm], axis=-1).astype(x.dtype)
    return mixed @ w_out

def memory_cross_attention_2(x, mem, w_q, w_kv, w_o):
    B, S, D = x.shape
    Mlen = mem.shape[1]
    q = (x @ w_q).reshape(B, S, XATTN_HEADS, XATTN_HEAD_DIM)
    kv = (mem @ w_kv).reshape(B, Mlen, 2, XATTN_HEADS, XATTN_HEAD_DIM)
    s = jnp.einsum('bshd,bmhd->bhsm', q, kv[:, :, 0]).astype(jnp.float32) * XATTN_HEAD_DIM ** -0.5
    p = jax.nn.softmax(s, axis=-1).astype(x.dtype)
    o = jnp.einsum('bhsm,bmhd->bshd', p, kv[:, :, 1]).reshape(B, S, D)
    return o @ w_o

def grouped_moe(x, router_w, router_bias, w_gate, w_up, w_down):
    B, S, D = x.shape
    T = B * S
    A = T * TOP_K
    xt = x.reshape(T, D)
    scores = jax.nn.sigmoid((xt @ router_w).astype(jnp.float32))
    sel = scores + router_bias.astype(jnp.float32)
    grp_score = lax.top_k(sel.reshape(T, N_GROUPS, EXPERTS_PER_GROUP), 2)[0].sum(-1)
    best = jnp.argmax(grp_score, axis=-1)
    in_grp = (jnp.arange(N_EXPERTS) // EXPERTS_PER_GROUP)[None, :] == best[:, None]
    _, idx = lax.top_k(jnp.where(in_grp, sel, -jnp.inf), TOP_K)
    gate = jnp.take_along_axis(scores, idx, axis=-1)
    gate = gate / gate.sum(-1, keepdims=True)

    e = idx.reshape(A).astype(jnp.int32)
    e_sorted, order = lax.sort((e, jnp.arange(A, dtype=jnp.int32)), num_keys=1)
    counts = jnp.bincount(e, length=N_EXPERTS)
    padded = (counts + MOE_BLOCK - 1) // MOE_BLOCK * MOE_BLOCK
    pend = jnp.cumsum(padded)
    pstart = pend - padded
    start = jnp.cumsum(counts) - counts
    dest_sorted = pstart[e_sorted] + jnp.arange(A, dtype=jnp.int32) - start[e_sorted]
    R = A + N_EXPERTS * MOE_BLOCK
    NB = R // MOE_BLOCK
    buf = jnp.zeros((R, D), x.dtype).at[dest_sorted].set(xt[order // TOP_K])
    blk_e = jnp.minimum(jnp.searchsorted(pend, jnp.arange(NB, dtype=jnp.int32) * MOE_BLOCK,
                                         side='right'), N_EXPERTS - 1)

    def expert_block(args):
        xb, ei = args
        hb = jax.nn.silu(xb @ w_gate[ei]) * (xb @ w_up[ei])
        return hb @ w_down[ei]

    yb = lax.map(expert_block, (buf.reshape(NB, MOE_BLOCK, D), blk_e)).reshape(R, D)
    dest = jnp.zeros((A,), jnp.int32).at[order].set(dest_sorted)
    y = (yb[dest].reshape(T, TOP_K, D) * gate[..., None].astype(x.dtype)).sum(1)
    return y.reshape(B, S, D)

def second_inputs(seed: int = 0) -> dict:
    key = jax.random.key(seed)
    ks = jax.random.split(key, 24)
    f32 = jnp.float32
    D, L_ = D_MODEL, DEPTH
    beta = DEEPNORM_BETA
    nrm = lambda k, shape, s: jax.random.normal(k, shape, f32) * s
    col_scale = jnp.asarray(np.concatenate([
        np.ones(2 * MLSTM_WIDTH), np.full(MLSTM_WIDTH, beta), np.ones(MLSTM_WIDTH + 2 * MLSTM_HEADS),
        np.full(POOL_WIDTH, beta)]).astype(np.float32))
    kv_scale = jnp.asarray(np.concatenate([np.ones(D), np.full(D, beta)]).astype(np.float32))
    return {
        "x": nrm(ks[0], (BATCH, SEQ, D), 1.0),
        "mem": nrm(ks[1], (BATCH, MEM_LEN, D), 1.0),
        "w_in": nrm(ks[2], (L_, D, N_IN), D ** -0.5) * col_scale,
        "b_i": nrm(ks[3], (L_, MLSTM_HEADS), 0.1),
        "b_f": jnp.linspace(3.0, 6.0, MLSTM_HEADS, dtype=f32)[None, :] + nrm(ks[4], (L_, MLSTM_HEADS), 0.1),
        "conv_qk": nrm(ks[5], (L_, CONV_WIDTH, 2 * MLSTM_WIDTH), CONV_WIDTH ** -0.5),
        "head_norm_g": 1.0 + nrm(ks[6], (L_, MLSTM_WIDTH), 0.05),
        "pool_w": nrm(ks[7], (L_, len(POOL_WINDOWS), POOL_GROUP, POOL_GROUP), POOL_GROUP ** -0.5),
        "pool_scale": 1.0 + nrm(ks[8], (L_, POOL_WIDTH), 0.1),
        "w_mix_out": nrm(ks[9], (L_, MIX_WIDTH_2, D), MIX_WIDTH_2 ** -0.5 * beta),
        "ln_mix_g": 1.0 + nrm(ks[10], (L_, D), 0.05),
        "ln_mix_b": nrm(ks[11], (L_, D), 0.02),
        "w_xq": nrm(ks[12], (L_, D, D), D ** -0.5),
        "w_xkv": nrm(ks[13], (L_, D, 2 * D), D ** -0.5) * kv_scale,
        "w_xo": nrm(ks[14], (L_, D, D), D ** -0.5 * beta),
        "ln_x_g": 1.0 + nrm(ks[15], (L_, D), 0.05),
        "ln_x_b": nrm(ks[16], (L_, D), 0.02),
        "router_w": nrm(ks[17], (D, N_EXPERTS), D ** -0.5),
        "router_bias": nrm(ks[18], (N_EXPERTS,), 0.01),
        "w_gate": nrm(ks[19], (L_, N_EXPERTS, D, D_EXPERT), D ** -0.5 * beta),
        "w_up": nrm(ks[20], (L_, N_EXPERTS, D, D_EXPERT), D ** -0.5 * beta),
        "w_down": nrm(ks[21], (L_, N_EXPERTS, D_EXPERT, D), D_EXPERT ** -0.5 * beta),
        "ln_moe_g": 1.0 + nrm(ks[22], (L_, D), 0.05),
        "ln_moe_b": nrm(ks[23], (L_, D), 0.02),
    }

def second_block(x, mem, w_in, b_i, b_f, conv_qk, head_norm_g, pool_w, pool_scale, w_mix_out,
              ln_mix_g, ln_mix_b, w_xq, w_xkv, w_xo, ln_x_g, ln_x_b, router_w, router_bias,
              w_gate, w_up, w_down, ln_moe_g, ln_moe_b):
    for l in range(DEPTH):
        mix = hybrid_mixer(x, w_in[l], b_i[l], b_f[l], conv_qk[l], head_norm_g[l],
                           pool_w[l], pool_scale[l], w_mix_out[l])
        x = layer_norm(DEEPNORM_ALPHA * x + mix, ln_mix_g[l], ln_mix_b[l])
        xa = memory_cross_attention_2(x, mem, w_xq[l], w_xkv[l], w_xo[l])
        x = layer_norm(DEEPNORM_ALPHA * x + xa, ln_x_g[l], ln_x_b[l])
        ff = grouped_moe(x, router_w, router_bias, w_gate[l], w_up[l], w_down[l])
        x = layer_norm(DEEPNORM_ALPHA * x + ff, ln_moe_g[l], ln_moe_b[l])
    return x


def setup_inputs(seed=0):
    out = dict(first_inputs(seed))
    for name, value in second_inputs(seed + 1).items():
        if name != "x":
            out[name + "_2"] = value
    return out


def reference(
    x, mem, pre_norm_g, post_norm_g, mem_norm_g, w_in, w_mem_kv, v_norm_g, v_norm_b, w_spatial,
    b_spatial, attn_sinks, rel_bias, w_out, mem_2, w_in_2, b_i_2, b_f_2, conv_qk_2,
    head_norm_g_2, pool_w_2, pool_scale_2, w_mix_out_2, ln_mix_g_2, ln_mix_b_2, w_xq_2, w_xkv_2,
    w_xo_2, ln_x_g_2, ln_x_b_2, router_w_2, router_bias_2, w_gate_2, w_up_2, w_down_2,
    ln_moe_g_2, ln_moe_b_2,
):
    x = first_block(
        x, mem, pre_norm_g, post_norm_g, mem_norm_g, w_in, w_mem_kv, v_norm_g, v_norm_b,
        w_spatial, b_spatial, attn_sinks, rel_bias, w_out,
    )
    return second_block(
        x, mem_2, w_in_2, b_i_2, b_f_2, conv_qk_2, head_norm_g_2, pool_w_2, pool_scale_2,
        w_mix_out_2, ln_mix_g_2, ln_mix_b_2, w_xq_2, w_xkv_2, w_xo_2, ln_x_g_2, ln_x_b_2,
        router_w_2, router_bias_2, w_gate_2, w_up_2, w_down_2, ln_moe_g_2, ln_moe_b_2,
    )


_drawn_inputs = setup_inputs


def setup_inputs(seed=0):
    import zlib

    import numpy as np

    out = dict(_drawn_inputs(seed))
    spreads = {}
    factors = {'mem_norm_g': 7.748,
     'v_norm_g': 9.734,
     'v_norm_b': 26.083,
     'attn_sinks': 49.182,
     'b_i_2': 64.0,
     'head_norm_g_2': 6.259,
     'pool_scale_2': 2.85,
     'router_bias_2': 3.036,
     'ln_moe_b_2': 2.853,
     'b_spatial': 3.306,
     'rel_bias': 4.768}
    for name, (base, spread) in spreads.items():
        noise = np.random.default_rng([zlib.crc32(name.encode()), seed]).standard_normal(out[name].shape)
        drawn = base * np.exp(spread * noise) if base else spread * noise
        out[name] = __import__('jax').numpy.asarray(drawn.astype(out[name].dtype))
    for name, factor in factors.items():
        out[name] = (out[name] * factor).astype(out[name].dtype)
    return out
```

```python
from contextlib import ExitStack

import numpy as np

import concourse.bass as bass
from concourse import mybir

F32 = mybir.dt.float32
I32 = mybir.dt.int32
ALU = mybir.AluOpType
ACT = mybir.ActivationFunctionType
AX = mybir.AxisListType.X

P = 128
S = 2048
D = 1024
NC = S // P
KT = D // P
MEM = 256
EPS = 1e-6
LN_EPS = 1e-5
NEG = -1e30
FAR = 1e30
GELU_C = 0.7978845608028654
GELU_A = 0.044715

A_W = 512
HD = 64
SWA_BUCKETS = 32
IN1 = 2816
QOFF, KOFF, VOFF, MQOFF, ZOFF = 1024, 1280, 1408, 1536, 1792
GROUPS1 = [(0, 512), (512, 512), (1024, 512), (1536, 512), (2048, 512), (2560, 256)]
EXT = 3 * P - 1
MEM_ORDER = (0, 2, 1, 3)

M_W = 512
LH = 4
LD = 128
IN2 = 2568
GATE = 2048
POOL = 2056
CONV = 4
POOL_WINDOWS = (2, 4, 8, 16)
ALPHA = 2.0 ** 0.25
XH = 4
XD = D // XH
NE = 16
NG = 4
EPG = NE // NG
FE = 256
NB = 2 * S // P + NE
LN_TERMS = [1.0 / (2 * k + 1) for k in range(7, 0, -1)]


def t5_buckets(dist):
    n = np.maximum(dist, 0)
    exact = SWA_BUCKETS // 2
    large = exact + (np.log(np.maximum(n, 1) / exact) / np.log(128 / exact) * (SWA_BUCKETS - exact)).astype(np.int32)
    return np.where(n < exact, n, np.minimum(large, SWA_BUCKETS - 1)).astype(np.int32)


def shape_constants():
    t = np.arange(P)
    c = {}
    c["causal"] = (t[None, :] <= t[:, None]) * 1.0
    j = np.arange(2 * P)
    dist = t[:, None] + P - j[None, :]
    c["window"] = np.where((dist >= 0) & (dist < P), 0.0, NEG)
    d = 2 * P - 1 - np.arange(EXT)
    hot = (t5_buckets(d)[None, :] == t[:, None]) & (d >= 0) & (d < P)
    c["bucket"] = hot * 1.0
    return {k: np.ascontiguousarray(v, np.float32) for k, v in c.items()}


def mixer_constants():
    t = np.arange(P)
    back = t[None, :] - t[:, None]
    c = {"pool_cur": [], "pool_prev": [], "pool_first": []}
    for w in POOL_WINDOWS:
        inside = (back >= 0) & (back < w)
        c["pool_cur"].append(inside / w - np.eye(P))
        c["pool_prev"].append((back + P < w) / w)
        c["pool_first"].append(inside / np.minimum(t + 1, w)[None, :] - np.eye(P))
    c = {k: np.concatenate(v, 1) for k, v in c.items()}
    c["after"] = np.where(back >= 0, 0.0, NEG)
    c["head_neg"] = -np.repeat(np.eye(P)[:, 0:LH], P, 1)
    return {k: np.ascontiguousarray(v, np.float32) for k, v in c.items()}


def routing_constants():
    p = np.arange(P)[:, None]
    row = lambda v: np.tile(np.asarray(v, np.float64)[None, :], (P, 1))
    c = {
        "expert": row(np.arange(NE)),
        "group_of": row(np.arange(NE) // EPG),
        "group": row(np.arange(NG)),
        "one": row(np.ones(P)),
        "fills": row(P * np.arange(NC)),
        "block": row(np.arange(NB)),
        "place": row(np.arange(P)),
        "token": np.arange(NC)[None, :] * P + p,
        "before": (p < np.arange(P)[None, :]) * 1.0,
    }
    return {k: np.ascontiguousarray(v, np.float32) for k, v in c.items()}


def layout(tables):
    at, out = 0, {}
    for k, v in tables.items():
        out[k] = (at, v.shape[1])
        at += v.shape[1]
    return out, at


CONST, CONST_W = layout(shape_constants())
CONST2, CONST2_W = layout(mixer_constants())
CONST3, CONST3_W = layout(routing_constants())



class Arena:

    def __init__(self, ap, width):
        self.ap, self.width, self.at = ap, width, 0

    def take(self, *shape):
        n = int(np.prod(shape))
        out = self.ap[:, self.at:self.at + n]
        self.at += n
        assert self.at <= self.width, (self.at, self.width)
        if len(shape) == 2:
            out = out.rearrange("p (a b) -> p a b", a=shape[0])
        if len(shape) == 3:
            out = out.rearrange("p (a b c) -> p a b c", a=shape[0], b=shape[1])
        return out


class Chain:

    def __init__(self, eng, sem):
        self.eng, self.sem, self.base, self.n = eng, sem, 0, 0

    def link(self, ins):
        self.n += 1
        ins.then_inc(self.sem, 1)
        return ins

    def wait(self):
        self.eng.wait_ge(self.sem, self.base + self.n)


def run_chunks(eng, step, chain=None, n=NC, before_last=None):
    pairs = (n - 4) // 2
    before = chain.n if chain else 0
    step(0, 0)
    if chain:
        per, first = chain.n - before, chain.n
    with eng.Fori(0, pairs) as i:
        if chain:
            chain.base, chain.n = i * (2 * per) + first, 0
        step(2 * i + 1, 1)
        step(2 * i + 2, 0)
    if chain:
        assert chain.n == 2 * per, (chain.n, per)
        chain.base, chain.n = 0, first + 2 * per * pairs
    for c in range(n - 3, n):
        if before_last and c == n - 1:
            before_last()
        step(c, c % 2)


def run_thirds(eng, step, chain=None, n=NC):
    threes = (n - 4) // 3
    before = chain.n if chain else 0
    step(0, 0, 0)
    if chain:
        per, first = chain.n - before, chain.n
    with eng.Fori(0, threes) as i:
        if chain:
            chain.base, chain.n = i * (3 * per) + first, 0
        step(3 * i + 1, 1, i)
        step(3 * i + 2, 2, i)
        step(3 * i + 3, 0, i + 1)
    if chain:
        assert chain.n == 3 * per, (chain.n, per)
        chain.base, chain.n = 0, first + 3 * per * threes
    for c in range(n - 3, n):
        step(c, c % 3, c // 3)


def static(c):
    return isinstance(c, int)


def rows(ap, c):
    return ap[c * P:(c + 1) * P, :] if static(c) else ap[bass.ds(c * P, P), :]


def build(nc, t, out, stop_after="all"):
    ctx = ExitStack()
    with ctx:
        def sem(name):
            return ctx.enter_context(nc.semaphore(name))

        def dram(name, shape, dt=F32):
            return nc.dram_tensor(name, shape, dt, kind="Internal").ap()

        SB = 53000
        arena = ctx.enter_context(nc.sbuf_tensor("arena", [P, SB], F32))
        psum = ctx.enter_context(nc.psum_tensor("psum", [P, 8, 512], F32))


        s_half = sem("neg_half_written")

        waited = sem("waited")

        def settled(eng):
            eng.sem_inc(waited, 1)

        x1_d = out if stop_after == "a" else dram("x1_scratch", [S, D])
        ext_d = dram("bias_scratch", [4, P * EXT])

        m = Arena(arena[:, :], SB)
        ident = m.take(P)
        chip_const = m.take(4)
        neg_half = chip_const

        shared_end = m.at

        W = m.take(KT * (IN1 + D))
        w_in = W[:, 0:KT * IN1].rearrange("p (k n) -> p k n", k=KT)
        w_out = W[:, KT * IN1:].rearrange("p (k n) -> p k n", k=KT)
        w_kv = W[:, KT * IN1:KT * IN1 + KT * 512].rearrange("p (k n) -> p k n", k=KT)
        x_in = m.take(D)
        x_res = m.take(D)
        xn = m.take(D)
        xT = m.take(KT, P)
        proj = m.take(2, IN1)
        free_end_a = m.at - IN1
        v_win = m.take(2, P)
        tmp = m.take(D)
        qT = m.take(2, P)
        kT = m.take(2, P)
        mqT = m.take(2, P)
        prob = m.take(4, 2 * P)
        pT = m.take(KT, P)
        tables = pT.rearrange("p a b -> p (a b)")[:, 0:CONST_W]

        def cst(name):
            o, n = CONST[name]
            return tables[:, o:o + n]

        out_stage = m.take(2 * D)
        o_sb = out_stage[:, 0:D]
        junk = out_stage[:, D:2 * D]
        ext_rows = out_stage[:, 0:4 * EXT].rearrange("p (h i) -> p h i", h=4)
        bias = m.take(4, 2 * P)
        g_pre = m.take(D)
        g_post = m.take(D)
        vn_g = m.take(A_W)
        vn_b = m.take(A_W)
        wsT = m.take(4, P)
        mkT = m.take(2, MEM)
        mv = m.take(2, MEM)
        bsT = m.take(4)
        sink = m.take(4)
        relb = m.take(4)
        x_ms, x_rstd = m.take(1), m.take(1)
        o_ss, o_ms, o_rstd = m.take(2), m.take(1), m.take(1)
        swa_max, swa_nmax, sink_arg, sink_exp = m.take(4), m.take(4), m.take(4), m.take(4)
        swa_sum, swa_rden = m.take(4), m.take(4)
        mem_max, mem_nmax, mem_sum, mem_rden = m.take(4), m.take(4), m.take(4), m.take(4)
        v_stats, v_mv, v_var, v_rstd = m.take(4, 6), m.take(4, 2), m.take(4), m.take(4)

        mem_rows = proj[:, 0, 0:2 * D].rearrange("p (a n) -> p a n", a=2)
        memT = proj[:, 1, 0:2 * D].rearrange("p (k n) -> p k n", k=KT)
        mem_g = x_res

        pj = [psum[:, 0, :], psum[:, 1, :]]
        tp = psum[:, 2:4, :].rearrange("p b (a n) -> p (b a) n", a=4)
        lg = psum[:, 4:6, :].rearrange("p b (a n) -> p (b a) n", a=2)
        sgu = psum[:, 6, :].rearrange("p (a n) -> p a n", a=4)
        pv = psum[:, 7, :].rearrange("p (a n) -> p a n", a=8)
        pv2 = psum[:, 6, :].rearrange("p (a n) -> p a n", a=8)

        s_const = sem("a_const_loaded")
        s_wkv = sem("a_w_kv_loaded")
        s_win = [sem(f"a_w_in_loaded{g}") for g in range(len(GROUPS1))]
        s_wout = sem("a_w_out_loaded")
        s_ws = sem("a_spatial_masked")
        s_rel = sem("a_rel_bias_spread")
        s_extp = sem("a_bias_product")
        s_exts = sem("a_bias_rows_ready")
        s_ext_st = sem("a_bias_stored")
        s_ext_ld = sem("a_bias_loaded")
        s_memms, s_memr, s_memn = sem("a_mem_meansq"), sem("a_mem_rstd"), sem("a_mem_normed")
        s_mkv, s_mkvt = sem("a_mem_kv_product"), sem("a_mem_kv_taken")
        s_pad = sem("a_window_padded")
        s_xin, s_xres = sem("a_x_in_loaded"), sem("a_x_res_loaded")
        s_xms, s_xrs, s_xn = sem("a_x_meansq"), sem("a_x_rstd"), sem("a_x_normed")
        s_tp, s_tpf = sem("a_turned"), sem("a_turned_taken")
        s_pj, s_pjf = sem("a_proj_done"), sem("a_proj_taken")
        s_gsq, s_garg, s_gth, s_gel = sem("a_gelu_square"), sem("a_gelu_arg"), sem("a_gelu_tanh"), sem("a_gelu_ready")
        s_vvar, s_vrs, s_vn = sem("a_v_var"), sem("a_v_rstd"), sem("a_v_normed")
        s_qk = sem("a_queries_keys_ready")
        s_zth, s_z = sem("a_z_tanh"), sem("a_z_ready")
        s_sgu, s_ya = sem("a_spatial_done"), sem("a_spatial_taken")
        s_lg, s_lgf = sem("a_logits_done"), sem("a_window_logits_taken")
        s_nm, s_ex = sem("a_window_max"), sem("a_window_exp")
        s_nm2, s_ex2 = sem("a_memory_max"), sem("a_memory_exp")
        s_pv, s_y = sem("a_values_done"), sem("a_y_ready")
        s_o, s_oms, s_ors, s_x1 = sem("a_out_taken"), sem("a_out_meansq"), sem("a_out_rstd"), sem("a_x1_ready")
        s_x1st = sem("a_x1_stored")
        s_dve = sem("vector_chain")

        N_CONST = 12

        def tp_at(c, n):
            return c * 5 + (4 + n)

        def pj_at(c, n):
            return c * 8 + (6 + n)

        def a_sync(sp, before_last):
            sp.dma_start(ident, t["ident"]).then_inc(s_const, 16)
            sp.dma_start(tables, t["tables"]).then_inc(s_const, 16)
            sp.dma_start(mem_rows, t["mem"].rearrange("(a p) n -> p a n", p=P)).then_inc(s_const, 16)
            for dst, name in ((mem_g, "mem_norm_g"), (g_pre, "pre_norm_g"), (g_post, "post_norm_g"), (vn_g, "v_norm_g"),
                              (vn_b, "v_norm_b"), (sink, "attn_sinks")):
                sp.dma_start(dst, t[name].partition_broadcast(P)).then_inc(s_const, 16)
            sp.dma_start(wsT, t["w_spatial"].rearrange("g t s -> t g s")).then_inc(s_const, 16)
            sp.dma_start(relb[0:SWA_BUCKETS, :], t["rel_bias"]).then_inc(s_const, 16)
            with nc.allow_non_contiguous_dma(reason="512 values once"):
                sp.dma_start(bsT, t["b_spatial"].rearrange("g t -> t g")).then_inc(s_const, 16)
            sp.dma_start(x_in, rows(t["x"], 0)).then_inc(s_xin, 16)
            sp.dma_start(w_kv, t["w_mem_kv"].rearrange("(k p) n -> p k n", p=P)).then_inc(s_wkv, 16)
            for g, (o, n) in enumerate(GROUPS1):
                sp.dma_start(w_in[:, :, o:o + n], t["w_in"].rearrange("(k p) n -> p k n", p=P)[:, :, o:o + n])\
                  .then_inc(s_win[g], 16)
            sp.wait_ge(s_exts, 1)
            sp.dma_start(ext_d.rearrange("h (q i) -> q h i", i=EXT), ext_rows).then_inc(s_ext_st, 16)
            sp.wait_ge(s_ext_st, 16)
            sp.dma_start(bias, bass.AP(ext_d.tensor, P - 1, [[EXT - 1, P], [P * EXT, 4], [1, 2 * P]])).then_inc(s_ext_ld, 16)
            sp.wait_ge(s_mkv, 2)
            sp.dma_start(w_out, t["w_out"].rearrange("(k p) n -> p k n", p=P)).then_inc(s_wout, 16)
            sp.wait_ge(s_xn, 1)
            sp.dma_start(x_in, rows(t["x"], 1)).then_inc(s_xin, 16)
            sp.wait_ge(s_memn, 2)
            sp.dma_start(x_res, rows(t["x"], 0)).then_inc(s_xres, 16)

            def step(c, par):
                if not static(c) or c + 2 < NC:
                    sp.wait_ge(s_xn, c + 2)
                    sp.dma_start(x_in, rows(t["x"], c + 2)).then_inc(s_xin, 16)
                sp.wait_ge(s_x1, c + 1)
                sp.dma_start(rows(x1_d, c), o_sb).then_inc(s_x1st, 16)
                if not static(c) or c + 1 < NC:
                    sp.dma_start(x_res, rows(t["x"], c + 1)).then_inc(s_xres, 16)

            run_chunks(sp, step, before_last=before_last)

        def a_sync_end(sp):
            sp.wait_ge(s_x1st, 16 * NC)

        def a_tensor(pe):
            def turn(src, at):
                if not static(at) or at:
                    pe.wait_ge(s_tpf, at)
                for i, tile in enumerate(src):
                    ins = nc.tensor.transpose(tp[:, i, :], tile, ident)
                ins.then_inc(s_tp, 1)

            def tiles(ap, n):
                return [ap[:, k * P:(k + 1) * P] for k in range(n)]

            def front(c, at):
                pe.wait_ge(s_xn, c + 1)
                turn(tiles(xn, KT), at)

            def group(c, g, at):
                o, n = GROUPS1[g]
                if not static(at) or at >= 2:
                    pe.wait_ge(s_pjf, at - 1)
                if static(c) and c == 0:
                    pe.wait_ge(s_win[g], 16)
                for k in range(KT):
                    ins = nc.tensor.matmul(pj[g % 2][:, 0:n], xT[:, k, :], w_in[:, k, o:o + n],
                                           start=(k == 0), stop=(k == KT - 1))
                ins.then_inc(s_pj, 1)

            pe.wait_ge(s_ws, 1)
            turn([wsT[:, g, :] for g in range(4)], 0)
            pe.wait_ge(s_rel, 1)
            for h in range(4):
                ins = nc.tensor.matmul(psum[:, 4 + h, 0:EXT], tmp[0:SWA_BUCKETS, h * P:(h + 1) * P],
                                       cst("bucket")[0:SWA_BUCKETS, :], start=True, stop=True)
            ins.then_inc(s_extp, 1)
            for a in range(2):
                pe.wait_ge(s_memn, a + 1)
                turn(tiles(mem_rows[:, a, :], KT), 1 + a)
            pe.wait_ge(s_tpf, 3)
            pe.wait_ge(s_wkv, 16)
            pe.wait_ge(s_exts, 1)
            for a in range(2):
                for k in range(KT):
                    ins = nc.tensor.matmul(psum[:, 4, a * MEM:(a + 1) * MEM], w_kv[:, k, a * P:(a + 1) * P], memT[:, k, :],
                                           start=(k == 0), stop=(k == KT - 1))
            ins.then_inc(s_mkv, 1)
            for a in range(2):
                for k in range(KT):
                    ins = nc.tensor.matmul(psum[:, 5, a * MEM:(a + 1) * MEM], memT[:, k, a * P:(a + 1) * P],
                                           w_kv[:, k, MEM:2 * MEM], start=(k == 0), stop=(k == KT - 1))
            ins.then_inc(s_mkv, 1)
            front(0, 3)
            pe.wait_ge(s_tpf, 4)
            for g in range(6):
                group(0, g, g)
            pe.wait_ge(s_mkvt, 2)
            pe.wait_ge(s_pad, 1)

            def step(c, par):
                nxt = not static(c) or c + 1 < NC
                pr = proj[:, par, :]
                n = 0
                if nxt:
                    front(c + 1, tp_at(c, 0))
                    n = 1
                pe.wait_ge(s_qk, c + 1)
                turn(tiles(pr[:, QOFF:], 3) + tiles(pr[:, MQOFF:], 2), tp_at(c, n))
                pe.wait_ge(s_vn, c + 1)
                if not static(c) or c:
                    pe.wait_ge(s_ya, c)
                for g in range(4):
                    ins = nc.tensor.matmul(sgu[:, g, :], wsT[:, g, :], pr[:, A_W + g * P:A_W + (g + 1) * P],
                                           start=True, stop=True)
                ins.then_inc(s_sgu, 1)
                pe.wait_ge(s_tpf, tp_at(c, n) + 1)
                if nxt:
                    group(c + 1, 0, pj_at(c, 0))
                if not static(c) or c:
                    pe.wait_ge(s_ex2, c)
                for h in range(4):
                    half = slice(HD * (h // 2), HD * (h // 2) + HD)
                    ins = nc.tensor.matmul(lg[:, h, :], qT[half, h % 2, :], kT[half, :, :], start=True, stop=True)
                ins.then_inc(s_lg, 1)
                if nxt:
                    group(c + 1, 1, pj_at(c, 1))
                pe.wait_ge(s_lgf, c + 1)
                for i, h in enumerate(MEM_ORDER):
                    half = slice(HD * (h % 2), HD * (h % 2) + HD)
                    ins = nc.tensor.matmul(lg[:, i, :], mqT[half, h // 2, :], mkT[half, h // 2, :], start=True, stop=True)
                ins.then_inc(s_lg, 1)
                if nxt:
                    group(c + 1, 2, pj_at(c, 2))
                n += 1
                pe.wait_ge(s_ex, c + 1)
                turn([prob[:, h, b * P:(b + 1) * P] for h in range(4) for b in range(2)], tp_at(c, n))
                if nxt:
                    group(c + 1, 3, pj_at(c, 3))
                pe.wait_ge(s_tpf, tp_at(c, n) + 1)
                if not static(c) or c:
                    pe.wait_ge(s_y, c)
                for h in range(4):
                    kv = h // 2
                    for b in range(2):
                        ins = nc.tensor.matmul(pv[:, h, :], pT[:, 2 * h + b, :], v_win[:, b, kv * HD:(kv + 1) * HD],
                                               start=(b == 0), stop=(b == 1))
                ins.then_inc(s_pv, 1)
                n += 1
                pe.wait_ge(s_ex2, c + 1)
                turn([prob[:, h, b * P:(b + 1) * P] for h in range(4) for b in range(2)], tp_at(c, n))
                if nxt:
                    group(c + 1, 4, pj_at(c, 4))
                pe.wait_ge(s_tpf, tp_at(c, n) + 1)
                pe.wait_ge(s_ya, c + 1)
                for i, h in enumerate(MEM_ORDER):
                    for b in range(2):
                        ins = nc.tensor.matmul(pv2[:, h, :], pT[:, 2 * i + b, :], mv[:, b, h * HD:(h + 1) * HD],
                                               start=(b == 0), stop=(b == 1))
                ins.then_inc(s_pv, 1)
                if nxt:
                    group(c + 1, 5, pj_at(c, 5))
                n += 1
                pe.wait_ge(s_y, c + 1)
                turn(tiles(pr, KT), tp_at(c, n))
                pe.wait_ge(s_tpf, tp_at(c, n) + 1)
                if static(c) and c == 0:
                    pe.wait_ge(s_wout, 16)
                for j in range(2):
                    at = pj_at(c, (6 if nxt else 0) + j)
                    pe.wait_ge(s_pjf, at - 1)
                    for k in range(KT):
                        ins = nc.tensor.matmul(pj[j], pT[:, k, :], w_out[:, k, j * 512:(j + 1) * 512],
                                               start=(k == 0), stop=(k == KT - 1))
                    ins.then_inc(s_pj, 1)

            run_chunks(pe, step)

        def a_scalar(act):
            def copy(dst, src, scale=1.0):
                return nc.scalar.activation(dst, src, ACT.Copy, scale=scale)

            def take_tiles(dst, at):
                act.wait_ge(s_tp, at + 1)
                copy(dst[:, 0:4, :], tp[:, 0:4, :])
                copy(dst[:, 4:8, :], tp[:, 4:8, :]).then_inc(s_tpf, 1)

            def take_gelu(c, par, g, at):
                o, n = GROUPS1[g]
                act.wait_ge(s_pj, at + 1)
                copy(proj[:, par, o:o + n], pj[g % 2][:, 0:n], 0.5)
                nc.scalar.activation(tmp[:, o:o + n], pj[g % 2][:, 0:n], ACT.Square).then_inc(s_pjf, 1)

            def take_qkv(c, par, at):
                pr = proj[:, par, :]
                act.wait_ge(s_pj, at + 1)
                q_in = pj[0][:, 0:4 * HD].rearrange("p (a b d) -> p b a d", a=2, b=2)
                q_out = pr[:, QOFF:QOFF + 4 * HD].rearrange("p (b a d) -> p b a d", b=2, a=2)
                copy(q_out, q_in, HD ** -0.5)
                copy(pr[:, KOFF:KOFF + 2 * P], pj[0][:, 4 * HD:4 * HD + 2 * P]).then_inc(s_pjf, 1)

            def take_z(par, o, n, ps):
                copy(proj[:, par, ZOFF + o:ZOFF + o + n], ps, 0.5)
                return nc.scalar.activation(tmp[:, o:o + n], ps, ACT.Tanh, scale=0.5)

            def take_mq_z(c, par, at):
                act.wait_ge(s_pj, at + 1)
                copy(proj[:, par, MQOFF:MQOFF + MEM], pj[1][:, 0:MEM], HD ** -0.5).then_inc(s_qk, 1)
                act.wait_ge(s_gel, c + 1)
                take_z(par, 0, 256, pj[1][:, MEM:2 * MEM]).then_inc(s_pjf, 1)

            def gelu_tanh(c):
                act.wait_ge(s_garg, c + 1)
                nc.scalar.activation(tmp, tmp, ACT.Tanh, scale=GELU_C).then_inc(s_gth, 1)

            act.wait_ge(s_tp, 1)
            copy(wsT, tp[:, 0:4, :]).then_inc(s_tpf, 1)
            act.wait_ge(s_extp, 1)
            copy(ext_rows, psum[:, 4:8, 0:EXT]).then_inc(s_exts, 1)
            for a in range(2):
                act.wait_ge(s_tp, 2 + a)
                copy(memT[:, 0:4, a * P:(a + 1) * P], tp[:, 0:4, :])
                copy(memT[:, 4:8, a * P:(a + 1) * P], tp[:, 4:8, :]).then_inc(s_tpf, 1)
            act.wait_ge(s_mkv, 1)
            copy(mkT, psum[:, 4, :].rearrange("p (a n) -> p a n", a=2)).then_inc(s_mkvt, 1)
            act.wait_ge(s_mkv, 2)
            copy(mv, psum[:, 5, :].rearrange("p (a n) -> p a n", a=2)).then_inc(s_mkvt, 1)
            take_tiles(xT, 3)
            take_gelu(0, 0, 0, 0)
            take_gelu(0, 0, 1, 1)
            gelu_tanh(0)
            take_qkv(0, 0, 2)
            take_mq_z(0, 0, 3)
            act.wait_ge(s_pj, 5)
            take_z(0, 256, 512, pj[0]).then_inc(s_pjf, 1)
            act.wait_ge(s_pj, 6)
            take_z(0, 768, 256, pj[1][:, 0:256]).then_inc(s_pjf, 1)

            def step(c, par):
                nxt = not static(c) or c + 1 < NC
                npar = 1 - par
                n = 0
                if nxt:
                    take_tiles(xT, tp_at(c, 0))
                    n = 1
                act.wait_ge(s_tp, tp_at(c, n) + 1)
                copy(qT, tp[:, 0:2, :])
                copy(kT[:, par, :], tp[:, 2, :])
                copy(v_win[:, par, :], proj[:, par, VOFF:VOFF + P])
                copy(mqT, tp[:, 3:5, :]).then_inc(s_tpf, 1)
                if nxt:
                    act.wait_ge(s_z, c + 1)
                    take_gelu(c + 1, npar, 0, pj_at(c, 0))
                    take_gelu(c + 1, npar, 1, pj_at(c, 1))
                act.wait_ge(s_nm, c + 1)
                for h in range(4):
                    nc.scalar.activation(prob[:, h, :], prob[:, h, :], ACT.Exp, bias=swa_nmax[:, h:h + 1],
                                         accum_out=swa_sum[:, h:h + 1])
                nc.scalar.activation(sink_exp, sink_arg, ACT.Exp).then_inc(s_ex, 1)
                if nxt:
                    gelu_tanh(c + 1)
                    take_qkv(c + 1, npar, pj_at(c, 2))
                n += 1
                take_tiles(pT, tp_at(c, n))
                act.wait_ge(s_nm2, c + 1)
                for h in range(4):
                    ins = nc.scalar.activation(prob[:, h, :], lg[:, h, :], ACT.Exp, bias=mem_nmax[:, h:h + 1],
                                               accum_out=mem_sum[:, h:h + 1])
                ins.then_inc(s_ex2, 1)
                if nxt:
                    take_mq_z(c + 1, npar, pj_at(c, 3))
                n += 1
                take_tiles(pT, tp_at(c, n))
                if nxt:
                    act.wait_ge(s_pj, pj_at(c, 4) + 1)
                    take_z(npar, 256, 512, pj[0]).then_inc(s_pjf, 1)
                    act.wait_ge(s_pj, pj_at(c, 5) + 1)
                    take_z(npar, 768, 256, pj[1][:, 0:256]).then_inc(s_pjf, 1)
                n += 1
                take_tiles(pT, tp_at(c, n))
                if not static(c) or c:
                    act.wait_ge(s_x1st, c * 16)
                for j in range(2):
                    act.wait_ge(s_pj, pj_at(c, (6 if nxt else 0) + j) + 1)
                    copy(o_sb[:, j * 512:(j + 1) * 512], pj[j])
                    ins = nc.scalar.activation(junk[:, j * 512:(j + 1) * 512], pj[j], ACT.Square, accum_out=o_ss[:, j:j + 1])
                    ins.then_inc(s_pjf, 1)
                    

            run_chunks(act, step)

        def a_vector(dve, ch):
            def gelu_arg(c, par, done):
                dve.wait_ge(s_pjf, done)
                ch.link(nc.vector.tensor_scalar(tmp, tmp, 2 * GELU_A, 2.0, ALU.mult, ALU.add))
                ch.wait()
                nc.vector.tensor_tensor(tmp, tmp, proj[:, par, 0:D], ALU.mult).then_inc(s_garg, 1)

            def gelu_end(c, par):
                pr = proj[:, par, :]
                v = pr[:, A_W:2 * A_W]
                dve.wait_ge(s_gth, c + 1)
                nc.vector.scalar_tensor_tensor(pr[:, 0:D], tmp, 1.0, pr[:, 0:D], ALU.add, ALU.mult).then_inc(s_gel, 1)
                dve.wait_ge(s_gel, c + 1)
                for g in range(4):
                    ins = nc.vector.bn_stats(v_stats[:, g, :], v[:, g * P:(g + 1) * P])
                ch.link(ins)
                ch.wait()
                settled(dve)
                for g in range(4):
                    ins = nc.vector.bn_aggr(v_mv[:, g, :], v_stats[:, g, :])
                ch.link(ins)
                ch.wait()
                nc.vector.tensor_scalar(v_var, v_mv[:, :, 1], EPS, None, ALU.add).then_inc(s_vvar, 1)
                dve.wait_ge(s_vrs, c + 1)
                for g in range(4):
                    vg = v[:, g * P:(g + 1) * P]
                    ins = nc.vector.tensor_scalar(vg, vg, v_mv[:, g, 0:1], v_rstd[:, g:g + 1], ALU.subtract, ALU.mult)
                ch.link(ins)
                ch.wait()
                ch.link(nc.vector.tensor_tensor(v, v, vn_g, ALU.mult))
                ch.wait()
                nc.vector.tensor_tensor(v, v, vn_b, ALU.add).then_inc(s_vn, 1)

            def z_end(c, par, done):
                dve.wait_ge(s_pjf, done)
                z = proj[:, par, ZOFF:ZOFF + D]
                nc.vector.scalar_tensor_tensor(z, tmp, 1.0, z, ALU.add, ALU.mult).then_inc(s_z, 1)

            def norm_x(c, turned):
                dve.wait_ge(s_xin, c * 16 + 16)
                if turned is not None:
                    dve.wait_ge(s_tp, turned + 1)
                nc.vector.tensor_tensor_reduce(xn, x_in, x_in, 1.0 / D, EPS, ALU.mult, ALU.add, x_ms).then_inc(s_xms, 1)
                dve.wait_ge(s_xrs, c + 1)
                nc.vector.scalar_tensor_tensor(xn, x_in, x_rstd, g_pre, ALU.mult, ALU.mult).then_inc(s_xn, 1)

            nc.vector.memset(kT, 0.0)
            nc.vector.memset(v_win, 0.0).then_inc(s_pad, 1)
            dve.wait_ge(s_const, 16 * N_CONST)
            nc.vector.tensor_tensor(wsT, wsT, cst("causal").unsqueeze(1).to_broadcast([P, 4, P]), ALU.mult).then_inc(s_ws, 1)
            nc.vector.tensor_copy(tmp[0:SWA_BUCKETS, 0:4 * P].rearrange("p (h n) -> p h n", h=4),
                                  relb[0:SWA_BUCKETS, :].unsqueeze(2).to_broadcast([SWA_BUCKETS, 4, P])).then_inc(s_rel, 1)
            for a in range(2):
                nc.vector.tensor_tensor_reduce(proj[:, 1, a * D:(a + 1) * D], mem_rows[:, a, :], mem_rows[:, a, :], 1.0 / D, EPS, ALU.mult, ALU.add,
                                               o_ss[:, a:a + 1]).then_inc(s_memms, 1)
            for a in range(2):
                dve.wait_ge(s_memr, a + 1)
                nc.vector.scalar_tensor_tensor(mem_rows[:, a, :], mem_rows[:, a, :], mem_max[:, a:a + 1], mem_g,
                                               ALU.mult, ALU.mult).then_inc(s_memn, 1)
            norm_x(0, None)
            dve.wait_ge(s_ext_ld, 16)
            ch.link(nc.vector.tensor_tensor(bias, bias, cst("window").unsqueeze(1).to_broadcast([P, 4, 2 * P]), ALU.add))
            norm_x(1, 3)
            gelu_arg(0, 0, 2)
            gelu_end(0, 0)
            z_end(0, 0, 6)

            def step(c, par):
                nxt = not static(c) or c + 1 < NC
                npar = 1 - par
                pr = proj[:, par, :]
                z = pr[:, ZOFF:ZOFF + D]
                dve.wait_ge(s_sgu, c + 1)
                dve.wait_ge(s_z, c + 1)
                for g in range(4):
                    u = pr[:, g * P:(g + 1) * P]
                    ins = nc.vector.scalar_tensor_tensor(u, sgu[:, g, :], bsT[:, g:g + 1], u, ALU.add, ALU.mult)
                ins.then_inc(s_ya, 1)
                if not static(c) or c + 2 < NC:
                    norm_x(c + 2, tp_at(c, 0))
                dve.wait_ge(s_lg, c * 2 + 1)
                ch.wait()
                for b in (1 - par, par):
                    cols = slice(b * P, (b + 1) * P)
                    side = slice(P, 2 * P) if b == par else slice(0, P)
                    if static(c) and c == 0 and b != par:
                        ins = nc.vector.memset(prob[:, :, cols], NEG)
                    else:
                        ins = nc.vector.tensor_tensor(prob[:, :, cols], lg[:, :, cols], bias[:, :, side], ALU.add)
                ins.then_inc(s_lgf, 1)
                dve.wait_ge(s_lgf, c + 1)
                ch.link(nc.vector.tensor_reduce(swa_max, prob, AX, ALU.max))
                ch.wait()
                ch.link(nc.vector.tensor_tensor(swa_max, swa_max, sink, ALU.max))
                ch.wait()
                nc.vector.tensor_tensor(sink_arg, sink, swa_max, ALU.subtract)
                nc.vector.tensor_scalar(swa_nmax, swa_max, -1.0, None, ALU.mult).then_inc(s_nm, 1)
                if nxt:
                    gelu_arg(c + 1, npar, pj_at(c, 2))
                dve.wait_ge(s_lg, c * 2 + 2)
                ch.link(nc.vector.tensor_reduce(mem_max, lg, AX, ALU.max))
                ch.wait()
                nc.vector.tensor_scalar(mem_nmax, mem_max, -1.0, None, ALU.mult).then_inc(s_nm2, 1)
                dve.wait_ge(s_ex, c + 1)
                ch.link(nc.vector.tensor_tensor(swa_sum, swa_sum, sink_exp, ALU.add))
                ch.wait()
                ch.link(nc.vector.reciprocal(swa_rden, swa_sum))
                if nxt:
                    gelu_end(c + 1, npar)
                dve.wait_ge(s_ya, c + 1)
                nc.vector.tensor_tensor(pr[:, 0:A_W], pr[:, 0:A_W], z[:, 0:A_W], ALU.mult)
                dve.wait_ge(s_pv, c * 2 + 1)
                ch.wait()
                for h in range(4):
                    o = A_W + h * HD
                    nc.vector.scalar_tensor_tensor(pr[:, o:o + HD], pv[:, h, :], swa_rden[:, h:h + 1], z[:, o:o + HD],
                                                   ALU.mult, ALU.mult)
                dve.wait_ge(s_ex2, c + 1)
                ch.link(nc.vector.reciprocal(mem_rden, mem_sum))
                ch.wait()
                dve.wait_ge(s_pv, c * 2 + 2)
                for i, h in enumerate(MEM_ORDER):
                    o = A_W + 4 * HD + h * HD
                    ins = nc.vector.scalar_tensor_tensor(pr[:, o:o + HD], pv2[:, h, :], mem_rden[:, i:i + 1], z[:, o:o + HD],
                                                         ALU.mult, ALU.mult)
                ins.then_inc(s_y, 1)
                if nxt:
                    z_end(c + 1, npar, pj_at(c, 6))
                dve.wait_ge(s_pjf, pj_at(c, 8 if nxt else 2))
                ch.link(nc.vector.tensor_tensor(o_ms, o_ss[:, 0:1], o_ss[:, 1:2], ALU.add))
                ch.wait()
                nc.vector.tensor_scalar(o_ms, o_ms, 1.0 / D, EPS, ALU.mult, ALU.add).then_inc(s_oms, 1)
                dve.wait_ge(s_ors, c + 1)
                ch.link(nc.vector.scalar_tensor_tensor(o_sb, o_sb, o_rstd, g_post, ALU.mult, ALU.mult))
                ch.wait()
                dve.wait_ge(s_xres, c * 16 + 16)
                nc.vector.tensor_tensor(o_sb, o_sb, x_res, ALU.add).then_inc(s_x1, 1)

            run_chunks(dve, step, ch)
            return ch

        def a_gpsimd(pool):
            def rsqrt(dst, src, n):
                return nc.gpsimd.tensor_tensor(dst, src, neg_half[:, 0:n], ALU.pow)

            nc.gpsimd.memset(neg_half, -0.5).then_inc(s_half, 1)
            pool.wait_ge(s_half, 1)
            for a in range(2):
                pool.wait_ge(s_memms, a + 1)
                rsqrt(mem_max[:, a:a + 1], o_ss[:, a:a + 1], 1).then_inc(s_memr, 1)

            def x_rsqrt(c):
                pool.wait_ge(s_xms, c + 1)
                rsqrt(x_rstd, x_ms, 1).then_inc(s_xrs, 1)

            def v_rsqrt(c):
                pool.wait_ge(s_vvar, c + 1)
                rsqrt(v_rstd, v_var, 4).then_inc(s_vrs, 1)

            x_rsqrt(0)
            x_rsqrt(1)
            v_rsqrt(0)

            def step(c, par):
                if not static(c) or c + 2 < NC:
                    x_rsqrt(c + 2)
                if not static(c) or c + 1 < NC:
                    v_rsqrt(c + 1)
                pool.wait_ge(s_oms, c + 1)
                rsqrt(o_rstd, o_ms, 1).then_inc(s_ors, 1)

            run_chunks(pool, step)

        x2_d = out if stop_after == "b" else dram("x2_scratch", [S, D])
        m = Arena(arena[:, :], SB)
        m.at = shared_end
        W2 = m.take(KT * (IN1 + D))
        w_in2 = W2[:, 0:KT * IN2].rearrange("p (k n) -> p k n", k=KT)
        w_mix = W2[:, KT * IN1:].rearrange("p (k n) -> p k n", k=KT)
        gate_rows = Arena(W2[:, KT * IN2:KT * IN1], KT * (IN1 - IN2))
        b_xin = m.take(D)
        b_xres = m.take(D)
        tab2 = m.take(CONST2_W)
        conv_w = m.take(KT, CONV)
        gate_b = m.take(8)
        pool_w = m.take(4, P)
        head_g = m.take(M_W)
        pool_sc = m.take(M_W)
        assert m.at <= free_end_a
        b_xT = m.take(KT, P)
        qk_win = m.take(KT, P + CONV - 1)
        qk = m.take(2, KT, P)
        b_tmp = m.take(KT, P)
        b_yT = b_tmp
        v_ext = m.take(2, LH, LD + 1)
        o_th = m.take(2, M_W)
        u_win = m.take(2, M_W)
        pk = m.take(KT, P)
        pooledT, k_tok = pk[:, 0:4, :], pk[:, 4:8, :]
        decay = m.take(LH, P)
        wv = m.take(LH, LD + 1)
        state = m.take(LH, LD + 1)
        hn = m.take(LH, LD + 1)
        b_y = m.take(D)
        b_o = m.take(D)
        mix_g, mix_b = m.take(D), m.take(D)
        gates = m.take(8)
        a_col = m.take(2, LH)
        e_col = m.take(2, 4 * LH)
        q_inter = m.take(LH)
        den, rden = m.take(LH), m.take(LH)
        h_stats, h_mv, h_var, h_rstd = m.take(LH, 6), m.take(LH, 2), m.take(LH), m.take(LH)
        r_stats, r_mv, r_var, r_rstd = m.take(2, 6), m.take(2), m.take(1), m.take(1)
        ones = m.take(P)
        m_diag = m.take(LH, P)
        g_if = gate_rows.take(2, P)
        g_abs, g_e, g_den, g_rec, g_s, g_s2, g_ser = [gate_rows.take(P) for _ in range(7)]
        g_b, g_m = gate_rows.take(P), gate_rows.take(P)
        g_out = gate_rows.take(4, P)
        g_dec = gate_rows.take(LH)
        m_state = gate_rows.take(1)

        def cst2(name):
            o, w = CONST2[name]
            return tab2[:, o:o + w]

        pool_first = cst2("pool_first").rearrange("p (g n) -> p g n", g=4)

        b_dt = psum[:, 4, :].rearrange("p (a n) -> p a n", a=4)
        b_small = psum[:, 4, :]
        b_st = psum[:, 5, :].rearrange("p (a n) -> p a n", a=4)
        b_ext = psum[:, 6:8, :]

        def ext(h):
            return b_ext[:, h // 2, (h % 2) * (LD + 1):(h % 2 + 1) * (LD + 1)]

        n_const, n_win, n_wout = sem("b_const_loaded"), [sem(f"b_w_in_loaded{g}") for g in range(6)], sem("b_w_mix_loaded")
        n_xin, n_xres, n_x2st = sem("b_x_in_loaded"), sem("b_x_res_loaded"), sem("b_x2_stored")
        n_zero, n_head = sem("b_state_zeroed"), sem("b_tables_scaled")
        n_tp, n_tpf, n_pj, n_pjf = sem("b_turned"), sem("b_turned_taken"), sem("b_proj_done"), sem("b_proj_taken")
        n_win_in, n_hist, n_conv, n_cth, n_qk = (sem("b_window_filled"), sem("b_window_shifted"), sem("b_conv_done"),
                                                 sem("b_conv_tanh"), sem("b_qk_ready"))
        n_gp, n_gb, n_gt, n_gabs, n_ge, n_rows = (sem("b_gates_product"), sem("b_gates_biased"), sem("b_gates_turned"),
                                                  sem("b_gates_abs"), sem("b_gates_exp"), sem("b_gate_rows_ready"))
        n_cols, n_colt = sem("b_gate_columns_done"), sem("b_gate_columns_taken")
        n_dt, n_darg, n_dexp, n_st, n_p = (sem("b_decay_product"), sem("b_decay_arg"), sem("b_decay_exp"),
                                           sem("b_scores_done"), sem("b_weights_ready"))
        n_qi, n_qc, n_qct = sem("b_inter_scaled"), sem("b_state_product"), sem("b_state_product_taken")
        n_upd, n_state = sem("b_update_product"), sem("b_state_ready")
        n_num, n_numt = sem("b_values_done"), sem("b_values_taken")
        n_hvar, n_hrs, n_pm, n_y = sem("b_head_var"), sem("b_head_rstd"), sem("b_pool_ready"), sem("b_y_ready")
        n_ot, n_rvar, n_rrs, n_x2 = sem("b_out_taken"), sem("b_row_var"), sem("b_row_rstd"), sem("b_x2_ready")

        N_CONST2 = 6 + CONV

        def tp2_at(c, n):
            return c * 3 + (1 + n)

        def pj2_at(c, n):
            return c * 8 + (5 + n)

        GROUPS2 = [0, M_W, 2 * M_W, 3 * M_W, POOL]

        def b_sync(sp):
            w_rows = t["w_in_2"].rearrange("(k p) n -> p k n", p=P)
            sp.wait_ge(s_x1st, 16 * (NC - 1))
            sp.wait_ge(s_xn, NC)
            sp.dma_start(b_xin, rows(x1_d, 0)).then_inc(n_xin, 16)
            sp.wait_ge(s_pj, pj_at(NC - 2, 6))
            for g, o in enumerate(GROUPS2):
                sp.dma_start(w_in2[:, :, o:o + M_W], w_rows[:, :, o:o + M_W]).then_inc(n_win[g], 16)
                if g == 1:
                    sp.dma_start(w_in2[:, :, GATE:POOL], w_rows[:, :, GATE:POOL]).then_inc(n_win[5], 16)
                    sp.dma_start(tab2, t["tables2"]).then_inc(n_const, 16)
                    for dst, name in ((gate_b[:, 0:4], "b_i_2"), (gate_b[:, 4:8], "b_f_2"), (head_g, "head_norm_g_2"),
                                      (pool_sc, "pool_scale_2")):
                        sp.dma_start(dst, t[name].partition_broadcast(P)).then_inc(n_const, 16)
                    with nc.allow_non_contiguous_dma(reason="4096 values once"):
                        for j in range(CONV):
                            sp.dma_start(conv_w[:, :, j], t["conv_qk_2"][j].rearrange("(k p) -> p k", p=P)).then_inc(n_const, 16)
                    sp.dma_start(pool_w, t["pool_w_2"].rearrange("g c d -> c g d")).then_inc(n_const, 16)

        def b_sync_main(sp, before_last):
            sp.dma_start(w_mix, t["w_mix_out_2"].rearrange("(k p) n -> p k n", p=P)).then_inc(n_wout, 16)
            for dst, name in ((mix_g, "ln_mix_g_2"), (mix_b, "ln_mix_b_2")):
                sp.dma_start(dst, t[name].partition_broadcast(P)).then_inc(n_wout, 16)
            sp.dma_start(b_xres, rows(x1_d, 0)).then_inc(n_xres, 16)
            sp.wait_ge(n_tp, 1)
            sp.dma_start(b_xin, rows(x1_d, 1)).then_inc(n_xin, 16)

            def step(c, par):
                if not static(c) or c + 2 < NC:
                    sp.wait_ge(n_tp, tp2_at(c, 1))
                    sp.dma_start(b_xin, rows(x1_d, c + 2)).then_inc(n_xin, 16)
                sp.wait_ge(n_x2, c + 1)
                sp.dma_start(rows(x2_d, c), b_o).then_inc(n_x2st, 16)
                if not static(c) or c + 1 < NC:
                    sp.dma_start(b_xres, rows(x1_d, c + 1)).then_inc(n_xres, 16)

            run_chunks(sp, step, before_last=before_last)

        def b_sync_end(sp):
            sp.wait_ge(n_x2st, 16 * NC)

        def b_tensor(pe):
            def tiles(ap, n):
                return [ap[:, k * P:(k + 1) * P] for k in range(n)]

            def free_tp(at):
                if not static(at) or at:
                    pe.wait_ge(n_tpf, at)

            def turn(src, at):
                free_tp(at)
                for i, tile in enumerate(src):
                    ins = nc.tensor.transpose(tp[:, i, :], tile, ident)
                ins.then_inc(n_tp, 1)

            def front(c, at):
                pe.wait_ge(n_xin, c * 16 + 16)
                turn(tiles(b_xin, KT), at)

            def free_pj(at):
                if not static(at) or at >= 2:
                    pe.wait_ge(n_pjf, at - 1)

            def group_turned(g, at, first):
                free_pj(at)
                if first:
                    pe.wait_ge(n_win[g], 16)
                for i in range(4):
                    o = GROUPS2[g] + i * P
                    for k in range(KT):
                        ins = nc.tensor.matmul(pj[0 if g == 0 else 1][:, i * P:(i + 1) * P], w_in2[:, k, o:o + P], b_xT[:, k, :],
                                               start=(k == 0), stop=(k == KT - 1))
                ins.then_inc(n_pj, 1)

            def group(g, at, bank, first):
                free_pj(at)
                if first:
                    pe.wait_ge(n_win[g], 16)
                o = GROUPS2[g]
                for k in range(KT):
                    ins = nc.tensor.matmul(pj[bank], b_xT[:, k, :], w_in2[:, k, o:o + M_W], start=(k == 0), stop=(k == KT - 1))
                ins.then_inc(n_pj, 1)

            def gate_product(c):
                if not static(c) or c:
                    pe.wait_ge(n_darg, c)
                if static(c) and c == 0:
                    pe.wait_ge(n_win[5], 16)
                for k in range(KT):
                    ins = nc.tensor.matmul(b_small[:, 0:8], b_xT[:, k, :], w_in2[:, k, GATE:POOL],
                                           start=(k == 0), stop=(k == KT - 1))
                ins.then_inc(n_gp, 1)

            def gate_turn(c):
                pe.wait_ge(n_gb, c + 1)
                nc.tensor.transpose(b_small[0:LH, P:2 * P], gates[:, 0:4], ident)
                nc.tensor.transpose(b_small[0:LH, 2 * P:3 * P], gates[:, 4:8], ident).then_inc(n_gt, 1)

            def gate_columns(c):
                pe.wait_ge(n_rows, c + 1)
                settled(pe)
                for i in range(4):
                    nc.tensor.transpose(b_small[:, 400 + 4 * i:404 + 4 * i], g_out[0:LH, i, :], ident[0:LH, 0:LH])
                nc.tensor.matmul(b_small[:, 416:420], ones[0:LH, :], g_dec[0:LH, :], start=True, stop=True).then_inc(n_cols, 1)

            front(0, 0)
            pe.wait_ge(n_tpf, 1)
            pe.wait_ge(s_pjf, pj_at(NC - 1, 2))
            group_turned(0, 0, True)
            group_turned(1, 1, True)
            gate_product(0)
            group(2, 2, 0, True)
            gate_turn(0)
            group(3, 3, 1, True)
            gate_columns(0)
            group(4, 4, 0, True)

            def step(c, par):
                nxt = not static(c) or c + 1 < NC
                qT2, kT2 = qk[:, par, 0:4, :], qk[:, par, 4:8, :]
                n = 0
                if nxt:
                    front(c + 1, tp2_at(c, 0))
                    n = 1
                pe.wait_ge(n_colt, c + 1)
                nc.tensor.matmul(psum[:, 4, :], ones[0:LH, :], m_diag[0:LH].rearrange("p a n -> p (a n)"),
                                 start=True, stop=True).then_inc(n_dt, 1)
                pe.wait_ge(n_qk, c + 1)
                if not static(c) or c:
                    pe.wait_ge(n_p, c)
                for h in range(LH):
                    ins = nc.tensor.matmul(b_st[:, h, :], kT2[:, h, :], qT2[:, h, :], start=True, stop=True)
                ins.then_inc(n_st, 1)
                if not static(c) or c:
                    pe.wait_ge(n_state, c)
                    pe.wait_ge(n_numt, c)
                for h in range(LH):
                    ins = nc.tensor.matmul(ext(h), qT2[:, h, :], state[:, h, :], start=True, stop=True)
                ins.then_inc(n_qc, 1)
                free_tp(tp2_at(c, n))
                first = static(c) and c == 0
                if first:
                    pe.wait_ge(n_pjf, 5)
                    pe.wait_ge(n_const, 16 * N_CONST2)
                for g in range(4):
                    cur = pool_first[:, g, :] if first else cst2("pool_cur")[:, g * P:(g + 1) * P]
                    nc.tensor.matmul(tp[:, g, :], u_win[:, par, g * P:(g + 1) * P], cur, start=True, stop=first)
                    if not first:
                        nc.tensor.matmul(tp[:, g, :], u_win[:, 1 - par, g * P:(g + 1) * P],
                                         cst2("pool_prev")[:, g * P:(g + 1) * P], start=False, stop=True)
                for h in range(LH):
                    ins = nc.tensor.transpose(tp[:, 4 + h, :], kT2[:, h, :], ident)
                ins.then_inc(n_tp, 1)
                if nxt:
                    group_turned(0, pj2_at(c, 0), False)
                    group_turned(1, pj2_at(c, 1), False)
                    gate_product(c + 1)
                pe.wait_ge(n_tpf, tp2_at(c, n) + 1)
                at = pj2_at(c, 2 if nxt else 0)
                free_pj(at)
                for g in range(4):
                    ins = nc.tensor.matmul(pj[0][:, g * P:(g + 1) * P], pooledT[:, g, :], pool_w[:, g, :], start=True, stop=True)
                ins.then_inc(n_pj, 1)
                pe.wait_ge(n_qct, c + 1)
                for h in range(LH):
                    ins = nc.tensor.matmul(ext(h), k_tok[:, h, :], wv[:, h, :], start=True, stop=True)
                ins.then_inc(n_upd, 1)
                if nxt:
                    group(2, pj2_at(c, 3), 1, False)
                    gate_turn(c + 1)
                pe.wait_ge(n_p, c + 1)
                pe.wait_ge(n_state, c + 1)
                for h in range(LH):
                    ins = nc.tensor.matmul(ext(h), decay[:, h, :], v_ext[:, par, h, :], start=True, stop=True)
                ins.then_inc(n_num, 1)
                if nxt:
                    group(3, pj2_at(c, 4), 0, False)
                    gate_columns(c + 1)
                    group(4, pj2_at(c, 5), 1, False)
                n += 1
                pe.wait_ge(n_y, c + 1)
                turn(tiles(b_y, KT), tp2_at(c, n))
                pe.wait_ge(n_tpf, tp2_at(c, n) + 1)
                if first:
                    pe.wait_ge(n_wout, 48)
                for j in range(2):
                    at = pj2_at(c, (6 if nxt else 1) + j)
                    free_pj(at)
                    bank = j if nxt else 1 - j
                    for k in range(KT):
                        ins = nc.tensor.matmul(pj[bank], b_yT[:, k, :], w_mix[:, k, j * 512:(j + 1) * 512],
                                               start=(k == 0), stop=(k == KT - 1))
                    ins.then_inc(n_pj, 1)

            run_chunks(pe, step)

        def b_scalar(act):
            def copy(dst, src, scale=1.0):
                return nc.scalar.activation(dst, src, ACT.Copy, scale=scale)

            def take_tiles(dst, at):
                act.wait_ge(n_tp, at + 1)
                copy(dst[:, 0:4, :], tp[:, 0:4, :])
                copy(dst[:, 4:8, :], tp[:, 4:8, :]).then_inc(n_tpf, 1)

            def take_qk(c, g, at):
                act.wait_ge(n_pj, at + 1)
                if g == 0:
                    act.wait_ge(n_hist, c + 1)
                copy(qk_win[:, 4 * g:4 * g + 4, CONV - 1:], pj[g].rearrange("p (a n) -> p a n", a=4)).then_inc(n_pjf, 1)

            def conv_tanh(c):
                act.wait_ge(n_conv, c + 1)
                nc.scalar.activation(b_tmp, qk[:, c % 2 if static(c) else conv_par[0]], ACT.Tanh).then_inc(n_cth, 1)

            def take_v(par, at, bank):
                act.wait_ge(n_pj, at + 1)
                copy(v_ext[:, par, :, 0:LD], pj[bank].rearrange("p (a n) -> p a n", a=4)).then_inc(n_pjf, 1)

            def take_o(par, at, bank):
                act.wait_ge(n_pj, at + 1)
                nc.scalar.activation(o_th[:, par, :], pj[bank], ACT.Tanh, scale=0.5).then_inc(n_pjf, 1)

            def take_u(par, at, bank):
                act.wait_ge(n_pj, at + 1)
                copy(u_win[:, par, :], pj[bank]).then_inc(n_pjf, 1)

            def gate_exp(c):
                act.wait_ge(n_gabs, c + 1)
                nc.scalar.activation(g_e[0:LH], g_abs[0:LH], ACT.Exp).then_inc(n_ge, 1)

            def take_columns(c, par):
                act.wait_ge(n_cols, c + 1)
                copy(a_col[:, par, :], b_small[:, 400:404])
                nc.scalar.activation(e_col[:, par, :], b_small[:, 404:420], ACT.Exp).then_inc(n_colt, 1)

            conv_par = [0]
            take_tiles(b_xT, 0)
            take_qk(0, 0, 0)
            take_qk(0, 1, 1)
            conv_tanh(0)
            take_v(0, 2, 0)
            gate_exp(0)
            take_o(0, 3, 1)
            take_columns(0, 0)
            take_u(0, 4, 0)

            def step(c, par):
                nxt = not static(c) or c + 1 < NC
                npar = 1 - par
                conv_par[0] = npar
                n = 0
                if nxt:
                    take_tiles(b_xT, tp2_at(c, 0))
                    n = 1
                act.wait_ge(n_colt, c + 1)
                for h in range(LH):
                    copy(wv[:, h, :], v_ext[:, par, h, :], e_col[:, par, 8 + h:9 + h])
                act.wait_ge(n_qi, c + 1)
                act.wait_ge(n_qc, c + 1)
                for h in range(LH):
                    ins = copy(hn[:, h, :], ext(h), q_inter[:, h:h + 1])
                ins.then_inc(n_qct, 1)
                take_tiles(pk, tp2_at(c, n))
                act.wait_ge(n_darg, c + 1)
                nc.scalar.activation(decay, decay, ACT.Exp).then_inc(n_dexp, 1)
                if nxt:
                    take_qk(c + 1, 0, pj2_at(c, 0))
                    take_qk(c + 1, 1, pj2_at(c, 1))
                act.wait_ge(n_pj, pj2_at(c, 2 if nxt else 0) + 1)
                copy(b_y[:, M_W:D], pj[0]).then_inc(n_pjf, 1)
                if nxt:
                    conv_tanh(c + 1)
                    take_v(npar, pj2_at(c, 3), 1)
                    gate_exp(c + 1)
                    take_o(npar, pj2_at(c, 4), 0)
                    take_columns(c + 1, npar)
                    take_u(npar, pj2_at(c, 5), 1)
                n += 1
                take_tiles(b_yT, tp2_at(c, n))
                if not static(c) or c:
                    act.wait_ge(n_x2st, c * 16)
                for j in range(2):
                    act.wait_ge(n_pj, pj2_at(c, (6 if nxt else 1) + j) + 1)
                    copy(b_o[:, j * 512:(j + 1) * 512], pj[j if nxt else 1 - j]).then_inc(n_pjf, 1)

            run_chunks(act, step)

        def b_vector(dve, ch):
            def seq(ins):
                ch.link(ins)
                ch.wait()

            def shift(c):
                if static(c) and c == 0:
                    nc.vector.memset(qk_win[:, :, 0:CONV - 1], 0.0).then_inc(n_hist, 1)
                else:
                    nc.vector.tensor_copy(qk_win[:, :, 0:CONV - 1], qk_win[:, :, P:P + CONV - 1]).then_inc(n_hist, 1)

            def conv(c, par, taken):
                dve.wait_ge(n_pjf, taken)
                dve.wait_ge(n_hist, c + 1)
                for j in range(CONV):
                    for i in range(KT):
                        dst, src = qk[:, par, i, :], qk_win[:, i, j:j + P]
                        if j == 0:
                            ins = nc.vector.tensor_scalar(dst, src, conv_w[:, i, j:j + 1], None, ALU.mult)
                        else:
                            ins = nc.vector.scalar_tensor_tensor(dst, src, conv_w[:, i, j:j + 1], dst, ALU.mult, ALU.add)
                    if j < CONV - 1:
                        seq(ins)
                ins.then_inc(n_conv, 1)

            def silu(c, par):
                dve.wait_ge(n_cth, c + 1)
                nc.vector.scalar_tensor_tensor(qk[:, par], b_tmp, 1.0, qk[:, par], ALU.add, ALU.mult).then_inc(n_qk, 1)

            def gate_bias(c):
                dve.wait_ge(n_gp, c + 1)
                nc.vector.tensor_tensor(gates, b_small[:, 0:8], gate_b, ALU.add).then_inc(n_gb, 1)

            def gate_abs(c):
                dve.wait_ge(n_gt, c + 1)
                seq(nc.vector.tensor_copy(g_if[0:LH], b_small[0:LH, P:3 * P].rearrange("p (a n) -> p a n", a=2)))
                f = g_if[0:LH, 1, :]
                nc.vector.scalar_tensor_tensor(g_abs[0:LH], f, -1.0, f, ALU.mult, ALU.min).then_inc(n_gabs, 1)

            def gate_math(c):
                ig, f = g_if[0:LH, 0, :], g_if[0:LH, 1, :]
                e, dn, rc, s, s2, q = (x[0:LH] for x in (g_e, g_den, g_rec, g_s, g_s2, g_ser))
                b, mx, o = g_b[0:LH], g_m[0:LH], g_out[0:LH]
                dve.wait_ge(n_ge, c + 1)
                seq(nc.vector.tensor_scalar(dn, e, 2.0, None, ALU.add))
                seq(nc.vector.reciprocal(rc, dn))
                seq(nc.vector.tensor_tensor(s, e, rc, ALU.mult))
                seq(nc.vector.tensor_tensor(s2, s, s, ALU.mult))
                seq(nc.vector.tensor_scalar(q, s2, LN_TERMS[0], None, ALU.mult))
                for term in LN_TERMS[1:]:
                    seq(nc.vector.scalar_tensor_tensor(q, q, term, s2, ALU.add, ALU.mult))
                seq(nc.vector.scalar_tensor_tensor(q, q, 1.0, s, ALU.add, ALU.mult))
                seq(nc.vector.tensor_scalar(q, q, 2.0, None, ALU.mult))
                seq(nc.vector.scalar_tensor_tensor(s, f, 0.0, q, ALU.min, ALU.subtract))
                seq(nc.vector.tensor_tensor_scan(b, ones[0:LH, :], s, 0.0, ALU.mult, ALU.add))
                seq(nc.vector.tensor_tensor(o[:, 0, :], ig, b, ALU.subtract))
                seq(nc.vector.tensor_tensor_scan(mx, o[:, 0, :], o[:, 0, :], m_state[0:LH, :], ALU.max, ALU.max))
                nc.vector.tensor_scalar(o[:, 1, :], mx, -1.0, m_state[0:LH, :], ALU.mult, ALU.add)
                nc.vector.scalar_tensor_tensor(o[:, 2, :], b, -1.0, mx, ALU.mult, ALU.subtract)
                nc.vector.tensor_scalar(o[:, 3, :], o[:, 0, :], mx[:, P - 1:P], None, ALU.subtract)
                seq(nc.vector.tensor_tensor(m_diag[0:LH], cst2("head_neg")[0:LH].rearrange("p (a n) -> p a n", a=4),
                                            mx.unsqueeze(1).to_broadcast([LH, LH, P]), ALU.mult))
                nc.vector.tensor_scalar(g_dec[0:LH], ident[0:LH, 0:LH], o[:, 1, P - 1:P], None, ALU.mult)
                nc.vector.tensor_scalar(m_state[0:LH, :], o[:, 2, P - 1:P], -1.0, None, ALU.mult).then_inc(n_rows, 1)

            dve.wait_ge(n_const, 16 * N_CONST2)
            nc.vector.memset(state, 0.0)
            nc.vector.memset(m_state, 0.0)
            nc.vector.memset(ones, 1.0)
            nc.vector.memset(v_ext[:, :, :, LD:LD + 1], 1.0)
            nc.vector.tensor_scalar(conv_w, conv_w, 0.5, None, ALU.mult)
            nc.vector.tensor_scalar(head_g, head_g, 0.5, None, ALU.mult).then_inc(n_head, 1)
            dve.wait_ge(n_head, 1)
            shift(0)
            conv(0, 0, 2)
            gate_bias(0)
            silu(0, 0)
            shift(1)
            gate_abs(0)
            gate_math(0)

            def step(c, par):
                nxt = not static(c) or c + 1 < NC
                npar = 1 - par
                dve.wait_ge(n_colt, c + 1)
                nc.vector.tensor_scalar(q_inter, e_col[:, par, 0:4], LD ** -0.5, None, ALU.mult).then_inc(n_qi, 1)
                dve.wait_ge(n_dt, c + 1)
                if not static(c) or c:
                    dve.wait_ge(n_num, c)
                for h in range(LH):
                    ins = nc.vector.scalar_tensor_tensor(decay[:, h, :], b_dt[:, h, :], a_col[:, par, h:h + 1], cst2("after"),
                                                         ALU.add, ALU.min)
                ins.then_inc(n_darg, 1)
                dve.wait_ge(n_st, c + 1)
                dve.wait_ge(n_dexp, c + 1)
                nc.vector.scalar_tensor_tensor(decay, b_st, LD ** -0.5, decay, ALU.mult, ALU.mult).then_inc(n_p, 1)
                if nxt:
                    gate_bias(c + 1)
                dve.wait_ge(n_upd, c + 1)
                for h in range(LH):
                    ins = nc.vector.scalar_tensor_tensor(state[:, h, :], state[:, h, :], e_col[:, par, 12 + h:13 + h], ext(h),
                                                         ALU.mult, ALU.add)
                ins.then_inc(n_state, 1)
                if nxt:
                    conv(c + 1, npar, pj2_at(c, 2))
                    gate_abs(c + 1)
                    gate_math(c + 1)
                dve.wait_ge(n_num, c + 1)
                dve.wait_ge(n_qct, c + 1)
                for j in range(2):
                    two = hn[:, 2 * j:2 * j + 2, :]
                    ins = nc.vector.tensor_tensor(two, b_ext[:, j, 0:2 * (LD + 1)].rearrange("p (a n) -> p a n", a=2), two, ALU.add)
                ins.then_inc(n_numt, 1)
                dve.wait_ge(n_numt, c + 1)
                d = hn[:, :, LD]
                seq(nc.vector.scalar_tensor_tensor(den, d, -1.0, d, ALU.mult, ALU.max))
                seq(nc.vector.tensor_tensor(den, den, e_col[:, par, 4:8], ALU.max))
                seq(nc.vector.reciprocal(rden, den))
                for h in range(LH):
                    ins = nc.vector.tensor_scalar(hn[:, h, 0:LD], hn[:, h, 0:LD], rden[:, h:h + 1], None, ALU.mult)
                seq(ins)
                for h in range(LH):
                    ins = nc.vector.bn_stats(h_stats[:, h, :], hn[:, h, 0:LD])
                seq(ins)
                settled(dve)
                for h in range(LH):
                    ins = nc.vector.bn_aggr(h_mv[:, h, :], h_stats[:, h, :])
                seq(ins)
                nc.vector.tensor_scalar(h_var, h_mv[:, :, 1], LN_EPS, None, ALU.add).then_inc(n_hvar, 1)
                if nxt:
                    silu(c + 1, npar)
                    if not static(c) or c + 2 < NC:
                        shift(c + 2)
                dve.wait_ge(n_hrs, c + 1)
                if not static(c) or c:
                    dve.wait_ge(n_tp, tp2_at(c, 0))
                for h in range(LH):
                    ins = nc.vector.tensor_scalar(b_y[:, h * LD:(h + 1) * LD], hn[:, h, 0:LD], h_mv[:, h, 0:1], h_rstd[:, h:h + 1],
                                                  ALU.subtract, ALU.mult)
                seq(ins)
                seq(nc.vector.tensor_tensor(b_y[:, 0:M_W], b_y[:, 0:M_W], head_g, ALU.mult))
                nc.vector.scalar_tensor_tensor(b_y[:, 0:M_W], o_th[:, par, :], 1.0, b_y[:, 0:M_W], ALU.add, ALU.mult)
                dve.wait_ge(n_pjf, pj2_at(c, 3 if nxt else 1))
                nc.vector.tensor_tensor(b_y[:, M_W:D], b_y[:, M_W:D], pool_sc, ALU.mult).then_inc(n_y, 1)
                dve.wait_ge(n_pjf, pj2_at(c, 8 if nxt else 3))
                dve.wait_ge(n_xres, c * 16 + 16)
                if static(c) and c == 0:
                    dve.wait_ge(n_wout, 48)
                seq(nc.vector.scalar_tensor_tensor(b_o, b_xres, ALPHA, b_o, ALU.mult, ALU.add))
                for j in range(2):
                    ins = nc.vector.bn_stats(r_stats[:, j, :], b_o[:, j * 512:(j + 1) * 512])
                seq(ins)
                settled(dve)
                seq(nc.vector.bn_aggr(r_mv, r_stats.rearrange("p a b -> p (a b)")))
                nc.vector.tensor_scalar(r_var, r_mv[:, 1:2], LN_EPS, None, ALU.add).then_inc(n_rvar, 1)
                dve.wait_ge(n_rrs, c + 1)
                seq(nc.vector.tensor_scalar(b_o, b_o, r_mv[:, 0:1], r_rstd, ALU.subtract, ALU.mult))
                seq(nc.vector.tensor_tensor(b_o, b_o, mix_g, ALU.mult))
                nc.vector.tensor_tensor(b_o, b_o, mix_b, ALU.add).then_inc(n_x2, 1)

            run_chunks(dve, step, ch)

        def b_gpsimd(pool):
            def step(c, par):
                pool.wait_ge(n_hvar, c + 1)
                nc.gpsimd.tensor_tensor(h_rstd, h_var, neg_half, ALU.pow).then_inc(n_hrs, 1)
                pool.wait_ge(n_rvar, c + 1)
                nc.gpsimd.tensor_tensor(r_rstd, r_var, neg_half[:, 0:1], ALU.pow).then_inc(n_rrs, 1)

            run_chunks(pool, step)

        x3_d = out if stop_after == "c" else dram("x3_scratch", [S, D])
        m = Arena(arena[:, :], SB)
        m.at = shared_end
        w_xkv = m.take(KT, 2 * D)
        c_rows = m.take(2, D)
        assert m.at <= shared_end + KT * IN2
        w_xq = m.take(KT, D)
        w_xo = m.take(KT, D)
        scores = m.take(NC, NE)
        c_end = m.at
        xkT = m.take(KT, MEM)
        xv = m.take(2, D)
        c_xin = m.take(D)
        c_xres = m.take(D)
        c_xT = m.take(KT, P)
        c_stage = m.take(4 * D)
        c_memT = c_stage[:, 2 * D:4 * D].rearrange("p (k n) -> p k n", k=KT)
        c_qT = m.take(KT, P)
        c_prob = c_stage[:, 0:D].rearrange("p (h n) -> p h n", h=XH)
        c_pT = c_stage[:, D:2 * D].rearrange("p (k n) -> p k n", k=KT)
        c_att = c_stage[:, 2 * D:3 * D]
        c_attT = c_stage[:, 3 * D:4 * D].rearrange("p (k n) -> p k n", k=KT)
        c_o = m.take(D)
        c_oT = m.take(KT, P)
        lnx_g, lnx_b = m.take(D), m.take(D)
        r_w = m.take(KT, NE)
        r_exp = m.take(NE)
        c_max, c_nmax, c_sum, c_rden = m.take(XH), m.take(XH), m.take(XH), m.take(XH)
        c_stats, c_mv, c_var, c_rstd = m.take(2, 6), m.take(2), m.take(1), m.take(1)
        c_pv = psum[:, 6:8, :].rearrange("p b (a n) -> p (b a) n", a=2)
        r_ps = psum[:, 4, 0:NE]

        c_mem, c_const, c_wkv, c_wq, c_wo = (sem("c_memory_loaded"), sem("c_const_loaded"), sem("c_w_kv_loaded"), sem("c_w_q_loaded"), sem("c_w_o_loaded"))
        c_xin_ld, c_xres_ld, c_x3st = sem("c_x_in_loaded"), sem("c_x_res_loaded"), sem("c_x3_stored")
        c_tp, c_tpf, c_pj, c_pjf = sem("c_turned"), sem("c_turned_taken"), sem("c_proj_done"), sem("c_proj_taken")
        c_lg, c_nm, c_ex, c_pvd, c_rd, c_pvt = (sem("c_logits_done"), sem("c_max_ready"), sem("c_exp_ready"), sem("c_values_done"),
                                                sem("c_denominator_ready"), sem("c_values_taken"))
        c_rvar, c_rrs, c_x3 = sem("c_row_var"), sem("c_row_rstd"), sem("c_x3_ready")
        r_lg, r_ex, r_sc = sem("c_router_done"), sem("c_router_exp"), sem("c_router_scores")
        N_CONST3 = 3
        SETUP_PJ = 8

        def tp3_at(c, n):
            return 3 + n if static(c) and c == 0 else c * 4 + (2 + n)

        def pj3_at(c, n):
            return c * 4 + (SETUP_PJ + 2 + n)

        def c_sync(sp):
            sp.wait_ge(n_pj, pj2_at(NC - 2, 6))
            sp.wait_ge(n_gp, NC)
            sp.dma_start(c_rows, t["mem_2"].rearrange("(a p) n -> p a n", p=P)).then_inc(c_mem, 16)
            sp.dma_start(w_xkv, t["w_xkv_2"].rearrange("(k p) n -> p k n", p=P)).then_inc(c_wkv, 16)

        def c_sync_main(sp, before_last):
            sp.dma_start(w_xq, t["w_xq_2"].rearrange("(k p) n -> p k n", p=P)).then_inc(c_wq, 16)
            sp.dma_start(c_xin, rows(x2_d, 0)).then_inc(c_xin_ld, 16)
            for dst, name in ((lnx_g, "ln_x_g_2"), (lnx_b, "ln_x_b_2")):
                sp.dma_start(dst, t[name].partition_broadcast(P)).then_inc(c_const, 16)
            sp.dma_start(r_w, t["router_w_2"].rearrange("(k p) n -> p k n", p=P)).then_inc(c_const, 16)
            sp.dma_start(w_xo, t["w_xo_2"].rearrange("(k p) n -> p k n", p=P)).then_inc(c_wo, 16)
            sp.dma_start(c_xres, rows(x2_d, 0)).then_inc(c_xres_ld, 16)
            sp.wait_ge(c_tp, 3)
            sp.dma_start(c_xin, rows(x2_d, 1)).then_inc(c_xin_ld, 16)

            def step(c, par):
                if not static(c) or c + 2 < NC:
                    sp.wait_ge(c_tp, tp3_at(c, 1))
                    sp.dma_start(c_xin, rows(x2_d, c + 2)).then_inc(c_xin_ld, 16)
                sp.wait_ge(c_x3, c + 1)
                sp.dma_start(rows(x3_d, c), c_o).then_inc(c_x3st, 16)
                if not static(c) or c + 1 < NC:
                    sp.dma_start(c_xres, rows(x2_d, c + 1)).then_inc(c_xres_ld, 16)

            run_chunks(sp, step, before_last=before_last)
            sp.wait_ge(c_x3st, 16 * NC)

        def c_tensor(pe):
            def turn(src, at):
                if not static(at) or at:
                    pe.wait_ge(c_tpf, at)
                for i, tile in enumerate(src):
                    ins = nc.tensor.transpose(tp[:, i, :], tile, ident)
                ins.then_inc(c_tp, 1)

            def tiles(ap):
                return [ap[:, k * P:(k + 1) * P] for k in range(KT)]

            def front(c, at):
                pe.wait_ge(c_xin_ld, c * 16 + 16)
                turn(tiles(c_xin), at)

            def free_pj(at):
                if not static(at) or at >= 2:
                    pe.wait_ge(c_pjf, at - 1)

            def queries(g, at):
                free_pj(at)
                for i in range(4):
                    o = (4 * g + i) * P
                    for k in range(KT):
                        ins = nc.tensor.matmul(pj[g][:, i * P:(i + 1) * P], w_xq[:, k, o:o + P], c_xT[:, k, :],
                                               start=(k == 0), stop=(k == KT - 1))
                ins.then_inc(c_pj, 1)

            def router(c):
                for k in range(KT):
                    ins = nc.tensor.matmul(r_ps, c_oT[:, k, :], r_w[:, k, :], start=(k == 0), stop=(k == KT - 1))
                ins.then_inc(r_lg, 1)

            pe.wait_ge(c_mem, 16)
            for a in range(2):
                turn(tiles(c_rows[:, a, :]), a)
            pe.wait_ge(c_tpf, 2)
            pe.wait_ge(c_wkv, 16)
            pe.wait_ge(n_pjf, pj2_at(NC - 1, 3))
            for j in range(4):
                free_pj(j)
                for i in range(2):
                    o = (2 * j + i) * P
                    for k in range(KT):
                        ins = nc.tensor.matmul(pj[j % 2][:, i * MEM:(i + 1) * MEM], w_xkv[:, k, o:o + P], c_memT[:, k, :],
                                               start=(k == 0), stop=(k == KT - 1))
                ins.then_inc(c_pj, 1)
            for j in range(4):
                free_pj(4 + j)
                a, o = j // 2, D + (j % 2) * 512
                for k in range(KT):
                    ins = nc.tensor.matmul(pj[j % 2], c_memT[:, k, a * P:(a + 1) * P], w_xkv[:, k, o:o + 512],
                                           start=(k == 0), stop=(k == KT - 1))
                ins.then_inc(c_pj, 1)
            front(0, 2)
            pe.wait_ge(c_tpf, 3)
            pe.wait_ge(c_wq, 16)
            for g in range(2):
                queries(g, SETUP_PJ + g)

            def step(c, par):
                first = static(c) and c == 0
                nxt = not static(c) or c + 1 < NC
                n = 0
                if nxt:
                    front(c + 1, tp3_at(c, 0))
                    n = 1
                pe.wait_ge(c_pjf, pj3_at(c, 0))
                if not first:
                    pe.wait_ge(r_ex, c - 1)
                for h in range(XH):
                    for k in range(2):
                        ins = nc.tensor.matmul(lg[:, h, :], c_qT[:, 2 * h + k, :], xkT[:, 2 * h + k, :], start=(k == 0), stop=(k == 1))
                ins.then_inc(c_lg, 1)
                if nxt:
                    pe.wait_ge(c_tpf, tp3_at(c, 0) + 1)
                    queries(0, pj3_at(c, 0))
                pe.wait_ge(c_ex, c + 1)
                turn([c_prob[:, h, b * P:(b + 1) * P] for h in range(XH) for b in range(2)], tp3_at(c, n))
                if nxt:
                    queries(1, pj3_at(c, 1))
                pe.wait_ge(c_tpf, tp3_at(c, n) + 1)
                if not first:
                    pe.wait_ge(c_pvt, c)
                for h in range(XH):
                    for b in range(2):
                        ins = nc.tensor.matmul(c_pv[:, h, :], c_pT[:, 2 * h + b, :], xv[:, b, h * XD:(h + 1) * XD],
                                               start=(b == 0), stop=(b == 1))
                ins.then_inc(c_pvd, 1)
                n += 1
                if not first:
                    pe.wait_ge(c_x3, c)
                    turn(tiles(c_o), tp3_at(c, n))
                    n += 1
                pe.wait_ge(c_pvt, c + 1)
                turn(tiles(c_att), tp3_at(c, n))
                if static(c) and c == 1:
                    pe.wait_ge(c_const, 16 * N_CONST3)
                if not first:
                    router(c - 1)
                pe.wait_ge(c_tpf, tp3_at(c, n) + 1)
                if first:
                    pe.wait_ge(c_wo, 16)
                for j in range(2):
                    at = pj3_at(c, (2 if nxt else 0) + j)
                    free_pj(at)
                    for k in range(KT):
                        ins = nc.tensor.matmul(pj[j], c_attT[:, k, :], w_xo[:, k, j * 512:(j + 1) * 512],
                                               start=(k == 0), stop=(k == KT - 1))
                    ins.then_inc(c_pj, 1)

            run_chunks(pe, step)
            pe.wait_ge(c_x3, NC)
            turn(tiles(c_o), tp3_at(NC - 1, 3))
            pe.wait_ge(c_tpf, tp3_at(NC - 1, 3) + 1)
            pe.wait_ge(r_ex, NC - 1)
            router(NC - 1)

        def c_scalar(act):
            def copy(dst, src, scale=1.0):
                return nc.scalar.activation(dst, src, ACT.Copy, scale=scale)

            def take_tiles(dst, at):
                act.wait_ge(c_tp, at + 1)
                copy(dst[:, 0:4, :], tp[:, 0:4, :])
                copy(dst[:, 4:8, :], tp[:, 4:8, :]).then_inc(c_tpf, 1)

            def take_queries(g, at):
                act.wait_ge(c_pj, at + 1)
                copy(c_qT[:, 4 * g:4 * g + 4, :], pj[g].rearrange("p (a n) -> p a n", a=4), XD ** -0.5).then_inc(c_pjf, 1)

            def router_exp(c):
                act.wait_ge(r_lg, c + 1)
                if not static(c) or c:
                    act.wait_ge(r_sc, c)
                nc.scalar.activation(r_exp, r_ps, ACT.Exp, scale=-1.0).then_inc(r_ex, 1)

            for a in range(2):
                act.wait_ge(c_tp, a + 1)
                copy(c_memT[:, 0:4, a * P:(a + 1) * P], tp[:, 0:4, :])
                copy(c_memT[:, 4:8, a * P:(a + 1) * P], tp[:, 4:8, :]).then_inc(c_tpf, 1)
            for j in range(4):
                act.wait_ge(c_pj, j + 1)
                copy(xkT[:, 2 * j:2 * j + 2, :], pj[j % 2].rearrange("p (a n) -> p a n", a=2)).then_inc(c_pjf, 1)
            for j in range(4):
                act.wait_ge(c_pj, 5 + j)
                copy(xv[:, j // 2, (j % 2) * 512:(j % 2) * 512 + 512], pj[j % 2]).then_inc(c_pjf, 1)
            take_tiles(c_xT, 2)
            for g in range(2):
                take_queries(g, SETUP_PJ + g)

            def step(c, par):
                first = static(c) and c == 0
                nxt = not static(c) or c + 1 < NC
                n = 0
                if nxt:
                    take_tiles(c_xT, tp3_at(c, 0))
                    n = 1
                act.wait_ge(c_nm, c + 1)
                for h in range(XH):
                    ins = nc.scalar.activation(c_prob[:, h, :], lg[:, h, :], ACT.Exp, bias=c_nmax[:, h:h + 1],
                                               accum_out=c_sum[:, h:h + 1])
                ins.then_inc(c_ex, 1)
                if nxt:
                    take_queries(0, pj3_at(c, 0))
                take_tiles(c_pT, tp3_at(c, n))
                if nxt:
                    take_queries(1, pj3_at(c, 1))
                n += 1
                act.wait_ge(c_rd, c + 1)
                act.wait_ge(c_pvd, c + 1)
                for h in range(XH):
                    ins = copy(c_att[:, h * XD:(h + 1) * XD], c_pv[:, h, :], c_rden[:, h:h + 1])
                ins.then_inc(c_pvt, 1)
                if not first:
                    take_tiles(c_oT, tp3_at(c, n))
                    n += 1
                take_tiles(c_attT, tp3_at(c, n))
                if not first:
                    router_exp(c - 1)
                    act.wait_ge(c_x3st, c * 16)
                for j in range(2):
                    act.wait_ge(c_pj, pj3_at(c, (2 if nxt else 0) + j) + 1)
                    copy(c_o[:, j * 512:(j + 1) * 512], pj[j]).then_inc(c_pjf, 1)

            run_chunks(act, step)
            take_tiles(c_oT, tp3_at(NC - 1, 3))
            router_exp(NC - 1)

        def c_vector(dve, ch):
            def seq(ins):
                ch.link(ins)
                ch.wait()

            def router_scores(c):
                dve.wait_ge(r_ex, c + 1)
                seq(nc.vector.tensor_scalar(r_exp, r_exp, 1.0, None, ALU.add))
                dst = scores[:, c, :] if static(c) else scores[:, bass.ds(c, 1), :].rearrange("p a n -> p (a n)")
                nc.vector.reciprocal(dst, r_exp).then_inc(r_sc, 1)

            def step(c, par):
                first = static(c) and c == 0
                nxt = not static(c) or c + 1 < NC
                dve.wait_ge(c_lg, c + 1)
                seq(nc.vector.tensor_reduce(c_max, lg, AX, ALU.max))
                nc.vector.tensor_scalar(c_nmax, c_max, -1.0, None, ALU.mult).then_inc(c_nm, 1)
                dve.wait_ge(c_ex, c + 1)
                if not first:
                    dve.wait_ge(c_pvt, c)
                nc.vector.reciprocal(c_rden, c_sum).then_inc(c_rd, 1)
                if not first:
                    router_scores(c - 1)
                else:
                    ch.n += 1
                    dve.sem_inc(s_dve, 1)
                dve.wait_ge(c_pjf, pj3_at(c, 4 if nxt else 2))
                dve.wait_ge(c_xres_ld, c * 16 + 16)
                seq(nc.vector.scalar_tensor_tensor(c_o, c_xres, ALPHA, c_o, ALU.mult, ALU.add))
                for j in range(2):
                    ins = nc.vector.bn_stats(c_stats[:, j, :], c_o[:, j * 512:(j + 1) * 512])
                seq(ins)
                settled(dve)
                seq(nc.vector.bn_aggr(c_mv, c_stats.rearrange("p a b -> p (a b)")))
                nc.vector.tensor_scalar(c_var, c_mv[:, 1:2], LN_EPS, None, ALU.add).then_inc(c_rvar, 1)
                dve.wait_ge(c_rrs, c + 1)
                seq(nc.vector.scalar_tensor_tensor(c_o, c_o, c_mv[:, 0:1], lnx_g, ALU.subtract, ALU.mult))
                nc.vector.scalar_tensor_tensor(c_o, c_o, c_rstd, lnx_b, ALU.mult, ALU.add).then_inc(c_x3, 1)

            dve.wait_ge(c_const, 16 * N_CONST3)
            run_chunks(dve, step, ch)
            router_scores(NC - 1)

        def c_gpsimd(pool):
            def step(c, par):
                pool.wait_ge(c_rvar, c + 1)
                nc.gpsimd.tensor_tensor(c_rstd, c_var, neg_half[:, 0:1], ALU.pow).then_inc(c_rrs, 1)

            run_chunks(pool, step)

        yb_d = dram("expert_rows_scratch", [NB * P, D])
        m = Arena(arena[:, :], SB)
        m.at = shared_end
        w_gu = m.take(2, KT, 2 * FE)
        w_dn = m.take(2, 2, D)
        below = Arena(arena[:, :], c_end - NC * NE)
        below.at = m.at
        m.at = c_end
        tab3 = below.take(CONST3_W)
        r_bias = below.take(NE)
        lnm_g, lnm_b = below.take(D), below.take(D)
        assert below.at <= shared_end + KT * 2 * D
        sel = m.take(NC, NE)
        pair = [m.take(NC * NG) for _ in range(7)]
        gsum = m.take(NC, NG)
        g_best, g_idx = m.take(NC), m.take(NC)
        g_cand = m.take(NC, NG)
        ingrp = m.take(NC, NE)
        selm = m.take(NC, NE)
        cand = m.take(NC, NE)
        best, pick_i = m.take(NC), m.take(NC)
        pick = m.take(2, NC, NE)
        took = m.take(NC, NE)
        prod = m.take(NC, NE)
        gate = m.take(2, NC)
        gate_sum = m.take(NC)
        total = m.take(NC, NE)
        rank = m.take(NC, NE)
        base = m.take(NC + 1, NE)
        more = m.take(NE, NC)
        nblk, pend, pstart = m.take(NE), m.take(NE), m.take(NE)
        blk_cmp = m.take(NB, NE)
        blk_e = m.take(NB)
        place_e = m.take(2, NC)
        q_f, s_f = m.take(2 * NC), m.take(2 * NC)
        hot_s = m.take(2 * NC, P)
        hot_q = m.take(2 * NC, 2, NB)
        row_gate = m.take(NB)
        dest_i = m.take(2 * NC).bitcast(I32)
        q_i = m.take(2 * NC).bitcast(I32)
        s_i = m.take(2 * NC).bitcast(I32)
        blk_i = m.take(NB).bitcast(I32)
        exp_done = m.take(NE).bitcast(I32)
        done_f = m.take(NE)
        src_i = m.take(NB).bitcast(I32)
        xb = below.take(2, D)
        xbT = below.take(2, KT, P)
        e_th = below.take(FE)
        e_h = below.take(FE)
        e_hT = below.take(2, P)
        yb = below.take(2, D)
        xidx = m.take(2, 1).bitcast(I32)
        yidx = m.take(3, 2).bitcast(I32)
        f_x = below.take(3, D)
        f_y = below.take(3, 2, D)
        f_stats, f_mv, f_var, f_rstd = m.take(2, 6), m.take(2), m.take(1), m.take(1)

        def cst3(name):
            o, w = CONST3[name]
            return tab3[:, o:o + w]

        r_prefix = psum[:, 6, 0:NC * NE].rearrange("p (a n) -> p a n", a=NC)
        r_total = psum[:, 7, 0:NC * NE].rearrange("p (a n) -> p a n", a=NC)
        r_rows = psum[:, 6, 0:2 * NB]
        r_src, r_gate = r_rows[:, 0:NB], r_rows[:, NB:2 * NB]
        gu_ps = [psum[:, 4, :], psum[:, 5, :]]
        hT_ps = psum[:, 6, 0:2 * P].rearrange("p (a n) -> p a n", a=2)

        d_const = sem("d_const_loaded")
        d_vec = sem("d_vector_steps")
        d_mm = sem("d_tensor_steps")
        e_idx = sem("e_rows_known")
        e_gath = [sem("e_even_rows_gathered"), sem("e_odd_rows_gathered")]
        e_w = sem("e_weights_loaded")
        e_st, f_xl = sem("e_rows_stored"), sem("f_x_loaded")
        f_g = [*e_gath, sem("f_third_rows_gathered")]
        f_g_from = [16 * NB // 2, 16 * NB // 2, 0]

        def done(b, par, each):
            return (b // 2 + 1) * each if static(b) else b * (each // 2) + (each - par * (each // 2))

        e_tp, e_tpf, e_gu, e_tanh, e_hr = (sem("e_turned"), sem("e_turned_taken"), sem("e_gate_up_done"), sem("e_tanh_ready"),
                                           sem("e_hidden_ready"))
        e_ht, e_htt, e_pj, e_pjf = (sem("e_hidden_turned"), sem("e_hidden_taken"), sem("e_down_done"), sem("e_down_taken"))
        f_idx, f_acc, f_rv, f_rr, f_out, f_st = (
            sem("f_rows_known"), sem("f_sum_ready"),
            sem("f_row_var"), sem("f_row_rstd"), sem("f_out_ready"), sem("f_out_stored"))

        def d_sync(sp):
            for dst, src in ((tab3, t["tables3"]), (r_bias, t["router_bias_2"].partition_broadcast(P)),
                             (lnm_g, t["ln_moe_g_2"].partition_broadcast(P)), (lnm_b, t["ln_moe_b_2"].partition_broadcast(P))):
                sp.dma_start(dst, src).then_inc(d_const, 16)

        def d_vector(dve, ch):
            def seq(ins):
                ch.link(ins)
                ch.wait()

            def over(ap, n):
                return ap.unsqueeze(2).to_broadcast([P, ap.shape[1], n])

            def under(ap, n):
                return ap.unsqueeze(1).to_broadcast([P, n, ap.shape[1]])

            V = nc.vector
            dve.wait_ge(d_const, 16 * 4)
            dve.wait_ge(r_sc, NC)
            seq(V.tensor_tensor(sel, scores, under(r_bias, NC), ALU.add))
            four = sel.rearrange("p c (g e) -> p (c g) e", e=EPG)
            hi1, lo1, hi2, lo2, top, mid, low = pair
            V.tensor_tensor(hi1, four[:, :, 0], four[:, :, 1], ALU.max)
            V.tensor_tensor(lo1, four[:, :, 0], four[:, :, 1], ALU.min)
            V.tensor_tensor(hi2, four[:, :, 2], four[:, :, 3], ALU.max)
            seq(V.tensor_tensor(lo2, four[:, :, 2], four[:, :, 3], ALU.min))
            V.tensor_tensor(top, hi1, hi2, ALU.max)
            V.tensor_tensor(mid, hi1, hi2, ALU.min)
            seq(V.tensor_tensor(low, lo1, lo2, ALU.max))
            seq(V.tensor_tensor(mid, mid, low, ALU.max))
            seq(V.tensor_tensor(gsum.rearrange("p c g -> p (c g)"), top, mid, ALU.add))

            def first_of(dst, values, biggest, numbers, n):
                seq(V.tensor_reduce(biggest, values, AX, ALU.max))
                c_ = g_cand if n == NG else cand
                seq(V.tensor_tensor(c_, values, over(biggest, n), ALU.is_ge))
                seq(V.scalar_tensor_tensor(c_, under(numbers, NC), float(-n), c_, ALU.add, ALU.mult))
                seq(V.tensor_scalar(c_, c_, float(n), None, ALU.add))
                seq(V.tensor_reduce(dst, c_, AX, ALU.min))

            first_of(g_idx, gsum, g_best, cst3("group"), NG)
            seq(V.tensor_tensor(ingrp, under(cst3("group_of"), NC), over(g_idx, NE), ALU.is_equal))
            seq(V.tensor_tensor(selm, sel, ingrp, ALU.mult))
            seq(V.tensor_scalar(ingrp, ingrp, -1.0, FAR, ALU.add, ALU.mult))
            seq(V.tensor_tensor(selm, selm, ingrp, ALU.add))
            for k in range(2):
                first_of(pick_i, selm, best, cst3("expert"), NE)
                seq(V.tensor_tensor(pick[:, k], under(cst3("expert"), NC), over(pick_i, NE), ALU.is_equal))
                if k == 0:
                    seq(V.scalar_tensor_tensor(selm, pick[:, 0], -FAR, selm, ALU.mult, ALU.add))
                seq(V.tensor_tensor(prod, scores, pick[:, k], ALU.mult))
                seq(V.tensor_reduce(gate[:, k, :], prod, AX, ALU.add))
            V.tensor_tensor(took, pick[:, 0], pick[:, 1], ALU.add).then_inc(d_vec, 1)
            seq(V.tensor_tensor(gate_sum, gate[:, 0, :], gate[:, 1, :], ALU.add))
            seq(V.reciprocal(gate_sum, gate_sum))
            seq(V.tensor_tensor(gate, gate, under(gate_sum, 2), ALU.mult))
            dve.wait_ge(d_mm, 1)
            V.memset(base[:, 0, :], 0.0)
            V.tensor_copy(rank, r_prefix)
            seq(V.tensor_copy(total, r_total))
            for c in range(NC):
                seq(V.tensor_tensor(base[:, c + 1, :], base[:, c, :], total[:, c, :], ALU.add))
            seq(V.tensor_tensor(more, over(base[:, NC, :], NC), under(cst3("fills"), NE), ALU.is_gt))
            seq(V.tensor_reduce(nblk, more, AX, ALU.add))
            seq(V.tensor_tensor_scan(pend, cst3("one")[:, 0:NE], nblk, 0.0, ALU.mult, ALU.add))
            seq(V.tensor_tensor(pstart, pend, nblk, ALU.subtract))
            seq(V.tensor_scalar(pstart, pstart, float(P), None, ALU.mult))
            seq(V.tensor_tensor(rank, rank, base[:, 0:NC, :], ALU.add))
            seq(V.tensor_tensor(rank, rank, under(pstart, NC), ALU.add))
            for k in range(2):
                seq(V.tensor_tensor(prod, rank, pick[:, k], ALU.mult))
                seq(V.tensor_reduce(place_e[:, k, :], prod, AX, ALU.add))
            seq(V.tensor_tensor(blk_cmp, under(pend, NB), over(cst3("block"), NE), ALU.is_le))
            seq(V.tensor_reduce(blk_e, blk_cmp, AX, ALU.add))
            seq(V.tensor_scalar(blk_e, blk_e, float(NE - 1), None, ALU.min))
            V.tensor_scalar(done_f, pend, 2.0, 1.0, ALU.mult, ALU.add)
            seq(V.tensor_copy(blk_i, blk_e))
            V.tensor_copy(exp_done, done_f)
            seq(V.tensor_copy(dest_i, place_e.rearrange("p k c -> p (k c)")))
            V.tensor_scalar(q_i, dest_i, 7, None, ALU.logical_shift_right)
            seq(V.tensor_scalar(s_i, dest_i, P - 1, None, ALU.bitwise_and))
            V.tensor_copy(q_f, q_i)
            seq(V.tensor_copy(s_f, s_i))
            dve.wait_ge(c_x3st, 16 * NC)
            V.tensor_tensor(hot_s, under(cst3("place"), 2 * NC), over(s_f, P), ALU.is_equal)
            seq(V.tensor_tensor(hot_q[:, :, 0, :], under(cst3("block"), 2 * NC), over(q_f, NB), ALU.is_equal))
            seq(V.tensor_tensor(hot_q[:, :, 1, :], hot_q[:, :, 0, :], over(gate.rearrange("p k c -> p (k c)"), NB), ALU.mult))
            for k in range(2):
                ins = V.tensor_tensor(hot_q[:, k * NC:(k + 1) * NC, 0, :], hot_q[:, k * NC:(k + 1) * NC, 0, :],
                                      over(cst3("token"), NB), ALU.mult)
            ins.then_inc(d_vec, 1)
            dve.wait_ge(d_mm, 2)
            V.tensor_copy(src_i, r_src)
            V.tensor_copy(row_gate, r_gate).then_inc(d_vec, 1)

        def d_tensor(pe):
            pe.wait_ge(d_vec, 1)
            flat = took.rearrange("p c e -> p (c e)")
            nc.tensor.matmul(psum[:, 6, 0:NC * NE], cst3("before"), flat, start=True, stop=True)
            nc.tensor.matmul(psum[:, 7, 0:NC * NE], cst3("one"), flat, start=True, stop=True).then_inc(d_mm, 1)
            pe.wait_ge(d_vec, 2)
            for i in range(2 * NC):
                ins = nc.tensor.matmul(r_rows, hot_s[:, i, :], hot_q[:, i].rearrange("p a n -> p (a n)"),
                                       start=(i == 0), stop=(i == 2 * NC - 1))
            ins.then_inc(d_mm, 1)

        def load_expert(sp, e, slot):
            for dst, name in ((w_gu[:, slot, :, 0:FE], "w_gate_2"), (w_gu[:, slot, :, FE:2 * FE], "w_up_2"),
                              (w_dn[:, slot], "w_down_2")):
                src = t[name].rearrange("e (k p) n -> e p k n", p=P)
                src = src[e] if static(e) else src[bass.ds(e, 1)].rearrange("e p k n -> (e p) k n")
                sp.dma_start(dst, src).then_inc(e_w, 16)

        def e_sync_first(sp):
            sp.wait_ge(c_pjf, SETUP_PJ)
            d_sync(sp)
            load_expert(sp, 0, 0)
            sp.wait_ge(e_w, 48)
            load_expert(sp, 1, 1)

        def e_sync(sp):

            def next_expert(e, slot):
                through = sp.value_load(exp_done[0:1, bass.ds(e - 2, 1)], min_val=1, max_val=2 * NB + 1)
                sp.wait_ge(e_pj, through)
                settled(sp)
                sp.wait_ge(e_w, e * 48)
                load_expert(sp, e, slot)

            sp.wait_ge(d_vec, 3)
            with sp.Fori(1, NE // 2) as i:
                next_expert(2 * i, 0)
                next_expert(2 * i + 1, 1)

        def e_tensor(pe):
            def front(b, par, at):
                pe.wait_ge(e_gath[par], done(b, par, 16))
                if not static(at) or at:
                    pe.wait_ge(e_tpf, at)
                for k in range(KT):
                    ins = nc.tensor.transpose(tp[:, k, :], xb[:, par, k * P:(k + 1) * P], ident)
                ins.then_inc(e_tp, 1)

            def expert(b):
                at = slice(b, b + 1) if static(b) else bass.ds(b, 1)
                return pe.value_load(blk_i[0:1, at], min_val=0, max_val=NE - 1)

            def buffer_of(e):
                return bass.ds(e & 1, 1)

            def gate_up(b, par, e):
                pe.wait_ge(e_w, e * 48 + 48)
                pe.wait_ge(e_tpf, b + 1)
                if not static(b) or b >= 2:
                    pe.wait_ge(e_hr, b - 1)
                for k in range(KT):
                    ins = nc.tensor.matmul(gu_ps[par], xbT[:, par, k, :], w_gu[:, buffer_of(e), k, :].rearrange("p a n -> p (a n)"),
                                           start=(k == 0), stop=(k == KT - 1))
                ins.then_inc(e_gu, 1)

            pe.sem_inc(e_pj, 1)
            pe.wait_ge(d_vec, 3)
            front(0, 0, 0)
            front(1, 1, 1)
            gate_up(0, 0, expert(0))

            def step(b, par):
                nxt = not static(b) or b + 1 < NB
                e = expert(b)
                pe.wait_ge(e_hr, b + 1)
                if not static(b) or b:
                    pe.wait_ge(e_htt, b)
                for k in range(2):
                    ins = nc.tensor.transpose(hT_ps[:, k, :], e_h[:, k * P:(k + 1) * P], ident)
                ins.then_inc(e_ht, 1)
                if nxt:
                    gate_up(b + 1, 1 - par, expert(b + 1))
                if not static(b) or b + 2 < NB:
                    front(b + 2, par, b + 2)
                pe.wait_ge(e_htt, b + 1)
                for j in range(2):
                    if not static(b) or b:
                        pe.wait_ge(e_pjf, b * 2 + (j - 1))
                    for k in range(2):
                        ins = nc.tensor.matmul(pj[j], e_hT[:, k, :],
                                               w_dn[:, buffer_of(e), k, j * 512:(j + 1) * 512].rearrange("p a n -> p (a n)"),
                                               start=(k == 0), stop=(k == 1))
                    ins.then_inc(e_pj, 1)

            run_chunks(pe, step, n=NB)

        def e_scalar(act):
            def copy(dst, src, scale=1.0):
                return nc.scalar.activation(dst, src, ACT.Copy, scale=scale)

            def take_x(b, par):
                act.wait_ge(e_tp, b + 1)
                copy(xbT[:, par, 0:4, :], tp[:, 0:4, :])
                copy(xbT[:, par, 4:8, :], tp[:, 4:8, :]).then_inc(e_tpf, 1)

            def tanh(b, par):
                act.wait_ge(e_gu, b + 1)
                if not static(b) or b:
                    act.wait_ge(e_hr, b)
                nc.scalar.activation(e_th, gu_ps[par][:, 0:FE], ACT.Tanh, scale=0.5).then_inc(e_tanh, 1)

            act.wait_ge(d_vec, 3)
            take_x(0, 0)
            take_x(1, 1)
            tanh(0, 0)

            def step(b, par):
                nxt = not static(b) or b + 1 < NB
                act.wait_ge(e_ht, b + 1)
                copy(e_hT, hT_ps).then_inc(e_htt, 1)
                if nxt:
                    tanh(b + 1, 1 - par)
                if not static(b) or b + 2 < NB:
                    take_x(b + 2, par)
                g = row_gate[:, b:b + 1] if static(b) else row_gate[:, bass.ds(b, 1)]
                for j in range(2):
                    act.wait_ge(e_pj, b * 2 + (j + 2))
                    settled(act)
                    copy(yb[:, par, j * 512:(j + 1) * 512], pj[j], g).then_inc(e_pjf, 1)
                act.wait_ge(e_pjf, b * 2 + 2)
                if not static(b) or b:
                    settled(act)
                    act.wait_ge(e_st, b * 16)
                act.dma_start(rows(yb_d, b), yb[:, par, :]).then_inc(e_st, 16)

            run_chunks(act, step, n=NB)
            act.wait_ge(e_st, 16 * NB)

        def e_vector(dve, ch):
            def index(b, par):
                src = src_i[:, b:b + 1] if static(b) else src_i[:, bass.ds(b, 1)]
                nc.vector.tensor_copy(xidx[:, par, :], src).then_inc(e_idx, 1)

            def hidden(b, par):
                dve.wait_ge(e_tanh, b + 1)
                if not static(b) or b:
                    dve.wait_ge(e_ht, b)
                ch.link(nc.vector.scalar_tensor_tensor(e_h, e_th, 1.0, gu_ps[par][:, 0:FE], ALU.add, ALU.mult))
                ch.wait()
                nc.vector.scalar_tensor_tensor(e_h, e_h, 0.5, gu_ps[par][:, FE:2 * FE], ALU.mult, ALU.mult).then_inc(e_hr, 1)

            dve.wait_ge(d_vec, 3)
            index(0, 0)
            index(1, 1)
            hidden(0, 0)

            def step(b, par):
                if not static(b) or b + 2 < NB:
                    dve.wait_ge(e_gath[par], done(b, par, 16))
                    index(b + 2, par)
                if not static(b) or b + 1 < NB:
                    hidden(b + 1, 1 - par)

            run_chunks(dve, step, ch, n=NB)

        def e_gpsimd(pool):
            def gather(b, par):
                pool.wait_ge(e_idx, b + 1)
                if not static(b) or b >= 2:
                    pool.wait_ge(e_tp, b - 1)
                settled(pool)
                nc.gpsimd.indirect_dma_start(out=xb[:, par, :], out_offset=None, in_=x3_d,
                                             in_offset=bass.IndirectOffsetOnAxis(ap=xidx[:, par, :], axis=0)).then_inc(e_gath[par], 16)

            pool.wait_ge(c_x3st, 16 * NC)
            gather(0, 0)
            gather(1, 1)

            def step(b, par):
                if not static(b) or b + 2 < NB:
                    gather(b + 2, par)

            run_chunks(pool, step, n=NB)

        def f_sync(sp):
            for c in range(3):
                sp.dma_start(f_x[:, c, :], rows(x3_d, c)).then_inc(f_xl, 16)
                sp.wait_ge(f_xl, 16 * (c + 1))

            def step(c, par, turn):
                sp.wait_ge(f_out, c + 1)
                sp.dma_start(rows(out, c), f_x[:, par, :]).then_inc(f_st, 16)
                if not static(c) or c + 3 < NC:
                    sp.wait_ge(f_st, c * 16 + 16)
                    settled(sp)
                    sp.wait_ge(f_xl, c * 16 + 48)
                    sp.dma_start(f_x[:, par, :], rows(x3_d, c + 3)).then_inc(f_xl, 16)

            run_thirds(sp, step)
            sp.wait_ge(f_st, 16 * NC)

        def f_gpsimd(pool):
            def gather(c, par):
                pool.wait_ge(f_idx, c + 1)
                if not static(c) or c >= 3:
                    pool.wait_ge(f_acc, c - 2)
                settled(pool)
                for k in range(2):
                    nc.gpsimd.indirect_dma_start(out=f_y[:, par, k, :], out_offset=None, in_=yb_d,
                                                 in_offset=bass.IndirectOffsetOnAxis(ap=yidx[:, par, k:k + 1], axis=0)).then_inc(f_g[par], 16)

            pool.wait_ge(e_st, 16 * NB)
            for c in range(3):
                gather(c, c)

            def step(c, par, turn):
                pool.wait_ge(f_rv, c + 1)
                nc.gpsimd.tensor_tensor(f_rstd, f_var, neg_half[:, 0:1], ALU.pow).then_inc(f_rr, 1)
                if not static(c) or c + 3 < NC:
                    gather(c + 3, par)

            run_thirds(pool, step)

        def f_vector(dve, ch):
            def seq(ins):
                ch.link(ins)
                ch.wait()

            both = dest_i.rearrange("p (k c) -> p c k", k=2)

            def index(c, par):
                src = both[:, c, :] if static(c) else both[:, bass.ds(c, 1), :].rearrange("p a k -> p (a k)")
                nc.vector.tensor_copy(yidx[:, par, :], src).then_inc(f_idx, 1)

            for c in range(3):
                index(c, c)

            def step(c, par, turn):
                x = f_x[:, par, :]
                dve.wait_ge(f_xl, c * 16 + 16)
                dve.wait_ge(f_g[par], turn * 32 + (f_g_from[par] + 32))
                seq(nc.vector.scalar_tensor_tensor(x, x, ALPHA, f_y[:, par, 0, :], ALU.mult, ALU.add))
                if not static(c) or c + 3 < NC:
                    index(c + 3, par)
                nc.vector.tensor_tensor(x, x, f_y[:, par, 1, :], ALU.add).then_inc(f_acc, 1)
                dve.wait_ge(f_acc, c + 1)
                for j in range(2):
                    ins = nc.vector.bn_stats(f_stats[:, j, :], x[:, j * 512:(j + 1) * 512])
                seq(ins)
                settled(dve)
                seq(nc.vector.bn_aggr(f_mv, f_stats.rearrange("p a b -> p (a b)")))
                nc.vector.tensor_scalar(f_var, f_mv[:, 1:2], LN_EPS, None, ALU.add).then_inc(f_rv, 1)
                seq(nc.vector.scalar_tensor_tensor(x, x, f_mv[:, 0:1], lnm_g, ALU.subtract, ALU.mult))
                dve.wait_ge(f_rr, c + 1)
                nc.vector.scalar_tensor_tensor(x, x, f_rstd, lnm_b, ALU.mult, ALU.add).then_inc(f_out, 1)

            run_thirds(dve, step, ch)

        block = ctx.enter_context(nc.Block())

        last = {"a": 1, "b": 2, "c": 3, "all": 4}[stop_after]

        @block.sync
        def _(sp):
            a_sync(sp, (lambda: b_sync(sp)) if last > 1 else None)
            a_sync_end(sp)
            if last > 1:
                b_sync_main(sp, (lambda: c_sync(sp)) if last > 2 else None)
                b_sync_end(sp)
            if last > 2:
                c_sync_main(sp, (lambda: e_sync_first(sp)) if last > 3 else None)
            if last > 3:
                e_sync(sp)
                f_sync(sp)

        @block.tensor
        def _(pe):
            for phase in (a_tensor, b_tensor, c_tensor, d_tensor, e_tensor)[:last if last < 4 else 5]:
                phase(pe)

        @block.scalar
        def _(act):
            for phase in (a_scalar, b_scalar, c_scalar, e_scalar)[:last]:
                phase(act)

        @block.vector
        def _(dve):
            ch = Chain(dve, s_dve)
            for phase in (a_vector, b_vector, c_vector, d_vector, e_vector, f_vector)[:last if last < 4 else 6]:
                phase(dve, ch)

        @block.gpsimd
        def _(pool):
            for phase in (a_gpsimd, b_gpsimd, c_gpsimd, e_gpsimd, f_gpsimd)[:last if last < 4 else 5]:
                phase(pool)


_SHAPES = {
    "x": (S, D), "mem": (MEM, D), "pre_norm_g": (D,), "post_norm_g": (D,), "mem_norm_g": (D,), "w_in": (D, IN1),
    "w_mem_kv": (D, 2 * MEM), "v_norm_g": (A_W,), "v_norm_b": (A_W,), "w_spatial": (4, P, P), "b_spatial": (4, P),
    "attn_sinks": (4,), "rel_bias": (SWA_BUCKETS, 4), "w_out": (D, D),
    "w_in_2": (D, IN2), "b_i_2": (LH,), "b_f_2": (LH,), "conv_qk_2": (CONV, D), "head_norm_g_2": (M_W,), "pool_w_2": (4, P, P),
    "pool_scale_2": (M_W,), "w_mix_out_2": (D, D), "ln_mix_g_2": (D,), "ln_mix_b_2": (D,),
    "mem_2": (MEM, D), "w_xq_2": (D, D), "w_xkv_2": (D, 2 * D), "w_xo_2": (D, D), "ln_x_g_2": (D,), "ln_x_b_2": (D,),
    "router_w_2": (D, NE), "router_bias_2": (NE,), "w_gate_2": (NE, D, FE), "w_up_2": (NE, D, FE), "w_down_2": (NE, FE, D),
    "ln_moe_g_2": (D,), "ln_moe_b_2": (D,),
}


def kernel(**inputs):
    import concourse.bacc as bacc
    from concourse.bass_utils import run_bass_kernel_spmd

    nc = bacc.Bacc("TRN2", target_bir_lowering=False, num_devices=1)
    arrays = {n: np.ascontiguousarray(np.asarray(inputs[n]).reshape(shape)) for n, shape in _SHAPES.items()}
    arrays["ident"] = np.eye(P, dtype=np.float32)
    for name, tables in (("tables", shape_constants()), ("tables2", mixer_constants()), ("tables3", routing_constants())):
        arrays[name] = np.ascontiguousarray(np.concatenate(list(tables.values()), 1))
    aps = {n: nc.dram_tensor(n, a.shape, mybir.dt.from_np(a.dtype), kind="ExternalInput").ap() for n, a in arrays.items()}
    out = nc.dram_tensor("result", (S, D), F32, kind="ExternalOutput").ap()
    build(nc, aps, out)
    r = run_bass_kernel_spmd(nc, [arrays], core_ids=[0])
    return r.results[0]["result"].reshape(1, S, D)
```

```python
from contextlib import ExitStack

import numpy as np

import concourse.bass as bass
from concourse import mybir

F32 = mybir.dt.float32
F16 = mybir.dt.float16
I32 = mybir.dt.int32
ALU = mybir.AluOpType
ACT = mybir.ActivationFunctionType
AX = mybir.AxisListType.X

P = 128
S = 2048
D = 1024
NC = S // P
KT = D // P
MEM = 256
EPS = 1e-6
LN_EPS = 1e-5
NEG = -1e30
FAR = 1e30
HALF_TOP = 4096.0
EXPONENT = 0x7F800000
INV_EXPONENT = 254 << 23
TINY, HUGE = 1e-30, 1e37
GELU_C = 0.7978845608028654
GELU_A = 0.044715

A_W = 512
HD = 64
SWA_BUCKETS = 32
IN1 = 2816
QOFF, KOFF, VOFF, MQOFF, ZOFF = 1024, 1280, 1408, 1536, 1792
GROUPS1 = [(0, 512), (512, 512), (1024, 512), (1536, 512), (2048, 512), (2560, 256)]
EXT = 3 * P - 1
MEM_ORDER = (0, 2, 1, 3)

M_W = 512
LH = 4
LD = 128
IN2 = 2568
GATE = 2048
POOL = 2056
CONV = 4
POOL_WINDOWS = (2, 4, 8, 16)
ALPHA = 2.0 ** 0.25
XH = 4
XD = D // XH
NE = 16
NG = 4
EPG = NE // NG
FE = 256
NB = 2 * S // P + NE
LN_TERMS = [1.0 / (2 * k + 1) for k in range(7, 0, -1)]


def t5_buckets(dist):
    n = np.maximum(dist, 0)
    exact = SWA_BUCKETS // 2
    large = exact + (np.log(np.maximum(n, 1) / exact) / np.log(128 / exact) * (SWA_BUCKETS - exact)).astype(np.int32)
    return np.where(n < exact, n, np.minimum(large, SWA_BUCKETS - 1)).astype(np.int32)


def shape_constants():
    t = np.arange(P)
    c = {}
    c["causal"] = (t[None, :] <= t[:, None]) * 1.0
    j = np.arange(2 * P)
    dist = t[:, None] + P - j[None, :]
    c["window"] = np.where((dist >= 0) & (dist < P), 0.0, NEG)
    d = 2 * P - 1 - np.arange(EXT)
    hot = (t5_buckets(d)[None, :] == t[:, None]) & (d >= 0) & (d < P)
    c["bucket"] = hot * 1.0
    return {k: np.ascontiguousarray(v, np.float32) for k, v in c.items()}


def mixer_constants():
    t = np.arange(P)
    back = t[None, :] - t[:, None]
    c = {"pool_cur": [], "pool_prev": [], "pool_first": []}
    for w in POOL_WINDOWS:
        inside = (back >= 0) & (back < w)
        c["pool_cur"].append(inside / w - np.eye(P))
        c["pool_prev"].append((back + P < w) / w)
        c["pool_first"].append(inside / np.minimum(t + 1, w)[None, :] - np.eye(P))
    c = {k: np.concatenate(v, 1) for k, v in c.items()}
    c["after"] = np.where(back >= 0, 0.0, NEG)
    c["head_neg"] = -np.repeat(np.eye(P)[:, 0:LH], P, 1)
    return {k: np.ascontiguousarray(v, np.float32) for k, v in c.items()}


def routing_constants():
    p = np.arange(P)[:, None]
    row = lambda v: np.tile(np.asarray(v, np.float64)[None, :], (P, 1))
    c = {
        "expert": row(np.arange(NE)),
        "group_of": row(np.arange(NE) // EPG),
        "group": row(np.arange(NG)),
        "one": row(np.ones(P)),
        "fills": row(P * np.arange(NC)),
        "block": row(np.arange(NB)),
        "place": row(np.arange(P)),
        "token": np.arange(NC)[None, :] * P + p,
        "before": (p < np.arange(P)[None, :]) * 1.0,
    }
    return {k: np.ascontiguousarray(v, np.float32) for k, v in c.items()}


def layout(tables):
    at, out = 0, {}
    for k, v in tables.items():
        out[k] = (at, v.shape[1])
        at += v.shape[1]
    return out, at


CONST, CONST_W = layout(shape_constants())
CONST2, CONST2_W = layout(mixer_constants())
CONST3, CONST3_W = layout(routing_constants())



class Arena:

    def __init__(self, ap, width):
        self.ap, self.width, self.at = ap, width, 0

    def take(self, *shape):
        n = int(np.prod(shape))
        out = self.ap[:, self.at:self.at + n]
        self.at += n
        assert self.at <= self.width, (self.at, self.width)
        if len(shape) == 2:
            out = out.rearrange("p (a b) -> p a b", a=shape[0])
        if len(shape) == 3:
            out = out.rearrange("p (a b c) -> p a b c", a=shape[0], b=shape[1])
        return out


def halves(ap, k):
    both = ap.bitcast(F16).rearrange("p (a k n) -> p a k n", a=2, k=k)
    return both[:, 0], both[:, 1]


class Chain:

    def __init__(self, eng, sem):
        self.eng, self.sem, self.base, self.n = eng, sem, 0, 0

    def link(self, ins):
        self.n += 1
        ins.then_inc(self.sem, 1)
        return ins

    def wait(self):
        self.eng.wait_ge(self.sem, self.base + self.n)


def run_chunks(eng, step, chain=None, n=NC, before_last=None):
    pairs = (n - 4) // 2
    before = chain.n if chain else 0
    step(0, 0)
    if chain:
        per, first = chain.n - before, chain.n
    with eng.Fori(0, pairs) as i:
        if chain:
            chain.base, chain.n = i * (2 * per) + first, 0
        step(2 * i + 1, 1)
        step(2 * i + 2, 0)
    if chain:
        assert chain.n == 2 * per, (chain.n, per)
        chain.base, chain.n = 0, first + 2 * per * pairs
    for c in range(n - 3, n):
        if before_last and c == n - 1:
            before_last()
        step(c, c % 2)


def run_thirds(eng, step, chain=None, n=NC):
    threes = (n - 4) // 3
    before = chain.n if chain else 0
    step(0, 0, 0)
    if chain:
        per, first = chain.n - before, chain.n
    with eng.Fori(0, threes) as i:
        if chain:
            chain.base, chain.n = i * (3 * per) + first, 0
        step(3 * i + 1, 1, i)
        step(3 * i + 2, 2, i)
        step(3 * i + 3, 0, i + 1)
    if chain:
        assert chain.n == 3 * per, (chain.n, per)
        chain.base, chain.n = 0, first + 3 * per * threes
    for c in range(n - 3, n):
        step(c, c % 3, c // 3)


def static(c):
    return isinstance(c, int)


def rows(ap, c):
    return ap[c * P:(c + 1) * P, :] if static(c) else ap[bass.ds(c * P, P), :]


def build(nc, t, out, stop_after="all"):
    ctx = ExitStack()
    with ctx:
        def sem(name):
            return ctx.enter_context(nc.semaphore(name))

        def dram(name, shape, dt=F32):
            return nc.dram_tensor(name, shape, dt, kind="Internal").ap()

        SB = 53208
        arena = ctx.enter_context(nc.sbuf_tensor("arena", [P, SB], F32))
        psum = ctx.enter_context(nc.psum_tensor("psum", [P, 8, 512], F32))


        s_half = sem("neg_half_written")

        waited = sem("waited")

        def settled(eng):
            eng.sem_inc(waited, 1)

        x1_d = out if stop_after == "a" else dram("x1_scratch", [S, D])
        ext_d = dram("bias_scratch", [4, P * EXT])

        h_am, h_gm, h_bc = sem("abs_max"), sem("abs_max_of_all"), sem("abs_max_spread")
        h_sc, h_wh, h_wl = sem("weight_scale_ready"), sem("upper_weights"), sem("lower_weights")
        B_GROUPS = 5
        C_SCALE, C_TILE = 1, B_GROUPS * KT

        def power(seq, dst, inv, largest):
            seq(nc.vector.tensor_scalar(dst, largest, TINY, HUGE, ALU.max, ALU.min))
            seq(nc.vector.tensor_scalar(dst.bitcast(I32), dst.bitcast(I32), EXPONENT, None, ALU.bitwise_and))
            seq(nc.vector.tensor_scalar(inv.bitcast(I32), dst.bitcast(I32), -1, INV_EXPONENT, ALU.mult, ALU.add))
            return nc.vector.tensor_scalar(inv, inv, HALF_TOP, None, ALU.mult)

        m = Arena(arena[:, :], SB)
        ident = m.take(P)
        chip_const = m.take(4)
        neg_half = chip_const

        shared_end = m.at

        W = m.take(KT * (IN1 + D))
        w_in = W[:, 0:KT * IN1].rearrange("p (k n) -> p k n", k=KT)
        w_out = W[:, KT * IN1:].rearrange("p (k n) -> p k n", k=KT)
        w_kv = W[:, KT * IN1:KT * IN1 + KT * 512].rearrange("p (k n) -> p k n", k=KT)
        x_in = m.take(D)
        x_res = m.take(D)
        xn = m.take(D)
        xT = m.take(KT, P)
        proj = m.take(2, IN1)
        free_end_a = m.at - IN1
        v_win = m.take(2, P)
        tmp = m.take(D)
        qT = m.take(2, P)
        kT = m.take(2, P)
        mqT = m.take(2, P)
        prob = m.take(4, 2 * P)
        pT = m.take(KT, P)
        tables = pT.rearrange("p a b -> p (a b)")[:, 0:CONST_W]

        def cst(name):
            o, n = CONST[name]
            return tables[:, o:o + n]

        out_stage = m.take(2 * D)
        o_sb = out_stage[:, 0:D]
        junk = out_stage[:, D:2 * D]
        ext_rows = out_stage[:, 0:4 * EXT].rearrange("p (h i) -> p h i", h=4)
        bias = m.take(4, 2 * P)
        g_pre = m.take(D)
        g_post = m.take(D)
        vn_g = m.take(A_W)
        vn_b = m.take(A_W)
        wsT = m.take(4, P)
        mkT = m.take(2, MEM)
        mv = m.take(2, MEM)
        bsT = m.take(4)
        sink = m.take(4)
        relb = m.take(4)
        x_ms, x_rstd = m.take(1), m.take(1)
        o_ss, o_ms, o_rstd = m.take(2), m.take(1), m.take(1)
        swa_max, swa_nmax, sink_arg, sink_exp = m.take(4), m.take(4), m.take(4), m.take(4)
        swa_sum, swa_rden = m.take(4), m.take(4)
        mem_max, mem_nmax, mem_sum, mem_rden = m.take(4), m.take(4), m.take(4), m.take(4)
        v_stats, v_mv, v_var, v_rstd = m.take(4, 6), m.take(4, 2), m.take(4), m.take(4)

        mem_rows = proj[:, 0, 0:2 * D].rearrange("p (a n) -> p a n", a=2)
        memT = proj[:, 1, 0:2 * D].rearrange("p (k n) -> p k n", k=KT)
        mem_g = x_res

        pj = [psum[:, 0, :], psum[:, 1, :]]
        tp = psum[:, 2:4, :].rearrange("p b (a n) -> p (b a) n", a=4)
        lg = psum[:, 4:6, :].rearrange("p b (a n) -> p (b a) n", a=2)
        sgu = psum[:, 6, :].rearrange("p (a n) -> p a n", a=4)
        pv = psum[:, 7, :].rearrange("p (a n) -> p a n", a=8)
        pv2 = psum[:, 6, :].rearrange("p (a n) -> p a n", a=8)

        s_const = sem("a_const_loaded")
        s_wkv = sem("a_w_kv_loaded")
        s_win = [sem(f"w_in_loaded{g}") for g in range(len(GROUPS1))]
        s_wout = sem("a_w_out_loaded")
        s_ws = sem("a_spatial_masked")
        s_rel = sem("a_rel_bias_spread")
        s_extp = sem("a_bias_product")
        s_exts = sem("a_bias_rows_ready")
        s_ext_st = sem("a_bias_stored")
        s_ext_ld = sem("a_bias_loaded")
        s_memms, s_memr, s_memn = sem("a_mem_meansq"), sem("a_mem_rstd"), sem("a_mem_normed")
        s_mkv, s_mkvt = sem("a_mem_kv_product"), sem("a_mem_kv_taken")
        s_pad = sem("a_window_padded")
        s_xin, s_xres = sem("a_x_in_loaded"), sem("a_x_res_loaded")
        s_xms, s_xrs, s_xn = sem("a_x_meansq"), sem("a_x_rstd"), sem("a_x_normed")
        s_tp, s_tpf = sem("a_turned"), sem("a_turned_taken")
        s_pj, s_pjf = sem("a_proj_done"), sem("a_proj_taken")
        s_garg, s_gth, s_gel = sem("a_gelu_arg"), sem("a_gelu_tanh"), sem("a_gelu_ready")
        s_vvar, s_vrs, s_vn = sem("a_v_var"), sem("a_v_rstd"), sem("a_v_normed")
        s_qk = sem("a_queries_keys_ready")
        s_z = sem("a_z_ready")
        s_sgu, s_ya = sem("a_spatial_done"), sem("a_spatial_taken")
        s_lg, s_lgf = sem("a_logits_done"), sem("a_window_logits_taken")
        s_nm, s_ex = sem("a_window_max"), sem("a_window_exp")
        s_nm2, s_ex2 = sem("a_memory_max"), sem("a_memory_exp")
        s_pv, s_y = sem("a_values_done"), sem("a_y_ready")
        s_oms, s_ors, s_x1 = sem("a_out_meansq"), sem("a_out_rstd"), sem("a_x1_ready")
        s_x1st = sem("a_x1_stored")
        s_dve = sem("vector_chain")

        N_CONST = 12

        def tp_at(c, n):
            return c * 5 + (4 + n)

        def pj_at(c, n):
            return c * 8 + (6 + n)

        def a_sync(sp, before_last):
            sp.dma_start(ident, t["ident"]).then_inc(s_const, 16)
            sp.dma_start(tables, t["tables"]).then_inc(s_const, 16)
            sp.dma_start(mem_rows, t["mem"].rearrange("(a p) n -> p a n", p=P)).then_inc(s_const, 16)
            for dst, name in ((mem_g, "mem_norm_g"), (g_pre, "pre_norm_g"), (g_post, "post_norm_g"), (vn_g, "v_norm_g"),
                              (vn_b, "v_norm_b"), (sink, "attn_sinks")):
                sp.dma_start(dst, t[name].partition_broadcast(P)).then_inc(s_const, 16)
            sp.dma_start(wsT, t["w_spatial"].rearrange("g t s -> t g s")).then_inc(s_const, 16)
            sp.dma_start(relb[0:SWA_BUCKETS, :], t["rel_bias"]).then_inc(s_const, 16)
            with nc.allow_non_contiguous_dma(reason="512 values once"):
                sp.dma_start(bsT, t["b_spatial"].rearrange("g t -> t g")).then_inc(s_const, 16)
            sp.dma_start(x_in, rows(t["x"], 0)).then_inc(s_xin, 16)
            sp.dma_start(w_kv, t["w_mem_kv"].rearrange("(k p) n -> p k n", p=P)).then_inc(s_wkv, 16)
            for g, (o, n) in enumerate(GROUPS1):
                sp.dma_start(w_in[:, :, o:o + n], t["w_in"].rearrange("(k p) n -> p k n", p=P)[:, :, o:o + n])\
                  .then_inc(s_win[g], 16)
            sp.wait_ge(s_exts, 1)
            sp.dma_start(ext_d.rearrange("h (q i) -> q h i", i=EXT), ext_rows).then_inc(s_ext_st, 16)
            sp.wait_ge(s_ext_st, 16)
            sp.dma_start(bias, bass.AP(ext_d.tensor, P - 1, [[EXT - 1, P], [P * EXT, 4], [1, 2 * P]])).then_inc(s_ext_ld, 16)
            sp.wait_ge(s_mkv, 2)
            sp.dma_start(w_out, t["w_out"].rearrange("(k p) n -> p k n", p=P)).then_inc(s_wout, 16)
            sp.wait_ge(s_xn, 1)
            sp.dma_start(x_in, rows(t["x"], 1)).then_inc(s_xin, 16)
            sp.wait_ge(s_memn, 2)
            sp.dma_start(x_res, rows(t["x"], 0)).then_inc(s_xres, 16)

            def step(c, par):
                if not static(c) or c + 2 < NC:
                    sp.wait_ge(s_xn, c + 2)
                    sp.dma_start(x_in, rows(t["x"], c + 2)).then_inc(s_xin, 16)
                sp.wait_ge(s_x1, c + 1)
                sp.dma_start(rows(x1_d, c), o_sb).then_inc(s_x1st, 16)
                if not static(c) or c + 1 < NC:
                    sp.dma_start(x_res, rows(t["x"], c + 1)).then_inc(s_xres, 16)

            run_chunks(sp, step, before_last=before_last)

        def a_sync_end(sp):
            sp.wait_ge(s_x1st, 16 * NC)

        def a_tensor(pe):
            def turn(src, at):
                if not static(at) or at:
                    pe.wait_ge(s_tpf, at)
                for i, tile in enumerate(src):
                    ins = nc.tensor.transpose(tp[:, i, :], tile, ident)
                ins.then_inc(s_tp, 1)

            def tiles(ap, n):
                return [ap[:, k * P:(k + 1) * P] for k in range(n)]

            def front(c, at):
                pe.wait_ge(s_xn, c + 1)
                turn(tiles(xn, KT), at)

            def group(c, g, at):
                o, n = GROUPS1[g]
                if not static(at) or at >= 2:
                    pe.wait_ge(s_pjf, at - 1)
                if static(c) and c == 0:
                    pe.wait_ge(s_win[g], 16)
                for k in range(KT):
                    ins = nc.tensor.matmul(pj[g % 2][:, 0:n], xT[:, k, :], w_in[:, k, o:o + n],
                                           start=(k == 0), stop=(k == KT - 1))
                ins.then_inc(s_pj, 1)

            pe.wait_ge(s_ws, 1)
            turn([wsT[:, g, :] for g in range(4)], 0)
            pe.wait_ge(s_rel, 1)
            for h in range(4):
                ins = nc.tensor.matmul(psum[:, 4 + h, 0:EXT], tmp[0:SWA_BUCKETS, h * P:(h + 1) * P],
                                       cst("bucket")[0:SWA_BUCKETS, :], start=True, stop=True)
            ins.then_inc(s_extp, 1)
            for a in range(2):
                pe.wait_ge(s_memn, a + 1)
                turn(tiles(mem_rows[:, a, :], KT), 1 + a)
            pe.wait_ge(s_tpf, 3)
            pe.wait_ge(s_wkv, 16)
            pe.wait_ge(s_exts, 1)
            for a in range(2):
                for k in range(KT):
                    ins = nc.tensor.matmul(psum[:, 4, a * MEM:(a + 1) * MEM], w_kv[:, k, a * P:(a + 1) * P], memT[:, k, :],
                                           start=(k == 0), stop=(k == KT - 1))
            ins.then_inc(s_mkv, 1)
            for a in range(2):
                for k in range(KT):
                    ins = nc.tensor.matmul(psum[:, 5, a * MEM:(a + 1) * MEM], memT[:, k, a * P:(a + 1) * P],
                                           w_kv[:, k, MEM:2 * MEM], start=(k == 0), stop=(k == KT - 1))
            ins.then_inc(s_mkv, 1)
            front(0, 3)
            pe.wait_ge(s_tpf, 4)
            for g in range(6):
                group(0, g, g)
            pe.wait_ge(s_mkvt, 2)
            pe.wait_ge(s_pad, 1)

            def step(c, par):
                nxt = not static(c) or c + 1 < NC
                pr = proj[:, par, :]
                n = 0
                if nxt:
                    front(c + 1, tp_at(c, 0))
                    n = 1
                pe.wait_ge(s_vn, c + 1)
                if not static(c) or c:
                    pe.wait_ge(s_ya, c)
                for g in range(4):
                    ins = nc.tensor.matmul(sgu[:, g, :], wsT[:, g, :], pr[:, A_W + g * P:A_W + (g + 1) * P],
                                           start=True, stop=True)
                ins.then_inc(s_sgu, 1)
                pe.wait_ge(s_qk, c + 1)
                turn(tiles(pr[:, QOFF:], 3) + tiles(pr[:, MQOFF:], 2), tp_at(c, n))
                pe.wait_ge(s_tpf, tp_at(c, n) + 1)
                if nxt:
                    group(c + 1, 0, pj_at(c, 0))
                if not static(c) or c:
                    pe.wait_ge(s_ex2, c)
                for h in range(4):
                    half = slice(HD * (h // 2), HD * (h // 2) + HD)
                    ins = nc.tensor.matmul(lg[:, h, :], qT[half, h % 2, :], kT[half, :, :], start=True, stop=True)
                ins.then_inc(s_lg, 1)
                if nxt:
                    group(c + 1, 1, pj_at(c, 1))
                pe.wait_ge(s_lgf, c + 1)
                for i, h in enumerate(MEM_ORDER):
                    half = slice(HD * (h % 2), HD * (h % 2) + HD)
                    ins = nc.tensor.matmul(lg[:, i, :], mqT[half, h // 2, :], mkT[half, h // 2, :], start=True, stop=True)
                ins.then_inc(s_lg, 1)
                if nxt:
                    group(c + 1, 2, pj_at(c, 2))
                n += 1
                pe.wait_ge(s_ex, c + 1)
                turn([prob[:, h, b * P:(b + 1) * P] for h in range(4) for b in range(2)], tp_at(c, n))
                if nxt:
                    group(c + 1, 3, pj_at(c, 3))
                pe.wait_ge(s_tpf, tp_at(c, n) + 1)
                if not static(c) or c:
                    pe.wait_ge(s_y, c)
                for h in range(4):
                    kv = h // 2
                    for b in range(2):
                        ins = nc.tensor.matmul(pv[:, h, :], pT[:, 2 * h + b, :], v_win[:, b, kv * HD:(kv + 1) * HD],
                                               start=(b == 0), stop=(b == 1))
                ins.then_inc(s_pv, 1)
                n += 1
                pe.wait_ge(s_ex2, c + 1)
                turn([prob[:, h, b * P:(b + 1) * P] for h in range(4) for b in range(2)], tp_at(c, n))
                if nxt:
                    group(c + 1, 4, pj_at(c, 4))
                pe.wait_ge(s_tpf, tp_at(c, n) + 1)
                pe.wait_ge(s_ya, c + 1)
                for i, h in enumerate(MEM_ORDER):
                    for b in range(2):
                        ins = nc.tensor.matmul(pv2[:, h, :], pT[:, 2 * i + b, :], mv[:, b, h * HD:(h + 1) * HD],
                                               start=(b == 0), stop=(b == 1))
                ins.then_inc(s_pv, 1)
                n += 1
                pe.wait_ge(s_y, c + 1)
                turn(tiles(pr, KT), tp_at(c, n))
                if nxt:
                    group(c + 1, 5, pj_at(c, 5))
                pe.wait_ge(s_tpf, tp_at(c, n) + 1)
                if static(c) and c == 0:
                    pe.wait_ge(s_wout, 16)
                for j in range(2):
                    at = pj_at(c, (6 if nxt else 0) + j)
                    pe.wait_ge(s_pjf, at - 1)
                    for k in range(KT):
                        ins = nc.tensor.matmul(pj[j], pT[:, k, :], w_out[:, k, j * 512:(j + 1) * 512],
                                               start=(k == 0), stop=(k == KT - 1))
                    ins.then_inc(s_pj, 1)

            run_chunks(pe, step)

        def a_scalar(act):
            def copy(dst, src, scale=1.0):
                return nc.scalar.activation(dst, src, ACT.Copy, scale=scale)

            def take_tiles(dst, at):
                act.wait_ge(s_tp, at + 1)
                copy(dst[:, 0:4, :], tp[:, 0:4, :])
                copy(dst[:, 4:8, :], tp[:, 4:8, :]).then_inc(s_tpf, 1)

            def take_gelu(c, par, g, at):
                o, n = GROUPS1[g]
                act.wait_ge(s_pj, at + 1)
                copy(proj[:, par, o:o + n], pj[g % 2][:, 0:n], 0.5)
                nc.scalar.activation(tmp[:, o:o + n], pj[g % 2][:, 0:n], ACT.Square).then_inc(s_pjf, 1)

            def take_qkv(c, par, at):
                pr = proj[:, par, :]
                act.wait_ge(s_pj, at + 1)
                q_in = pj[0][:, 0:4 * HD].rearrange("p (a b d) -> p b a d", a=2, b=2)
                q_out = pr[:, QOFF:QOFF + 4 * HD].rearrange("p (b a d) -> p b a d", b=2, a=2)
                copy(q_out, q_in, HD ** -0.5)
                copy(pr[:, KOFF:KOFF + 2 * P], pj[0][:, 4 * HD:4 * HD + 2 * P]).then_inc(s_pjf, 1)

            def take_z(par, o, n, ps):
                copy(proj[:, par, ZOFF + o:ZOFF + o + n], ps, 0.5)
                return nc.scalar.activation(tmp[:, o:o + n], ps, ACT.Tanh, scale=0.5)

            def take_mq_z(c, par, at):
                act.wait_ge(s_pj, at + 1)
                copy(proj[:, par, MQOFF:MQOFF + MEM], pj[1][:, 0:MEM], HD ** -0.5).then_inc(s_qk, 1)
                act.wait_ge(s_gel, c + 1)
                take_z(par, 0, 256, pj[1][:, MEM:2 * MEM]).then_inc(s_pjf, 1)

            def gelu_tanh(c):
                act.wait_ge(s_garg, c + 1)
                nc.scalar.activation(tmp, tmp, ACT.Tanh, scale=GELU_C).then_inc(s_gth, 1)

            act.wait_ge(s_tp, 1)
            copy(wsT, tp[:, 0:4, :]).then_inc(s_tpf, 1)
            act.wait_ge(s_extp, 1)
            copy(ext_rows, psum[:, 4:8, 0:EXT]).then_inc(s_exts, 1)
            for a in range(2):
                act.wait_ge(s_tp, 2 + a)
                copy(memT[:, 0:4, a * P:(a + 1) * P], tp[:, 0:4, :])
                copy(memT[:, 4:8, a * P:(a + 1) * P], tp[:, 4:8, :]).then_inc(s_tpf, 1)
            act.wait_ge(s_mkv, 1)
            copy(mkT, psum[:, 4, :].rearrange("p (a n) -> p a n", a=2)).then_inc(s_mkvt, 1)
            act.wait_ge(s_mkv, 2)
            copy(mv, psum[:, 5, :].rearrange("p (a n) -> p a n", a=2)).then_inc(s_mkvt, 1)
            take_tiles(xT, 3)
            take_gelu(0, 0, 0, 0)
            take_gelu(0, 0, 1, 1)
            gelu_tanh(0)
            take_qkv(0, 0, 2)
            take_mq_z(0, 0, 3)
            act.wait_ge(s_pj, 5)
            take_z(0, 256, 512, pj[0]).then_inc(s_pjf, 1)
            act.wait_ge(s_pj, 6)
            take_z(0, 768, 256, pj[1][:, 0:256]).then_inc(s_pjf, 1)

            def step(c, par):
                nxt = not static(c) or c + 1 < NC
                npar = 1 - par
                n = 0
                if nxt:
                    take_tiles(xT, tp_at(c, 0))
                    n = 1
                act.wait_ge(s_tp, tp_at(c, n) + 1)
                copy(qT, tp[:, 0:2, :])
                copy(kT[:, par, :], tp[:, 2, :])
                copy(v_win[:, par, :], proj[:, par, VOFF:VOFF + P])
                copy(mqT, tp[:, 3:5, :]).then_inc(s_tpf, 1)
                if nxt:
                    act.wait_ge(s_z, c + 1)
                    take_gelu(c + 1, npar, 0, pj_at(c, 0))
                    take_gelu(c + 1, npar, 1, pj_at(c, 1))
                act.wait_ge(s_nm, c + 1)
                for h in range(4):
                    nc.scalar.activation(prob[:, h, :], prob[:, h, :], ACT.Exp, bias=swa_nmax[:, h:h + 1],
                                         accum_out=swa_sum[:, h:h + 1])
                nc.scalar.activation(sink_exp, sink_arg, ACT.Exp).then_inc(s_ex, 1)
                if nxt:
                    gelu_tanh(c + 1)
                    take_qkv(c + 1, npar, pj_at(c, 2))
                n += 1
                take_tiles(pT, tp_at(c, n))
                act.wait_ge(s_nm2, c + 1)
                for h in range(4):
                    ins = nc.scalar.activation(prob[:, h, :], lg[:, h, :], ACT.Exp, bias=mem_nmax[:, h:h + 1],
                                               accum_out=mem_sum[:, h:h + 1])
                ins.then_inc(s_ex2, 1)
                if nxt:
                    take_mq_z(c + 1, npar, pj_at(c, 3))
                n += 1
                take_tiles(pT, tp_at(c, n))
                if nxt:
                    act.wait_ge(s_pj, pj_at(c, 4) + 1)
                    take_z(npar, 256, 512, pj[0]).then_inc(s_pjf, 1)
                n += 1
                take_tiles(pT, tp_at(c, n))
                if nxt:
                    act.wait_ge(s_pj, pj_at(c, 5) + 1)
                    take_z(npar, 768, 256, pj[1][:, 0:256]).then_inc(s_pjf, 1)
                if not static(c) or c:
                    act.wait_ge(s_x1st, c * 16)
                for j in range(2):
                    act.wait_ge(s_pj, pj_at(c, (6 if nxt else 0) + j) + 1)
                    copy(o_sb[:, j * 512:(j + 1) * 512], pj[j])
                    ins = nc.scalar.activation(junk[:, j * 512:(j + 1) * 512], pj[j], ACT.Square, accum_out=o_ss[:, j:j + 1])
                    ins.then_inc(s_pjf, 1)
                    

            run_chunks(act, step)

        def a_vector(dve, ch):
            def gelu_arg(c, par, done):
                dve.wait_ge(s_pjf, done)
                ch.link(nc.vector.tensor_scalar(tmp, tmp, 2 * GELU_A, 2.0, ALU.mult, ALU.add))
                ch.wait()
                nc.vector.tensor_tensor(tmp, tmp, proj[:, par, 0:D], ALU.mult).then_inc(s_garg, 1)

            def gelu_end(c, par):
                pr = proj[:, par, :]
                v = pr[:, A_W:2 * A_W]
                dve.wait_ge(s_gth, c + 1)
                nc.vector.scalar_tensor_tensor(pr[:, 0:D], tmp, 1.0, pr[:, 0:D], ALU.add, ALU.mult).then_inc(s_gel, 1)
                dve.wait_ge(s_gel, c + 1)
                for g in range(4):
                    ins = nc.vector.bn_stats(v_stats[:, g, :], v[:, g * P:(g + 1) * P])
                ch.link(ins)
                ch.wait()
                settled(dve)
                for g in range(4):
                    ins = nc.vector.bn_aggr(v_mv[:, g, :], v_stats[:, g, :])
                ch.link(ins)
                ch.wait()
                nc.vector.tensor_scalar(v_var, v_mv[:, :, 1], EPS, None, ALU.add).then_inc(s_vvar, 1)
                dve.wait_ge(s_vrs, c + 1)
                for g in range(4):
                    vg = v[:, g * P:(g + 1) * P]
                    ins = nc.vector.tensor_scalar(vg, vg, v_mv[:, g, 0:1], v_rstd[:, g:g + 1], ALU.subtract, ALU.mult)
                ch.link(ins)
                ch.wait()
                ch.link(nc.vector.tensor_tensor(v, v, vn_g, ALU.mult))
                ch.wait()
                nc.vector.tensor_tensor(v, v, vn_b, ALU.add).then_inc(s_vn, 1)

            def z_end(c, par, done):
                dve.wait_ge(s_pjf, done)
                z = proj[:, par, ZOFF:ZOFF + D]
                nc.vector.scalar_tensor_tensor(z, tmp, 1.0, z, ALU.add, ALU.mult).then_inc(s_z, 1)

            def norm_x(c, turned):
                dve.wait_ge(s_xin, c * 16 + 16)
                if turned is not None:
                    dve.wait_ge(s_tp, turned + 1)
                nc.vector.tensor_tensor_reduce(xn, x_in, x_in, 1.0 / D, EPS, ALU.mult, ALU.add, x_ms).then_inc(s_xms, 1)
                dve.wait_ge(s_xrs, c + 1)
                nc.vector.scalar_tensor_tensor(xn, x_in, x_rstd, g_pre, ALU.mult, ALU.mult).then_inc(s_xn, 1)

            nc.vector.memset(kT, 0.0)
            nc.vector.memset(v_win, 0.0).then_inc(s_pad, 1)
            dve.wait_ge(s_const, 16 * N_CONST)
            nc.vector.tensor_tensor(wsT, wsT, cst("causal").unsqueeze(1).to_broadcast([P, 4, P]), ALU.mult).then_inc(s_ws, 1)
            nc.vector.tensor_copy(tmp[0:SWA_BUCKETS, 0:4 * P].rearrange("p (h n) -> p h n", h=4),
                                  relb[0:SWA_BUCKETS, :].unsqueeze(2).to_broadcast([SWA_BUCKETS, 4, P])).then_inc(s_rel, 1)
            for a in range(2):
                nc.vector.tensor_tensor_reduce(proj[:, 1, a * D:(a + 1) * D], mem_rows[:, a, :], mem_rows[:, a, :], 1.0 / D, EPS, ALU.mult, ALU.add,
                                               o_ss[:, a:a + 1]).then_inc(s_memms, 1)
            for a in range(2):
                dve.wait_ge(s_memr, a + 1)
                nc.vector.scalar_tensor_tensor(mem_rows[:, a, :], mem_rows[:, a, :], mem_max[:, a:a + 1], mem_g,
                                               ALU.mult, ALU.mult).then_inc(s_memn, 1)
            norm_x(0, None)
            dve.wait_ge(s_ext_ld, 16)
            ch.link(nc.vector.tensor_tensor(bias, bias, cst("window").unsqueeze(1).to_broadcast([P, 4, 2 * P]), ALU.add))
            norm_x(1, 3)
            gelu_arg(0, 0, 2)
            gelu_end(0, 0)
            z_end(0, 0, 6)

            def step(c, par):
                nxt = not static(c) or c + 1 < NC
                npar = 1 - par
                pr = proj[:, par, :]
                z = pr[:, ZOFF:ZOFF + D]
                dve.wait_ge(s_sgu, c + 1)
                dve.wait_ge(s_z, c + 1)
                for g in range(4):
                    u = pr[:, g * P:(g + 1) * P]
                    ins = nc.vector.scalar_tensor_tensor(u, sgu[:, g, :], bsT[:, g:g + 1], u, ALU.add, ALU.mult)
                ins.then_inc(s_ya, 1)
                if not static(c) or c + 2 < NC:
                    norm_x(c + 2, tp_at(c, 0))
                dve.wait_ge(s_lg, c * 2 + 1)
                ch.wait()
                for b in (1 - par, par):
                    cols = slice(b * P, (b + 1) * P)
                    side = slice(P, 2 * P) if b == par else slice(0, P)
                    if static(c) and c == 0 and b != par:
                        ins = nc.vector.memset(prob[:, :, cols], NEG)
                    else:
                        ins = nc.vector.tensor_tensor(prob[:, :, cols], lg[:, :, cols], bias[:, :, side], ALU.add)
                ins.then_inc(s_lgf, 1)
                dve.wait_ge(s_lgf, c + 1)
                ch.link(nc.vector.tensor_reduce(swa_max, prob, AX, ALU.max))
                ch.wait()
                ch.link(nc.vector.tensor_tensor(swa_max, swa_max, sink, ALU.max))
                ch.wait()
                nc.vector.tensor_tensor(sink_arg, sink, swa_max, ALU.subtract)
                nc.vector.tensor_scalar(swa_nmax, swa_max, -1.0, None, ALU.mult).then_inc(s_nm, 1)
                if nxt:
                    gelu_arg(c + 1, npar, pj_at(c, 2))
                dve.wait_ge(s_lg, c * 2 + 2)
                ch.link(nc.vector.tensor_reduce(mem_max, lg, AX, ALU.max))
                ch.wait()
                nc.vector.tensor_scalar(mem_nmax, mem_max, -1.0, None, ALU.mult).then_inc(s_nm2, 1)
                dve.wait_ge(s_ex, c + 1)
                ch.link(nc.vector.tensor_tensor(swa_sum, swa_sum, sink_exp, ALU.add))
                ch.wait()
                ch.link(nc.vector.reciprocal(swa_rden, swa_sum))
                if nxt:
                    gelu_end(c + 1, npar)
                dve.wait_ge(s_ya, c + 1)
                nc.vector.tensor_tensor(pr[:, 0:A_W], pr[:, 0:A_W], z[:, 0:A_W], ALU.mult)
                dve.wait_ge(s_pv, c * 2 + 1)
                ch.wait()
                for h in range(4):
                    o = A_W + h * HD
                    nc.vector.scalar_tensor_tensor(pr[:, o:o + HD], pv[:, h, :], swa_rden[:, h:h + 1], z[:, o:o + HD],
                                                   ALU.mult, ALU.mult)
                dve.wait_ge(s_ex2, c + 1)
                ch.link(nc.vector.reciprocal(mem_rden, mem_sum))
                ch.wait()
                dve.wait_ge(s_pv, c * 2 + 2)
                for i, h in enumerate(MEM_ORDER):
                    o = A_W + 4 * HD + h * HD
                    ins = nc.vector.scalar_tensor_tensor(pr[:, o:o + HD], pv2[:, h, :], mem_rden[:, i:i + 1], z[:, o:o + HD],
                                                         ALU.mult, ALU.mult)
                ins.then_inc(s_y, 1)
                if nxt:
                    z_end(c + 1, npar, pj_at(c, 6))
                if not nxt:
                    for g in range(B_GROUPS - 1):
                        b_largest_of(dve, g)
                dve.wait_ge(s_pjf, pj_at(c, 8 if nxt else 2))
                ch.link(nc.vector.tensor_tensor(o_ms, o_ss[:, 0:1], o_ss[:, 1:2], ALU.add))
                ch.wait()
                nc.vector.tensor_scalar(o_ms, o_ms, 1.0 / D, EPS, ALU.mult, ALU.add).then_inc(s_oms, 1)
                dve.wait_ge(s_ors, c + 1)
                ch.link(nc.vector.scalar_tensor_tensor(o_sb, o_sb, o_rstd, g_post, ALU.mult, ALU.mult))
                ch.wait()
                dve.wait_ge(s_xres, c * 16 + 16)
                nc.vector.tensor_tensor(o_sb, o_sb, x_res, ALU.add).then_inc(s_x1, 1)

            run_chunks(dve, step, ch)
            return ch

        def a_gpsimd(pool):
            def rsqrt(dst, src, n):
                return nc.gpsimd.tensor_tensor(dst, src, neg_half[:, 0:n], ALU.pow)

            nc.gpsimd.memset(neg_half, -0.5).then_inc(s_half, 1)
            pool.wait_ge(s_half, 1)
            for a in range(2):
                pool.wait_ge(s_memms, a + 1)
                rsqrt(mem_max[:, a:a + 1], o_ss[:, a:a + 1], 1).then_inc(s_memr, 1)

            def x_rsqrt(c):
                pool.wait_ge(s_xms, c + 1)
                rsqrt(x_rstd, x_ms, 1).then_inc(s_xrs, 1)

            def v_rsqrt(c):
                pool.wait_ge(s_vvar, c + 1)
                rsqrt(v_rstd, v_var, 4).then_inc(s_vrs, 1)

            x_rsqrt(0)
            x_rsqrt(1)
            v_rsqrt(0)

            def step(c, par):
                if not static(c) or c + 2 < NC:
                    x_rsqrt(c + 2)
                if not static(c) or c + 1 < NC:
                    v_rsqrt(c + 1)
                pool.wait_ge(s_oms, c + 1)
                rsqrt(o_rstd, o_ms, 1).then_inc(s_ors, 1)

            run_chunks(pool, step)

        x2_d = out if stop_after == "b" else dram("x2_scratch", [S, D])
        m = Arena(arena[:, :], SB)
        m.at = shared_end
        W2 = m.take(KT * (IN1 + D))
        SLOT = KT * M_W
        w_raw = [W2[:, SLOT // 2 + g * SLOT:SLOT // 2 + (g + 1) * SLOT].rearrange("p (k n) -> p k n", k=KT) for g in range(B_GROUPS)]
        w_hi, w_lo = zip(*[halves(W2[:, g * SLOT:(g + 1) * SLOT], KT) for g in range(B_GROUPS)])
        w_mix = W2[:, KT * IN1:].rearrange("p (k n) -> p k n", k=KT)
        gate_rows = Arena(W2[:, B_GROUPS * SLOT:KT * IN1], SLOT // 2)
        b_xin = m.take(D)
        b_xres = m.take(D)
        tab2 = m.take(CONST2_W)
        conv_w = m.take(KT, CONV)
        gate_b = m.take(8)
        pool_w = m.take(4, P)
        head_g = m.take(M_W)
        pool_sc = m.take(M_W)
        gate_raw = m.take(KT, 8)
        b_abs = m.take(6)
        assert m.at <= free_end_a
        gate_hi, gate_lo = halves(m.take(KT * 8), KT)
        x_hi, x_lo = halves(m.take(D), KT)
        qk_win = m.take(KT, P + CONV - 1)
        qk = m.take(2, KT, P)
        b_tmp = m.take(KT, P)
        b_yT = b_tmp
        v_ext = m.take(2, LH, LD + 1)
        o_th = m.take(2, M_W)
        u_win = m.take(2, M_W)
        pk = m.take(KT, P)
        pooledT, k_tok = pk[:, 0:4, :], pk[:, 4:8, :]
        decay = m.take(LH, P)
        wv = m.take(LH, LD + 1)
        state = m.take(LH, LD + 1)
        hn = m.take(LH, LD + 1)
        b_y = m.take(D)
        b_o = m.take(D)
        mix_g, mix_b = m.take(D), m.take(D)
        gates = m.take(8)
        a_col = m.take(2, LH)
        e_col = m.take(2, 4 * LH)
        q_inter = m.take(LH)
        den, rden = m.take(LH), m.take(LH)
        h_mv, h_var, h_rstd = m.take(LH, 2), m.take(LH), m.take(LH)
        r_mv, r_var, r_rstd = m.take(2), m.take(1), m.take(1)
        ones = m.take(P)
        b_diag = m.take(P)
        b_rows = m.take(P)
        b_all = m.take(6)
        w_pow, w_inv = m.take(6), m.take(6)
        b_pow, b_inv, b_back = m.take(1), m.take(1), m.take(1)
        b_scale = m.take(2, 4)
        m_diag = m.take(LH, P)
        g_if = gate_rows.take(2, P)
        g_abs, g_e, g_den, g_rec, g_s, g_s2, g_ser = [gate_rows.take(P) for _ in range(7)]
        g_b, g_m = gate_rows.take(P), gate_rows.take(P)
        g_out = gate_rows.take(4, P)
        g_dec = gate_rows.take(LH)
        m_state = gate_rows.take(1)
        h_stats, r_stats = gate_rows.take(LH, 6), gate_rows.take(2, 6)

        def cst2(name):
            o, w = CONST2[name]
            return tab2[:, o:o + w]

        pool_first = cst2("pool_first").rearrange("p (g n) -> p g n", g=4)

        b_dt = psum[:, 4, :].rearrange("p (a n) -> p a n", a=4)
        b_small = psum[:, 4, :]
        b_st = psum[:, 5, :].rearrange("p (a n) -> p a n", a=4)
        b_ext = psum[:, 6:8, :]
        tok_rows = psum[:, 6, 3 * P:4 * P]
        b_largest = psum[:, 7, 3 * P:3 * P + 6]

        def ext(h):
            return b_ext[:, h // 2, (h % 2) * (LD + 1):(h % 2 + 1) * (LD + 1)]

        n_const, n_wout = sem("b_const_loaded"), sem("b_w_mix_loaded")
        n_win = s_win
        n_xin, n_xres, n_x2st = sem("b_x_in_loaded"), sem("b_x_res_loaded"), sem("b_x2_stored")
        n_head = sem("b_tables_scaled")
        n_tp, n_tpf, n_pj, n_pjf = sem("b_turned"), sem("b_turned_taken"), sem("b_proj_done"), sem("b_proj_taken")
        n_hist, n_conv, n_cth, n_qk = (sem("b_window_shifted"), sem("b_conv_done"),
                                                 sem("b_conv_tanh"), sem("b_qk_ready"))
        n_dg, n_hi = sem("b_token_scale_ready"), sem("b_upper_half_ready")
        n_gp, n_gb, n_gt, n_gabs, n_ge, n_rows = (sem("b_gates_product"), sem("b_gates_biased"), sem("b_gates_turned"),
                                                  sem("b_gates_abs"), sem("b_gates_exp"), sem("b_gate_rows_ready"))
        n_cols, n_colt = sem("b_gate_columns_done"), sem("b_gate_columns_taken")
        n_dt, n_darg, n_dexp, n_st, n_p = (sem("b_decay_product"), sem("b_decay_arg"), sem("b_decay_exp"),
                                           sem("b_scores_done"), sem("b_weights_ready"))
        n_qi, n_qc, n_qct = sem("b_inter_scaled"), sem("b_state_product"), sem("b_state_product_taken")
        n_upd, n_state = sem("b_update_product"), sem("b_state_ready")
        n_num, n_numt = sem("b_values_done"), sem("b_values_taken")
        n_hvar, n_hrs, n_y = sem("b_head_var"), sem("b_head_rstd"), sem("b_y_ready")
        n_rvar, n_rrs, n_x2 = sem("b_row_var"), sem("b_row_rstd"), sem("b_x2_ready")

        N_CONST2 = 6 + CONV

        def tp2_at(c, n):
            return c * 3 + (2 + n) - (1 if static(c) and c == NC - 1 else 0)

        def pj2_at(c, n):
            return c * 8 + (5 + n)

        GROUPS2 = [0, M_W, 2 * M_W, 3 * M_W, POOL]
        SCALE_OF = [0, 1, 3, 4, 5]

        def b_sync(sp):
            w_rows = t["w_in_2"].rearrange("(k p) n -> p k n", p=P)
            sp.wait_ge(s_x1st, 16 * (NC - 1))
            sp.wait_ge(s_xn, NC)
            sp.dma_start(b_xin, rows(x1_d, 0)).then_inc(n_xin, 16)
            sp.wait_ge(s_pj, pj_at(NC - 2, 6))
            for g, o in enumerate(GROUPS2):
                sp.dma_start(w_raw[g], w_rows[:, :, o:o + M_W]).then_inc(n_win[g], 16)
                if g == 1:
                    sp.dma_start(gate_raw, w_rows[:, :, GATE:POOL]).then_inc(n_win[5], 16)
                    sp.dma_start(tab2, t["tables2"]).then_inc(n_const, 16)
                    for dst, name in ((gate_b[:, 0:4], "b_i_2"), (gate_b[:, 4:8], "b_f_2"), (head_g, "head_norm_g_2"),
                                      (pool_sc, "pool_scale_2")):
                        sp.dma_start(dst, t[name].partition_broadcast(P)).then_inc(n_const, 16)
                    with nc.allow_non_contiguous_dma(reason="4096 values once"):
                        for j in range(CONV):
                            sp.dma_start(conv_w[:, :, j], t["conv_qk_2"][j].rearrange("(k p) -> p k", p=P)).then_inc(n_const, 16)
                    sp.dma_start(pool_w, t["pool_w_2"].rearrange("g c d -> c g d")).then_inc(n_const, 16)

        def b_sync_main(sp, before_last):
            sp.dma_start(w_mix, t["w_mix_out_2"].rearrange("(k p) n -> p k n", p=P)).then_inc(n_wout, 16)
            for dst, name in ((mix_g, "ln_mix_g_2"), (mix_b, "ln_mix_b_2")):
                sp.dma_start(dst, t[name].partition_broadcast(P)).then_inc(n_wout, 16)
            sp.dma_start(b_xres, rows(x1_d, 0)).then_inc(n_xres, 16)
            for c in (1, 2):
                sp.wait_ge(n_tp, c)
                sp.dma_start(b_xin, rows(x1_d, c)).then_inc(n_xin, 16)

            def step(c, par):
                if not static(c) or c + 3 < NC:
                    sp.wait_ge(n_tp, tp2_at(c, 2) + 1)
                    sp.dma_start(b_xin, rows(x1_d, c + 3)).then_inc(n_xin, 16)
                sp.wait_ge(n_x2, c + 1)
                sp.dma_start(rows(x2_d, c), b_o).then_inc(n_x2st, 16)
                if not static(c) or c + 1 < NC:
                    sp.dma_start(b_xres, rows(x1_d, c + 1)).then_inc(n_xres, 16)

            run_chunks(sp, step, before_last=before_last)

        def b_sync_end(sp):
            sp.wait_ge(n_x2st, 16 * NC)

        def b_tensor(pe):
            def tiles(ap, n):
                return [ap[:, k * P:(k + 1) * P] for k in range(n)]

            def free_tp(at):
                if not static(at) or at:
                    pe.wait_ge(n_tpf, at)

            def turn(src, at):
                free_tp(at)
                for i, tile in enumerate(src):
                    ins = nc.tensor.transpose(tp[:, i, :], tile, ident)
                ins.then_inc(n_tp, 1)

            def front(c, at):
                pe.wait_ge(n_dg, c + 1)
                free_tp(at)
                nc.tensor.matmul(tok_rows, ones, b_rows, start=True, stop=True)
                for i, tile in enumerate(tiles(b_xin, KT)):
                    ins = nc.tensor.matmul(tp[:, i, :], tile, b_diag, start=True, stop=True)
                ins.then_inc(n_tp, 1)

            def spread():
                pe.wait_ge(h_gm, 1)
                nc.tensor.matmul(b_largest, ones[0:1, :], b_all[0:1, :], start=True, stop=True).then_inc(h_bc, 1)

            def free_pj(at):
                if not static(at) or at >= 2:
                    pe.wait_ge(n_pjf, at - 1)

            def all_taken(at):
                if not static(at) or at:
                    pe.wait_ge(n_pjf, at)

            def group_turned(g, at, first):
                if g == 0:
                    all_taken(at)
                else:
                    free_pj(at)
                if first:
                    pe.wait_ge(h_wl, (g + 1) * KT)
                for i in range(4):
                    cols = slice(i * P, (i + 1) * P)
                    for k in range(KT):
                        for n, (w, x) in enumerate(((w_hi[g], x_hi), (w_hi[g], x_lo), (w_lo[g], x_hi))):
                            ins = nc.tensor.matmul(pj[g][:, cols], w[:, k, cols], x[:, k, :],
                                                   start=(k == 0 and n == 0), stop=(k == KT - 1 and n == 2))
                ins.then_inc(n_pj, 1)

            def by_token(dst, hi, lo, of):
                for k in of:
                    for n, (x, w) in enumerate(((x_hi, hi), (x_hi, lo), (x_lo, hi))):
                        ins = nc.tensor.matmul(dst, x[:, k, :], w[:, k, :], start=(k == 0 and n == 0), stop=(k == KT - 1 and n == 2))
                return ins

            def group(g, at, bank, first, of=range(KT)):
                if of[0] == 0:
                    free_pj(at)
                if first:
                    pe.wait_ge(h_wl, (g + 1) * KT)
                ins = by_token(pj[bank], w_hi[g], w_lo[g], of)
                if of[-1] == KT - 1:
                    ins.then_inc(n_pj, 1)

            def gate_product(c):
                if not static(c) or c:
                    pe.wait_ge(n_darg, c)
                by_token(b_small[:, 0:8], gate_hi, gate_lo, range(KT)).then_inc(n_gp, 1)

            def gate_turn(c):
                pe.wait_ge(n_gb, c + 1)
                nc.tensor.transpose(b_small[0:LH, P:2 * P], gates[:, 0:4], ident)
                nc.tensor.transpose(b_small[0:LH, 2 * P:3 * P], gates[:, 4:8], ident).then_inc(n_gt, 1)

            def gate_columns(c):
                pe.wait_ge(n_rows, c + 1)
                settled(pe)
                for i in range(4):
                    nc.tensor.transpose(b_small[:, 400 + 4 * i:404 + 4 * i], g_out[0:LH, i, :], ident[0:LH, 0:LH])
                nc.tensor.matmul(b_small[:, 416:420], ones[0:LH, :], g_dec[0:LH, :], start=True, stop=True).then_inc(n_cols, 1)

            front(0, 0)
            spread()
            pe.wait_ge(n_tpf, 1)
            pe.wait_ge(s_pjf, pj_at(NC - 1, 2))
            group_turned(0, 0, True)
            group_turned(1, 1, True)
            gate_product(0)
            all_taken(2)
            group(2, 2, 0, True)
            gate_turn(0)
            group(3, 3, 1, True)
            group(4, 4, 0, True)
            front(1, 1)
            gate_columns(0)

            def step(c, par):
                nxt = not static(c) or c + 1 < NC
                qT2, kT2 = qk[:, par, 0:4, :], qk[:, par, 4:8, :]
                pe.wait_ge(n_colt, c + 1)
                nc.tensor.matmul(psum[:, 4, :], ones[0:LH, :], m_diag[0:LH].rearrange("p a n -> p (a n)"),
                                 start=True, stop=True).then_inc(n_dt, 1)
                pe.wait_ge(n_qk, c + 1)
                if not static(c) or c:
                    pe.wait_ge(n_p, c)
                for h in range(LH):
                    ins = nc.tensor.matmul(b_st[:, h, :], kT2[:, h, :], qT2[:, h, :], start=True, stop=True)
                ins.then_inc(n_st, 1)
                if not static(c) or c:
                    pe.wait_ge(n_state, c)
                    pe.wait_ge(n_numt, c)
                if nxt:
                    pe.wait_ge(n_tpf, tp2_at(c, 0))
                for h in range(LH):
                    ins = nc.tensor.matmul(ext(h), qT2[:, h, :], state[:, h, :], start=True, stop=True)
                ins.then_inc(n_qc, 1)
                free_tp(tp2_at(c, 0))
                first = static(c) and c == 0
                if first:
                    pe.wait_ge(n_pjf, 5)
                    pe.wait_ge(n_const, 16 * N_CONST2)
                for g in range(4):
                    cur = pool_first[:, g, :] if first else cst2("pool_cur")[:, g * P:(g + 1) * P]
                    nc.tensor.matmul(tp[:, g, :], u_win[:, par, g * P:(g + 1) * P], cur, start=True, stop=first)
                    if not first:
                        nc.tensor.matmul(tp[:, g, :], u_win[:, 1 - par, g * P:(g + 1) * P],
                                         cst2("pool_prev")[:, g * P:(g + 1) * P], start=False, stop=True)
                for h in range(LH):
                    ins = nc.tensor.transpose(tp[:, 4 + h, :], kT2[:, h, :], ident)
                ins.then_inc(n_tp, 1)
                if nxt:
                    group_turned(0, pj2_at(c, 0), False)
                    group_turned(1, pj2_at(c, 1), False)
                    gate_product(c + 1)
                pe.wait_ge(n_tpf, tp2_at(c, 0) + 1)
                at = pj2_at(c, 2 if nxt else 0)
                all_taken(at)
                for g in range(4):
                    ins = nc.tensor.matmul(pj[0][:, g * P:(g + 1) * P], pooledT[:, g, :], pool_w[:, g, :], start=True, stop=True)
                ins.then_inc(n_pj, 1)
                pe.wait_ge(n_qct, c + 1)
                for h in range(LH):
                    ins = nc.tensor.matmul(ext(h), k_tok[:, h, :], wv[:, h, :], start=True, stop=True)
                ins.then_inc(n_upd, 1)
                if nxt:
                    group(2, pj2_at(c, 3), 1, False)
                    gate_turn(c + 1)
                pe.wait_ge(n_p, c + 1)
                pe.wait_ge(n_state, c + 1)
                for h in range(LH):
                    ins = nc.tensor.matmul(ext(h), decay[:, h, :], v_ext[:, par, h, :], start=True, stop=True)
                ins.then_inc(n_num, 1)
                if nxt:
                    group(3, pj2_at(c, 4), 0, False)
                    group(4, pj2_at(c, 5), 1, False, range(0, KT - 3))
                pe.wait_ge(n_y, c + 1)
                turn(tiles(b_y, KT), tp2_at(c, 1))
                if nxt:
                    group(4, pj2_at(c, 5), 1, False, range(KT - 3, KT))
                pe.wait_ge(n_tpf, tp2_at(c, 1) + 1)
                if first:
                    pe.wait_ge(n_wout, 48)
                for j in range(2):
                    at = pj2_at(c, (6 if nxt else 1) + j)
                    free_pj(at)
                    bank = j if nxt else 1 - j
                    if j == 1 and (not static(c) or c + 2 < NC):
                        front(c + 2, tp2_at(c, 2))
                    if nxt and j == 1:
                        gate_columns(c + 1)
                    for k in range(KT):
                        ins = nc.tensor.matmul(pj[bank], b_yT[:, k, :], w_mix[:, k, j * 512:(j + 1) * 512],
                                               start=(k == 0), stop=(k == KT - 1))
                    ins.then_inc(n_pj, 1)

            run_chunks(pe, step)

        def b_scalar(act):
            def copy(dst, src, scale=1.0):
                return nc.scalar.activation(dst, src, ACT.Copy, scale=scale)

            def take_tiles(dst, at):
                act.wait_ge(n_tp, at + 1)
                copy(dst[:, 0:4, :], tp[:, 0:4, :])
                copy(dst[:, 4:8, :], tp[:, 4:8, :]).then_inc(n_tpf, 1)

            def take_upper(at):
                act.wait_ge(n_tp, at + 1)
                copy(x_hi[:, 0:4, :], tp[:, 0:4, :])
                copy(x_hi[:, 4:8, :], tp[:, 4:8, :]).then_inc(n_hi, 1)

            def upper_weights(g):
                if g == 0:
                    act.wait_ge(h_sc, 1)
                if g == 1:
                    copy(gate_hi, gate_raw, w_inv[:, 2:3])
                inv = w_inv[:, SCALE_OF[g]:SCALE_OF[g] + 1]
                for k in range(KT):
                    if g and k % 2 == 0:
                        act.wait_ge(h_wl, (g - 1) * KT + KT // 2 + k // 2 + 1)
                    copy(w_hi[g][:, k, :], w_raw[g][:, k, :], inv).then_inc(h_wh, 1)

            def conv_tanh(c):
                act.wait_ge(n_conv, c + 1)
                nc.scalar.activation(b_tmp, qk[:, c % 2 if static(c) else conv_par[0]], ACT.Tanh).then_inc(n_cth, 1)

            def take_v(par, at, bank):
                act.wait_ge(n_pj, at + 1)
                copy(v_ext[:, par, :, 0:LD], pj[bank].rearrange("p (a n) -> p a n", a=4), b_scale[:, par, 1:2]).then_inc(n_pjf, 1)

            def take_o(par, at, bank):
                act.wait_ge(n_pj, at + 1)
                nc.scalar.activation(o_th[:, par, :], pj[bank], ACT.Tanh, scale=b_scale[:, par, 2:3]).then_inc(n_pjf, 1)

            def take_u(par, at, bank):
                act.wait_ge(n_pj, at + 1)
                copy(u_win[:, par, :], pj[bank], b_scale[:, par, 3:4]).then_inc(n_pjf, 1)

            def gate_exp(c):
                act.wait_ge(n_gabs, c + 1)
                nc.scalar.activation(g_e[0:LH], g_abs[0:LH], ACT.Exp).then_inc(n_ge, 1)

            def take_columns(c, par):
                act.wait_ge(n_cols, c + 1)
                copy(a_col[:, par, :], b_small[:, 400:404])
                nc.scalar.activation(e_col[:, par, :], b_small[:, 404:420], ACT.Exp).then_inc(n_colt, 1)

            conv_par = [0]
            take_upper(0)
            for g in range(4):
                upper_weights(g)
            take_v(0, 2, 0)
            upper_weights(4)
            take_o(0, 3, 1)
            gate_exp(0)
            take_u(0, 4, 0)
            conv_tanh(0)
            take_upper(1)
            take_columns(0, 0)

            def step(c, par):
                nxt = not static(c) or c + 1 < NC
                npar = 1 - par
                conv_par[0] = npar
                act.wait_ge(n_colt, c + 1)
                for h in range(LH):
                    copy(wv[:, h, :], v_ext[:, par, h, :], e_col[:, par, 8 + h:9 + h])
                act.wait_ge(n_qi, c + 1)
                act.wait_ge(n_qc, c + 1)
                for h in range(LH):
                    ins = copy(hn[:, h, :], ext(h), q_inter[:, h:h + 1])
                ins.then_inc(n_qct, 1)
                take_tiles(pk, tp2_at(c, 0))
                act.wait_ge(n_darg, c + 1)
                nc.scalar.activation(decay, decay, ACT.Exp).then_inc(n_dexp, 1)
                act.wait_ge(n_pj, pj2_at(c, 2 if nxt else 0) + 1)
                copy(b_y[:, M_W:D], pj[0]).then_inc(n_pjf, 1)
                if nxt:
                    conv_tanh(c + 1)
                    take_v(npar, pj2_at(c, 3), 1)
                    gate_exp(c + 1)
                    take_o(npar, pj2_at(c, 4), 0)
                take_tiles(b_yT, tp2_at(c, 1))
                if nxt:
                    take_u(npar, pj2_at(c, 5), 1)
                if not static(c) or c:
                    act.wait_ge(n_x2st, c * 16)
                for j in range(2):
                    if j == 1 and (not static(c) or c + 2 < NC):
                        take_upper(tp2_at(c, 2))
                    if nxt and j == 1:
                        take_columns(c + 1, npar)
                    act.wait_ge(n_pj, pj2_at(c, (6 if nxt else 1) + j) + 1)
                    copy(b_o[:, j * 512:(j + 1) * 512], pj[j if nxt else 1 - j]).then_inc(n_pjf, 1)

            run_chunks(act, step)

        def b_largest_of(dve, g):
            dve.wait_ge(n_win[g], 32)
            nc.vector.tensor_reduce(b_abs[:, SCALE_OF[g]:SCALE_OF[g] + 1], w_raw[g], mybir.AxisListType.XY, ALU.max,
                                    apply_absolute_value=True)
            if g == B_GROUPS - 1:
                dve.wait_ge(n_win[5], 32)
                nc.vector.tensor_reduce(b_abs[:, 2:3], gate_raw, mybir.AxisListType.XY, ALU.max, apply_absolute_value=True).then_inc(h_am, 1)

        def b_vector(dve, ch):
            def seq(ins):
                ch.link(ins)
                ch.wait()

            def token_scale(c, par):
                dve.wait_ge(n_xin, c * 16 + 16)
                seq(nc.vector.tensor_reduce(b_pow, b_xin, AX, ALU.max, apply_absolute_value=True))
                seq(power(seq, b_pow, b_inv, b_pow))
                seq(nc.vector.tensor_scalar(b_back, b_pow, HALF_TOP ** -2, None, ALU.mult))
                if not static(c) or c:
                    nc.vector.tensor_scalar(b_scale[:, par, :], w_pow[:, 2:6], b_back, None, ALU.mult)
                nc.vector.tensor_scalar(b_rows, ident, b_back, None, ALU.mult)
                nc.vector.tensor_scalar(b_diag, ident, b_inv, None, ALU.mult).then_inc(n_dg, 1)

            def take_lower(c):
                dve.wait_ge(n_hi, c + 1)
                nc.vector.tensor_copy(b_rows, tok_rows)
                for i in range(0, KT, 4):
                    ins = nc.vector.tensor_tensor(x_lo[:, i:i + 4, :], tp[:, i:i + 4, :], x_hi[:, i:i + 4, :], ALU.subtract)
                ins.then_inc(n_tpf, 1)

            def weight_scales():
                b_largest_of(dve, B_GROUPS - 1)
                dve.wait_ge(h_bc, 1)
                seq(power(seq, w_pow, w_inv, b_largest))
                seq(nc.vector.tensor_scalar(w_pow[:, 4:5], w_pow[:, 4:5], 0.5, None, ALU.mult))
                for g in range(2):
                    taps = conv_w[:, 4 * g:4 * g + 4, :]
                    nc.vector.tensor_scalar(taps, taps, w_pow[:, g:g + 1], 0.5, ALU.mult, ALU.mult)
                nc.vector.tensor_scalar(b_scale[:, 0, :], w_pow[:, 2:6], b_back, None, ALU.mult).then_inc(h_sc, 1)

            def lower_weights(g):
                for k in range(KT):
                    dve.wait_ge(h_wh, g * KT + k + 1)
                    if k:
                        dve.wait_ge(h_wl, g * KT + k // 2 + 1)
                    if g == 1 and k == 0:
                        nc.vector.scalar_tensor_tensor(gate_lo, gate_raw, w_inv[:, 2:3], gate_hi, ALU.mult, ALU.subtract)
                    nc.vector.scalar_tensor_tensor(w_lo[g][:, k, :], w_raw[g][:, k, :], w_inv[:, SCALE_OF[g]:SCALE_OF[g] + 1],
                                                   w_hi[g][:, k, :], ALU.mult, ALU.subtract).then_inc(h_wl, 1)

            def take_qk(c, g, at):
                dve.wait_ge(n_pj, at + 1)
                if g == 0:
                    dve.wait_ge(n_hist, c + 1)
                nc.vector.tensor_tensor(qk_win[:, 4 * g:4 * g + 4, CONV - 1:], pj[g].rearrange("p (a n) -> p a n", a=4),
                                        b_rows.unsqueeze(1).to_broadcast([P, 4, P]), ALU.mult).then_inc(n_pjf, 1)

            def shift(c):
                if static(c) and c == 0:
                    nc.vector.memset(qk_win[:, :, 0:CONV - 1], 0.0).then_inc(n_hist, 1)
                else:
                    nc.vector.tensor_copy(qk_win[:, :, 0:CONV - 1], qk_win[:, :, P:P + CONV - 1]).then_inc(n_hist, 1)

            def conv(c, par, half, taps):
                for j in taps:
                    for i in range(4 * half, 4 * half + 4):
                        dst, src = qk[:, par, i, :], qk_win[:, i, j:j + P]
                        if j == 0:
                            ins = nc.vector.tensor_scalar(dst, src, conv_w[:, i, j:j + 1], None, ALU.mult)
                        else:
                            ins = nc.vector.scalar_tensor_tensor(dst, src, conv_w[:, i, j:j + 1], dst, ALU.mult, ALU.add)
                    if half and j == CONV - 1:
                        ins.then_inc(n_conv, 1)
                    else:
                        seq(ins)

            def silu(c, par):
                dve.wait_ge(n_cth, c + 1)
                nc.vector.scalar_tensor_tensor(qk[:, par], b_tmp, 1.0, qk[:, par], ALU.add, ALU.mult).then_inc(n_qk, 1)

            def gate_bias(c, par):
                dve.wait_ge(n_gp, c + 1)
                nc.vector.scalar_tensor_tensor(gates, b_small[:, 0:8], b_scale[:, par, 0:1], gate_b, ALU.mult, ALU.add).then_inc(n_gb, 1)

            def gate_abs(c):
                dve.wait_ge(n_gt, c + 1)
                seq(nc.vector.tensor_copy(g_if[0:LH], b_small[0:LH, P:3 * P].rearrange("p (a n) -> p a n", a=2)))
                f = g_if[0:LH, 1, :]
                nc.vector.scalar_tensor_tensor(g_abs[0:LH], f, -1.0, f, ALU.mult, ALU.min).then_inc(n_gabs, 1)

            def gate_math(c):
                ig, f = g_if[0:LH, 0, :], g_if[0:LH, 1, :]
                e, dn, rc, s, s2, q = (x[0:LH] for x in (g_e, g_den, g_rec, g_s, g_s2, g_ser))
                b, mx, o = g_b[0:LH], g_m[0:LH], g_out[0:LH]
                dve.wait_ge(n_ge, c + 1)
                seq(nc.vector.tensor_scalar(dn, e, 2.0, None, ALU.add))
                seq(nc.vector.reciprocal(rc, dn))
                seq(nc.vector.tensor_tensor(s, e, rc, ALU.mult))
                seq(nc.vector.tensor_tensor(s2, s, s, ALU.mult))
                seq(nc.vector.tensor_scalar(q, s2, LN_TERMS[0], None, ALU.mult))
                for term in LN_TERMS[1:]:
                    seq(nc.vector.scalar_tensor_tensor(q, q, term, s2, ALU.add, ALU.mult))
                seq(nc.vector.scalar_tensor_tensor(q, q, 1.0, s, ALU.add, ALU.mult))
                seq(nc.vector.tensor_scalar(q, q, 2.0, None, ALU.mult))
                seq(nc.vector.scalar_tensor_tensor(s, f, 0.0, q, ALU.min, ALU.subtract))
                seq(nc.vector.tensor_tensor_scan(b, ones[0:LH, :], s, 0.0, ALU.mult, ALU.add))
                seq(nc.vector.tensor_tensor(o[:, 0, :], ig, b, ALU.subtract))
                seq(nc.vector.tensor_tensor_scan(mx, o[:, 0, :], o[:, 0, :], m_state[0:LH, :], ALU.max, ALU.max))
                nc.vector.tensor_scalar(o[:, 1, :], mx, -1.0, m_state[0:LH, :], ALU.mult, ALU.add)
                nc.vector.scalar_tensor_tensor(o[:, 2, :], b, -1.0, mx, ALU.mult, ALU.subtract)
                nc.vector.tensor_scalar(o[:, 3, :], o[:, 0, :], mx[:, P - 1:P], None, ALU.subtract)
                seq(nc.vector.tensor_tensor(m_diag[0:LH], cst2("head_neg")[0:LH].rearrange("p (a n) -> p a n", a=4),
                                            mx.unsqueeze(1).to_broadcast([LH, LH, P]), ALU.mult))
                nc.vector.tensor_scalar(g_dec[0:LH], ident[0:LH, 0:LH], o[:, 1, P - 1:P], None, ALU.mult)
                nc.vector.tensor_scalar(m_state[0:LH, :], o[:, 2, P - 1:P], -1.0, None, ALU.mult).then_inc(n_rows, 1)

            dve.wait_ge(n_const, 16 * N_CONST2)
            nc.vector.memset(state, 0.0)
            nc.vector.memset(ones, 1.0)
            nc.vector.memset(v_ext[:, :, :, LD:LD + 1], 1.0)
            nc.vector.tensor_scalar(head_g, head_g, 0.5, None, ALU.mult).then_inc(n_head, 1)
            dve.wait_ge(n_head, 1)
            token_scale(0, 0)
            weight_scales()
            take_lower(0)
            for g in range(3):
                lower_weights(g)
            shift(0)
            take_qk(0, 0, 0)
            take_qk(0, 1, 1)
            gate_bias(0, 0)
            lower_weights(3)
            lower_weights(4)
            dve.wait_ge(h_wl, B_GROUPS * KT)
            seq(nc.vector.memset(m_state, 0.0))
            gate_abs(0)
            dve.wait_ge(n_pjf, 2)
            conv(0, 0, 0, range(CONV))
            conv(0, 0, 1, range(CONV))
            silu(0, 0)
            shift(1)
            token_scale(1, 1)
            gate_math(0)
            take_lower(1)

            def step(c, par):
                nxt = not static(c) or c + 1 < NC
                npar = 1 - par
                dve.wait_ge(n_colt, c + 1)
                nc.vector.tensor_scalar(q_inter, e_col[:, par, 0:4], LD ** -0.5, None, ALU.mult).then_inc(n_qi, 1)
                dve.wait_ge(n_dt, c + 1)
                if not static(c) or c:
                    dve.wait_ge(n_num, c)
                for h in range(LH):
                    ins = nc.vector.scalar_tensor_tensor(decay[:, h, :], b_dt[:, h, :], a_col[:, par, h:h + 1], cst2("after"),
                                                         ALU.add, ALU.min)
                ins.then_inc(n_darg, 1)
                dve.wait_ge(n_st, c + 1)
                dve.wait_ge(n_dexp, c + 1)
                nc.vector.scalar_tensor_tensor(decay, b_st, LD ** -0.5, decay, ALU.mult, ALU.mult).then_inc(n_p, 1)
                if nxt:
                    take_qk(c + 1, 0, pj2_at(c, 0))
                    dve.wait_ge(n_pjf, pj2_at(c, 1))
                    conv(c + 1, npar, 0, range(0, CONV - 1))
                    take_qk(c + 1, 1, pj2_at(c, 1))
                    gate_bias(c + 1, npar)
                    dve.wait_ge(n_pjf, pj2_at(c, 2))
                    conv(c + 1, npar, 0, range(CONV - 1, CONV))
                    conv(c + 1, npar, 1, range(0, 1))
                dve.wait_ge(n_upd, c + 1)
                for h in range(LH):
                    ins = nc.vector.scalar_tensor_tensor(state[:, h, :], state[:, h, :], e_col[:, par, 12 + h:13 + h], ext(h),
                                                         ALU.mult, ALU.add)
                ins.then_inc(n_state, 1)
                if nxt:
                    conv(c + 1, npar, 1, range(1, CONV))
                dve.wait_ge(n_num, c + 1)
                dve.wait_ge(n_qct, c + 1)
                for j in range(2):
                    two = hn[:, 2 * j:2 * j + 2, :]
                    ins = nc.vector.tensor_tensor(two, b_ext[:, j, 0:2 * (LD + 1)].rearrange("p (a n) -> p a n", a=2), two, ALU.add)
                ins.then_inc(n_numt, 1)
                dve.wait_ge(n_numt, c + 1)
                d = hn[:, :, LD]
                seq(nc.vector.scalar_tensor_tensor(den, d, -1.0, d, ALU.mult, ALU.max))
                seq(nc.vector.tensor_tensor(den, den, e_col[:, par, 4:8], ALU.max))
                seq(nc.vector.reciprocal(rden, den))
                for h in range(LH):
                    ins = nc.vector.tensor_scalar(hn[:, h, 0:LD], hn[:, h, 0:LD], rden[:, h:h + 1], None, ALU.mult)
                seq(ins)
                for h in range(LH):
                    ins = nc.vector.bn_stats(h_stats[:, h, :], hn[:, h, 0:LD])
                seq(ins)
                settled(dve)
                for h in range(LH):
                    ins = nc.vector.bn_aggr(h_mv[:, h, :], h_stats[:, h, :])
                seq(ins)
                nc.vector.tensor_scalar(h_var, h_mv[:, :, 1], LN_EPS, None, ALU.add).then_inc(n_hvar, 1)
                if nxt:
                    gate_abs(c + 1)
                    silu(c + 1, npar)
                    if not static(c) or c + 2 < NC:
                        shift(c + 2)
                dve.wait_ge(n_hrs, c + 1)
                if not static(c) or c:
                    dve.wait_ge(n_tp, c * 3 + 1)
                for h in range(LH):
                    ins = nc.vector.tensor_scalar(b_y[:, h * LD:(h + 1) * LD], hn[:, h, 0:LD], h_mv[:, h, 0:1], h_rstd[:, h:h + 1],
                                                  ALU.subtract, ALU.mult)
                seq(ins)
                seq(nc.vector.tensor_tensor(b_y[:, 0:M_W], b_y[:, 0:M_W], head_g, ALU.mult))
                nc.vector.scalar_tensor_tensor(b_y[:, 0:M_W], o_th[:, par, :], 1.0, b_y[:, 0:M_W], ALU.add, ALU.mult)
                dve.wait_ge(n_pjf, pj2_at(c, 3 if nxt else 1))
                nc.vector.tensor_tensor(b_y[:, M_W:D], b_y[:, M_W:D], pool_sc, ALU.mult).then_inc(n_y, 1)
                if not static(c) or c + 2 < NC:
                    token_scale(c + 2, par)
                if nxt:
                    gate_math(c + 1)
                if not static(c) or c + 2 < NC:
                    take_lower(c + 2)
                dve.wait_ge(n_pjf, pj2_at(c, 8 if nxt else 3))
                dve.wait_ge(n_xres, c * 16 + 16)
                if static(c) and c == 0:
                    dve.wait_ge(n_wout, 48)
                seq(nc.vector.scalar_tensor_tensor(b_o, b_xres, ALPHA, b_o, ALU.mult, ALU.add))
                for j in range(2):
                    ins = nc.vector.bn_stats(r_stats[:, j, :], b_o[:, j * 512:(j + 1) * 512])
                seq(ins)
                settled(dve)
                seq(nc.vector.bn_aggr(r_mv, r_stats.rearrange("p a b -> p (a b)")))
                nc.vector.tensor_scalar(r_var, r_mv[:, 1:2], LN_EPS, None, ALU.add).then_inc(n_rvar, 1)
                dve.wait_ge(n_rrs, c + 1)
                seq(nc.vector.tensor_scalar(b_o, b_o, r_mv[:, 0:1], r_rstd, ALU.subtract, ALU.mult))
                seq(nc.vector.tensor_tensor(b_o, b_o, mix_g, ALU.mult))
                nc.vector.tensor_tensor(b_o, b_o, mix_b, ALU.add).then_inc(n_x2, 1)

            run_chunks(dve, step, ch)

        def b_gpsimd(pool):
            pool.wait_ge(h_am, 1)
            nc.gpsimd.tensor_reduce(b_all[0:1, :], b_abs, mybir.AxisListType.C, ALU.max).then_inc(h_gm, 1)

            def step(c, par):
                pool.wait_ge(n_hvar, c + 1)
                nc.gpsimd.tensor_tensor(h_rstd, h_var, neg_half, ALU.pow).then_inc(n_hrs, 1)
                pool.wait_ge(n_rvar, c + 1)
                nc.gpsimd.tensor_tensor(r_rstd, r_var, neg_half[:, 0:1], ALU.pow).then_inc(n_rrs, 1)

            run_chunks(pool, step)

        x3_d = out if stop_after == "c" else dram("x3_scratch", [S, D])
        m = Arena(arena[:, :], SB)
        m.at = shared_end
        w_k_at, w_v_at = m.take(KT * D), m.take(KT * D)
        w_xk, w_xv = (w.rearrange("p (k n) -> p k n", k=KT) for w in (w_k_at, w_v_at))
        q_hi, q_lo = halves(w_k_at, KT)
        o_hi, o_lo = halves(w_v_at, KT)
        c_rows = m.take(2, D)
        assert m.at <= shared_end + KT * IN2
        raw_at = m.at
        raw_q = m.take(KT, D)
        raw_o = m.take(KT, D)
        scores = m.take(NC, NE)
        c_end = m.at
        xkT = m.take(KT, MEM)
        xv = m.take(2, D)
        c_xin = m.take(D)
        c_xres = m.take(D)
        cx_hi, cx_lo = halves(m.take(D), KT)
        c_stage = m.take(4 * D)
        c_memT = c_stage[:, 2 * D:4 * D].rearrange("p (k n) -> p k n", k=KT)
        c_qT = m.take(KT, P)
        c_prob = c_stage[:, 0:D].rearrange("p (h n) -> p h n", h=XH)
        c_pT = c_stage[:, D:2 * D].rearrange("p (k n) -> p k n", k=KT)
        c_att = c_stage[:, 2 * D:3 * D]
        att_hi, att_lo = halves(c_stage[:, 3 * D:4 * D], KT)
        c_o = m.take(D)
        c_oT = m.take(KT, P)
        lnx_g, lnx_b = m.take(D), m.take(D)
        r_w = m.take(KT, NE)
        r_exp = m.take(NE)
        tok_diag, att_diag = m.take(P), m.take(P)
        ones_row = m.take(P)
        abs_max, all_max = m.take(1), m.take(1)
        tok_pow, tok_inv, tok_back = m.take(1), m.take(1), m.take(2, 1)
        q_pow, q_inv, q_back = m.take(1), m.take(1), m.take(1)
        o_pow, o_inv = m.take(1), m.take(1)
        v_pow, v_inv, out_back = m.take(1), m.take(1), m.take(1)
        c_max, c_nmax, c_sum, c_rden = m.take(XH), m.take(XH), m.take(XH), m.take(XH)
        c_stats, c_mv, c_var, c_rstd = m.take(2, 6), m.take(2), m.take(1), m.take(1)
        c_pv = psum[:, 6:8, :].rearrange("p b (a n) -> p (b a) n", a=2)
        r_ps = psum[:, 4, 0:NE]

        c_mem, c_const, c_wkv, c_wq, c_wo = (sem("c_memory_loaded"), sem("c_const_loaded"), sem("c_w_kv_loaded"), sem("c_w_q_loaded"), sem("c_w_o_loaded"))
        c_xin_ld, c_xres_ld, c_x3st = sem("c_x_in_loaded"), sem("c_x_res_loaded"), sem("c_x3_stored")
        c_tp, c_tpf, c_pj, c_pjf = sem("c_turned"), sem("c_turned_taken"), sem("c_proj_done"), sem("c_proj_taken")
        c_lg, c_nm, c_ex, c_pvd, c_rd, c_pvt = (sem("c_logits_done"), sem("c_max_ready"), sem("c_exp_ready"), sem("c_values_done"),
                                                sem("c_denominator_ready"), sem("c_values_taken"))
        c_dg, c_hi = sem("c_token_scale_ready"), sem("c_upper_half_ready")
        c_rvar, c_rrs, c_x3 = sem("c_row_var"), sem("c_row_rstd"), sem("c_x3_ready")
        r_lg, r_ex, r_sc = sem("c_router_done"), sem("c_router_exp"), sem("c_router_scores")
        N_CONST3 = 3
        TOKEN_SCALE_LINKS = 5
        SETUP_PJ = 8

        def tp3_at(c, n):
            if static(c) and c == 0:
                return 4 + n
            return c * 4 + (3 + n) - (1 if static(c) and c == NC - 1 else 0)

        def pj3_at(c, n):
            return c * 4 + (SETUP_PJ + 2 + n)

        def hi_at(c, n):
            return c * 2 + (2 + n) - (1 if static(c) and c == NC - 1 else 0)

        def c_sync(sp):
            sp.wait_ge(n_pj, pj2_at(NC - 2, 6))
            sp.wait_ge(n_gp, NC)
            sp.dma_start(c_rows, t["mem_2"].rearrange("(a p) n -> p a n", p=P)).then_inc(c_mem, 16)
            for dst, o in ((w_xk, 0), (w_xv, D)):
                sp.dma_start(dst, t["w_xkv_2"].rearrange("(k p) n -> p k n", p=P)[:, :, o:o + D]).then_inc(c_wkv, 16)

        def c_sync_main(sp, before_last):
            sp.dma_start(raw_q, t["w_xq_2"].rearrange("(k p) n -> p k n", p=P)).then_inc(c_wq, 16)
            sp.dma_start(c_xin, rows(x2_d, 0)).then_inc(c_xin_ld, 16)
            for dst, name in ((lnx_g, "ln_x_g_2"), (lnx_b, "ln_x_b_2")):
                sp.dma_start(dst, t[name].partition_broadcast(P)).then_inc(c_const, 16)
            sp.dma_start(r_w, t["router_w_2"].rearrange("(k p) n -> p k n", p=P)).then_inc(c_const, 16)
            sp.dma_start(raw_o, t["w_xo_2"].rearrange("(k p) n -> p k n", p=P)).then_inc(c_wo, 16)
            sp.dma_start(c_xres, rows(x2_d, 0)).then_inc(c_xres_ld, 16)
            for c in (1, 2):
                sp.wait_ge(c_tp, c + 2)
                sp.dma_start(c_xin, rows(x2_d, c)).then_inc(c_xin_ld, 16)

            def step(c, par):
                if not static(c) or c + 3 < NC:
                    sp.wait_ge(c_tp, tp3_at(c, 2 if static(c) and c == 0 else 3) + 1)
                    sp.dma_start(c_xin, rows(x2_d, c + 3)).then_inc(c_xin_ld, 16)
                sp.wait_ge(c_x3, c + 1)
                sp.dma_start(rows(x3_d, c), c_o).then_inc(c_x3st, 16)
                if not static(c) or c + 1 < NC:
                    sp.dma_start(c_xres, rows(x2_d, c + 1)).then_inc(c_xres_ld, 16)

            run_chunks(sp, step, before_last=before_last)
            sp.wait_ge(c_x3st, 16 * NC)

        def c_tensor(pe):
            def turn(src, at):
                if not static(at) or at:
                    pe.wait_ge(c_tpf, at)
                for i, tile in enumerate(src):
                    ins = nc.tensor.transpose(tp[:, i, :], tile, ident)
                ins.then_inc(c_tp, 1)

            def tiles(ap):
                return [ap[:, k * P:(k + 1) * P] for k in range(KT)]

            def turn_scaled(src, diag, at):
                pe.wait_ge(c_tpf, at)
                for i, tile in enumerate(src):
                    ins = nc.tensor.matmul(tp[:, i, :], tile, diag, start=True, stop=True)
                ins.then_inc(c_tp, 1)

            def front(c, at):
                pe.wait_ge(c_dg, c + 1)
                turn_scaled(tiles(c_xin), tok_diag, at)

            def spread(n):
                pe.wait_ge(h_gm, C_SCALE + n + 1)
                nc.tensor.matmul(psum[:, 7, 0:1], ones_row[0:1, :], all_max[0:1, :], start=True, stop=True).then_inc(h_bc, 1)

            def free_pj(at):
                if not static(at) or at >= 2:
                    pe.wait_ge(c_pjf, at - 1)

            def queries(g, at, tiles_of=range(4)):
                if tiles_of[0] == 0:
                    free_pj(at)
                for i in tiles_of:
                    o = (4 * g + i) * P
                    for k in range(KT):
                        for w, x in ((q_hi, cx_hi), (q_hi, cx_lo), (q_lo, cx_hi)):
                            ins = nc.tensor.matmul(pj[g][:, i * P:(i + 1) * P], w[:, k, o:o + P], x[:, k, :],
                                                   start=(k == 0 and x is cx_hi and w is q_hi), stop=(k == KT - 1 and w is q_lo))
                if tiles_of[-1] == 3:
                    ins.then_inc(c_pj, 1)

            def router(c):
                for k in range(KT):
                    ins = nc.tensor.matmul(r_ps, c_oT[:, k, :], r_w[:, k, :], start=(k == 0), stop=(k == KT - 1))
                ins.then_inc(r_lg, 1)

            pe.wait_ge(c_mem, 16)
            for a in range(2):
                turn(tiles(c_rows[:, a, :]), a)
            pe.wait_ge(c_tpf, 2)
            pe.wait_ge(c_wkv, 32)
            pe.wait_ge(n_pjf, pj2_at(NC - 1, 3))
            for j in range(4):
                free_pj(j)
                for i in range(2):
                    o = (2 * j + i) * P
                    for k in range(KT):
                        ins = nc.tensor.matmul(pj[j % 2][:, i * MEM:(i + 1) * MEM], w_xk[:, k, o:o + P], c_memT[:, k, :],
                                               start=(k == 0), stop=(k == KT - 1))
                ins.then_inc(c_pj, 1)
            spread(0)
            for j in range(4):
                free_pj(4 + j)
                a, o = j // 2, (j % 2) * 512
                for k in range(KT):
                    ins = nc.tensor.matmul(pj[j % 2], c_memT[:, k, a * P:(a + 1) * P], w_xv[:, k, o:o + 512],
                                           start=(k == 0), stop=(k == KT - 1))
                ins.then_inc(c_pj, 1)
            front(0, 2)
            pe.wait_ge(c_tpf, 3)
            pe.wait_ge(h_wl, C_TILE + KT)
            for g in range(2):
                queries(g, SETUP_PJ + g)
            spread(1)
            spread(2)
            front(1, 3)

            def step(c, par):
                first = static(c) and c == 0
                nxt = not static(c) or c + 1 < NC
                n = 0
                pe.wait_ge(c_pjf, pj3_at(c, 0))
                if not first:
                    pe.wait_ge(r_ex, c - 1)
                for h in range(XH):
                    for k in range(2):
                        ins = nc.tensor.matmul(lg[:, h, :], c_qT[:, 2 * h + k, :], xkT[:, 2 * h + k, :], start=(k == 0), stop=(k == 1))
                ins.then_inc(c_lg, 1)
                if nxt:
                    pe.wait_ge(c_tpf, tp3_at(c, 0))
                    queries(0, pj3_at(c, 0))
                pe.wait_ge(c_ex, c + 1)
                turn([c_prob[:, h, b * P:(b + 1) * P] for h in range(XH) for b in range(2)], tp3_at(c, n))
                if nxt:
                    queries(1, pj3_at(c, 1), range(0, 2))
                pe.wait_ge(c_tpf, tp3_at(c, n) + 1)
                if first:
                    pe.wait_ge(h_sc, C_SCALE + 3)
                else:
                    pe.wait_ge(c_pvt, c)
                for h in range(XH):
                    for b in range(2):
                        ins = nc.tensor.matmul(c_pv[:, h, :], c_pT[:, 2 * h + b, :], xv[:, b, h * XD:(h + 1) * XD],
                                               start=(b == 0), stop=(b == 1))
                ins.then_inc(c_pvd, 1)
                n += 1
                if not first:
                    pe.wait_ge(c_x3, c)
                    turn(tiles(c_o), tp3_at(c, n))
                    n += 1
                pe.wait_ge(c_pvt, c + 1)
                if first:
                    pe.wait_ge(h_wl, C_TILE + 2 * KT)
                turn_scaled(tiles(c_att), att_diag, tp3_at(c, n))
                if static(c) and c == 1:
                    pe.wait_ge(c_const, 16 * N_CONST3)
                if not first:
                    router(c - 1)
                if nxt:
                    queries(1, pj3_at(c, 1), range(2, 4))
                n += 1
                if not static(c) or c + 2 < NC:
                    front(c + 2, tp3_at(c, n))
                pe.wait_ge(c_tpf, tp3_at(c, n))
                for j in range(2):
                    at = pj3_at(c, (2 if nxt else 0) + j)
                    free_pj(at)
                    for k in range(KT):
                        for x, w in ((att_hi, o_hi), (att_hi, o_lo), (att_lo, o_hi)):
                            ins = nc.tensor.matmul(pj[j], x[:, k, :], w[:, k, j * 512:(j + 1) * 512],
                                                   start=(k == 0 and x is att_hi and w is o_hi), stop=(k == KT - 1 and x is att_lo))
                    ins.then_inc(c_pj, 1)

            run_chunks(pe, step)
            pe.wait_ge(c_x3, NC)
            turn(tiles(c_o), tp3_at(NC - 1, 3))
            pe.wait_ge(c_tpf, tp3_at(NC - 1, 3) + 1)
            pe.wait_ge(r_ex, NC - 1)
            router(NC - 1)

        def c_scalar(act):
            def copy(dst, src, scale=1.0):
                return nc.scalar.activation(dst, src, ACT.Copy, scale=scale)

            def take_tiles(dst, at):
                act.wait_ge(c_tp, at + 1)
                copy(dst[:, 0:4, :], tp[:, 0:4, :])
                copy(dst[:, 4:8, :], tp[:, 4:8, :]).then_inc(c_tpf, 1)

            def take_upper(dst, at):
                act.wait_ge(c_tp, at + 1)
                copy(dst[:, 0:4, :], tp[:, 0:4, :])
                copy(dst[:, 4:8, :], tp[:, 4:8, :]).then_inc(c_hi, 1)

            def upper_weights(dst, src, scale, n):
                for k in range(*n):
                    copy(dst[:, k, :], src[:, k, :], scale).then_inc(h_wh, 1)

            def take_queries(g, at):
                act.wait_ge(c_pj, at + 1)
                copy(c_qT[:, 4 * g:4 * g + 4, :], pj[g].rearrange("p (a n) -> p a n", a=4)).then_inc(c_pjf, 1)

            def router_exp(c):
                act.wait_ge(r_lg, c + 1)
                if not static(c) or c:
                    act.wait_ge(r_sc, c)
                nc.scalar.activation(r_exp, r_ps, ACT.Exp, scale=-1.0).then_inc(r_ex, 1)

            for a in range(2):
                act.wait_ge(c_tp, a + 1)
                copy(c_memT[:, 0:4, a * P:(a + 1) * P], tp[:, 0:4, :])
                copy(c_memT[:, 4:8, a * P:(a + 1) * P], tp[:, 4:8, :]).then_inc(c_tpf, 1)
            for j in range(4):
                act.wait_ge(c_pj, j + 1)
                copy(xkT[:, 2 * j:2 * j + 2, :], pj[j % 2].rearrange("p (a n) -> p a n", a=2)).then_inc(c_pjf, 1)
            act.wait_ge(h_sc, C_SCALE + 1)
            for j in range(4):
                upper_weights(q_hi, raw_q, q_inv, (2 * j, 2 * j + 2))
                act.wait_ge(c_pj, 5 + j)
                copy(xv[:, j // 2, (j % 2) * 512:(j % 2) * 512 + 512], pj[j % 2]).then_inc(c_pjf, 1)
            take_upper(cx_hi, 2)
            act.wait_ge(h_sc, C_SCALE + 2)
            upper_weights(o_hi, raw_o, o_inv, (0, KT))
            for g in range(2):
                take_queries(g, SETUP_PJ + g)
            take_upper(cx_hi, 3)

            def step(c, par):
                first = static(c) and c == 0
                nxt = not static(c) or c + 1 < NC
                n = 0
                act.wait_ge(c_nm, c + 1)
                for h in range(XH):
                    ins = nc.scalar.activation(c_prob[:, h, :], lg[:, h, :], ACT.Exp, bias=c_nmax[:, h:h + 1],
                                               scale=tok_back[:, par, :], accum_out=c_sum[:, h:h + 1])
                ins.then_inc(c_ex, 1)
                if nxt:
                    take_queries(0, pj3_at(c, 0))
                take_tiles(c_pT, tp3_at(c, n))
                n += 1
                act.wait_ge(c_rd, c + 1)
                act.wait_ge(c_pvd, c + 1)
                for h in range(XH):
                    ins = copy(c_att[:, h * XD:(h + 1) * XD], c_pv[:, h, :], c_rden[:, h:h + 1])
                ins.then_inc(c_pvt, 1)
                if not first:
                    take_tiles(c_oT, tp3_at(c, n))
                    n += 1
                take_upper(att_hi, tp3_at(c, n))
                if not first:
                    router_exp(c - 1)
                n += 1
                if nxt:
                    take_queries(1, pj3_at(c, 1))
                if not static(c) or c + 2 < NC:
                    take_upper(cx_hi, tp3_at(c, n))
                if not first:
                    act.wait_ge(c_x3st, c * 16)
                for j in range(2):
                    act.wait_ge(c_pj, pj3_at(c, (2 if nxt else 0) + j) + 1)
                    copy(c_o[:, j * 512:(j + 1) * 512], pj[j], out_back).then_inc(c_pjf, 1)

            run_chunks(act, step)
            take_tiles(c_oT, tp3_at(NC - 1, 3))
            router_exp(NC - 1)

        def c_vector(dve, ch):
            def seq(ins):
                ch.link(ins)
                ch.wait()

            def largest_of(src, n):
                dve.wait_ge(h_bc, C_SCALE + n)
                nc.vector.tensor_reduce(abs_max, src, mybir.AxisListType.XY, ALU.max, apply_absolute_value=True).then_inc(h_am, 1)
                dve.wait_ge(h_bc, C_SCALE + n + 1)

            def lower_weights(dst, src, hi, scale, first):
                for k in range(KT):
                    dve.wait_ge(h_wh, C_TILE + first * KT + k + 1)
                    nc.vector.scalar_tensor_tensor(dst[:, k, :], src[:, k, :], scale, hi[:, k, :], ALU.mult, ALU.subtract)\
                      .then_inc(h_wl, 1)

            def take_lower(dst, hi, at):
                dve.wait_ge(c_hi, at + 1)
                for i in range(0, KT, 4):
                    ins = nc.vector.tensor_tensor(dst[:, i:i + 4, :], tp[:, i:i + 4, :], hi[:, i:i + 4, :], ALU.subtract)
                ins.then_inc(c_tpf, 1)

            def token_scale(c, par):
                dve.wait_ge(c_xin_ld, c * 16 + 16)
                seq(nc.vector.tensor_reduce(tok_pow, c_xin, AX, ALU.max, apply_absolute_value=True))
                seq(power(seq, tok_pow, tok_inv, tok_pow))
                nc.vector.tensor_tensor(tok_back[:, par, :], tok_pow, q_back, ALU.mult)
                nc.vector.tensor_scalar(tok_diag, ident, tok_inv, None, ALU.mult).then_inc(c_dg, 1)

            def router_scores(c):
                dve.wait_ge(r_ex, c + 1)
                seq(nc.vector.tensor_scalar(r_exp, r_exp, 1.0, None, ALU.add))
                dst = scores[:, c, :] if static(c) else scores[:, bass.ds(c, 1), :].rearrange("p a n -> p (a n)")
                nc.vector.reciprocal(dst, r_exp).then_inc(r_sc, 1)

            def step(c, par):
                first = static(c) and c == 0
                nxt = not static(c) or c + 1 < NC
                dve.wait_ge(c_lg, c + 1)
                seq(nc.vector.tensor_reduce(c_max, lg, AX, ALU.max))
                nc.vector.tensor_scalar(c_nmax, c_max, tok_back[:, par, :], -1.0, ALU.mult, ALU.mult).then_inc(c_nm, 1)
                dve.wait_ge(c_ex, c + 1)
                if not first:
                    dve.wait_ge(c_pvt, c)
                nc.vector.reciprocal(c_rden, c_sum).then_inc(c_rd, 1)
                if not static(c) or c + 2 < NC:
                    token_scale(c + 2, par)
                else:
                    for _ in range(TOKEN_SCALE_LINKS):
                        ch.n += 1
                        dve.sem_inc(s_dve, 1)
                if not first:
                    router_scores(c - 1)
                else:
                    ch.n += 1
                    dve.sem_inc(s_dve, 1)
                take_lower(att_lo, att_hi, hi_at(c, 0))
                if not static(c) or c + 2 < NC:
                    take_lower(cx_lo, cx_hi, hi_at(c, 1))
                dve.wait_ge(c_pjf, pj3_at(c, 4 if nxt else 2))
                dve.wait_ge(c_xres_ld, c * 16 + 16)
                seq(nc.vector.scalar_tensor_tensor(c_o, c_xres, ALPHA, c_o, ALU.mult, ALU.add))
                for j in range(2):
                    ins = nc.vector.bn_stats(c_stats[:, j, :], c_o[:, j * 512:(j + 1) * 512])
                seq(ins)
                settled(dve)
                seq(nc.vector.bn_aggr(c_mv, c_stats.rearrange("p a b -> p (a b)")))
                nc.vector.tensor_scalar(c_var, c_mv[:, 1:2], LN_EPS, None, ALU.add).then_inc(c_rvar, 1)
                dve.wait_ge(c_rrs, c + 1)
                seq(nc.vector.scalar_tensor_tensor(c_o, c_o, c_mv[:, 0:1], lnx_g, ALU.subtract, ALU.mult))
                nc.vector.scalar_tensor_tensor(c_o, c_o, c_rstd, lnx_b, ALU.mult, ALU.add).then_inc(c_x3, 1)

            dve.wait_ge(n_x2, NC)
            nc.vector.memset(ones_row, 1.0)
            dve.wait_ge(c_wq, 16)
            largest_of(raw_q, 0)
            seq(power(seq, q_pow, q_inv, psum[:, 7, 0:1]))
            nc.vector.tensor_scalar(q_back, q_pow, XD ** -0.5 / HALF_TOP ** 2, None, ALU.mult).then_inc(h_sc, 1)
            token_scale(0, 0)
            lower_weights(q_lo, raw_q, q_hi, q_inv, 0)
            take_lower(cx_lo, cx_hi, 0)
            dve.wait_ge(c_wo, 16)
            largest_of(raw_o, 1)
            power(seq, o_pow, o_inv, psum[:, 7, 0:1]).then_inc(h_sc, 1)
            token_scale(1, 1)
            dve.wait_ge(c_pjf, SETUP_PJ)
            largest_of(xv, 2)
            seq(power(seq, v_pow, v_inv, psum[:, 7, 0:1]))
            seq(nc.vector.tensor_scalar(att_diag, ident, v_inv, None, ALU.mult))
            nc.vector.scalar_tensor_tensor(out_back, v_pow, HALF_TOP ** -2, o_pow, ALU.mult, ALU.mult).then_inc(h_sc, 1)
            take_lower(cx_lo, cx_hi, 1)
            lower_weights(o_lo, raw_o, o_hi, o_inv, 1)
            dve.wait_ge(c_const, 16 * N_CONST3)
            run_chunks(dve, step, ch)
            router_scores(NC - 1)

        def c_gpsimd(pool):
            for n in range(3):
                pool.wait_ge(h_am, C_SCALE + n + 1)
                nc.gpsimd.tensor_reduce(all_max[0:1, :], abs_max, mybir.AxisListType.C, ALU.max).then_inc(h_gm, 1)

            def step(c, par):
                pool.wait_ge(c_rvar, c + 1)
                nc.gpsimd.tensor_tensor(c_rstd, c_var, neg_half[:, 0:1], ALU.pow).then_inc(c_rrs, 1)

            run_chunks(pool, step)

        yb_d = dram("expert_rows_scratch", [NB * P, D])
        m = Arena(arena[:, :], c_end - NC * NE)
        m.at = raw_at
        w_gu = m.take(2, KT, 2 * FE)
        w_dn = m.take(2, 2, D)
        tab3 = m.take(CONST3_W)
        r_bias = m.take(NE)
        lnm_g, lnm_b = m.take(D), m.take(D)
        below = Arena(arena[:, :], raw_at)
        below.at = shared_end
        m = Arena(arena[:, :], SB)
        m.at = c_end
        sel = m.take(NC, NE)
        pair = [m.take(NC * NG) for _ in range(7)]
        gsum = m.take(NC, NG)
        g_best, g_idx = m.take(NC), m.take(NC)
        g_cand = m.take(NC, NG)
        ingrp = m.take(NC, NE)
        selm = m.take(NC, NE)
        cand = m.take(NC, NE)
        best, pick_i = m.take(NC), m.take(NC)
        pick = m.take(2, NC, NE)
        took = m.take(NC, NE)
        prod = m.take(NC, NE)
        gate = m.take(2, NC)
        gate_sum = m.take(NC)
        total = m.take(NC, NE)
        rank = m.take(NC, NE)
        base = m.take(NC + 1, NE)
        more = m.take(NE, NC)
        nblk, pend, pstart = m.take(NE), m.take(NE), m.take(NE)
        blk_cmp = m.take(NB, NE)
        blk_e = m.take(NB)
        place_e = m.take(2, NC)
        q_f, s_f = m.take(2 * NC), m.take(2 * NC)
        hot_s = m.take(2 * NC, P)
        hot_q = m.take(2 * NC, 2, NB)
        row_gate = m.take(NB)
        dest_i = m.take(2 * NC).bitcast(I32)
        q_i = m.take(2 * NC).bitcast(I32)
        s_i = m.take(2 * NC).bitcast(I32)
        blk_i = m.take(NB).bitcast(I32)
        exp_done = m.take(NE).bitcast(I32)
        done_f = m.take(NE)
        src_i = m.take(NB).bitcast(I32)
        xb = below.take(2, D)
        xbT = below.take(2, KT, P)
        e_th = below.take(FE)
        e_h = below.take(FE)
        e_hT = below.take(2, P)
        yb = below.take(2, D)
        xidx = m.take(2, 1).bitcast(I32)
        yidx = m.take(3, 2).bitcast(I32)
        f_x = below.take(3, D)
        f_y = below.take(3, 2, D)
        f_stats, f_mv, f_var, f_rstd = m.take(2, 6), m.take(2), m.take(1), m.take(1)

        def cst3(name):
            o, w = CONST3[name]
            return tab3[:, o:o + w]

        r_prefix = psum[:, 6, 0:NC * NE].rearrange("p (a n) -> p a n", a=NC)
        r_total = psum[:, 7, 0:NC * NE].rearrange("p (a n) -> p a n", a=NC)
        r_rows = psum[:, 6, 0:2 * NB]
        r_src, r_gate = r_rows[:, 0:NB], r_rows[:, NB:2 * NB]
        gu_ps = [psum[:, 4, :], psum[:, 5, :]]
        hT_ps = psum[:, 6, 0:2 * P].rearrange("p (a n) -> p a n", a=2)

        d_const = sem("d_const_loaded")
        d_vec = sem("d_vector_steps")
        d_mm = sem("d_tensor_steps")
        e_idx = sem("e_rows_known")
        e_gath = [sem("e_even_rows_gathered"), sem("e_odd_rows_gathered")]
        e_w = sem("e_weights_loaded")
        e_st, f_xl = sem("e_rows_stored"), sem("f_x_loaded")
        f_g = [*e_gath, sem("f_third_rows_gathered")]
        f_g_from = [16 * NB // 2, 16 * NB // 2, 0]

        def done(b, par, each):
            return (b // 2 + 1) * each if static(b) else b * (each // 2) + (each - par * (each // 2))

        e_tp, e_tpf, e_gu, e_tanh, e_hr = (sem("e_turned"), sem("e_turned_taken"), sem("e_gate_up_done"), sem("e_tanh_ready"),
                                           sem("e_hidden_ready"))
        e_ht, e_htt, e_pj, e_pjf = (sem("e_hidden_turned"), sem("e_hidden_taken"), sem("e_down_done"), sem("e_down_taken"))
        f_idx, f_acc, f_rv, f_rr, f_out, f_st = (
            sem("f_rows_known"), sem("f_sum_ready"),
            sem("f_row_var"), sem("f_row_rstd"), sem("f_out_ready"), sem("f_out_stored"))

        def d_sync(sp):
            for dst, src in ((tab3, t["tables3"]), (r_bias, t["router_bias_2"].partition_broadcast(P)),
                             (lnm_g, t["ln_moe_g_2"].partition_broadcast(P)), (lnm_b, t["ln_moe_b_2"].partition_broadcast(P))):
                sp.dma_start(dst, src).then_inc(d_const, 16)

        def d_vector(dve, ch):
            def seq(ins):
                ch.link(ins)
                ch.wait()

            def over(ap, n):
                return ap.unsqueeze(2).to_broadcast([P, ap.shape[1], n])

            def under(ap, n):
                return ap.unsqueeze(1).to_broadcast([P, n, ap.shape[1]])

            V = nc.vector
            dve.wait_ge(d_const, 16 * 4)
            dve.wait_ge(r_sc, NC)
            seq(V.tensor_tensor(sel, scores, under(r_bias, NC), ALU.add))
            four = sel.rearrange("p c (g e) -> p (c g) e", e=EPG)
            hi1, lo1, hi2, lo2, top, mid, low = pair
            V.tensor_tensor(hi1, four[:, :, 0], four[:, :, 1], ALU.max)
            V.tensor_tensor(lo1, four[:, :, 0], four[:, :, 1], ALU.min)
            V.tensor_tensor(hi2, four[:, :, 2], four[:, :, 3], ALU.max)
            seq(V.tensor_tensor(lo2, four[:, :, 2], four[:, :, 3], ALU.min))
            V.tensor_tensor(top, hi1, hi2, ALU.max)
            V.tensor_tensor(mid, hi1, hi2, ALU.min)
            seq(V.tensor_tensor(low, lo1, lo2, ALU.max))
            seq(V.tensor_tensor(mid, mid, low, ALU.max))
            seq(V.tensor_tensor(gsum.rearrange("p c g -> p (c g)"), top, mid, ALU.add))

            def first_of(dst, values, biggest, numbers, n):
                seq(V.tensor_reduce(biggest, values, AX, ALU.max))
                c_ = g_cand if n == NG else cand
                seq(V.tensor_tensor(c_, values, over(biggest, n), ALU.is_ge))
                seq(V.scalar_tensor_tensor(c_, under(numbers, NC), float(-n), c_, ALU.add, ALU.mult))
                seq(V.tensor_scalar(c_, c_, float(n), None, ALU.add))
                seq(V.tensor_reduce(dst, c_, AX, ALU.min))

            first_of(g_idx, gsum, g_best, cst3("group"), NG)
            seq(V.tensor_tensor(ingrp, under(cst3("group_of"), NC), over(g_idx, NE), ALU.is_equal))
            seq(V.tensor_tensor(selm, sel, ingrp, ALU.mult))
            seq(V.tensor_scalar(ingrp, ingrp, -1.0, FAR, ALU.add, ALU.mult))
            seq(V.tensor_tensor(selm, selm, ingrp, ALU.add))
            for k in range(2):
                first_of(pick_i, selm, best, cst3("expert"), NE)
                seq(V.tensor_tensor(pick[:, k], under(cst3("expert"), NC), over(pick_i, NE), ALU.is_equal))
                if k == 0:
                    seq(V.scalar_tensor_tensor(selm, pick[:, 0], -FAR, selm, ALU.mult, ALU.add))
                seq(V.tensor_tensor(prod, scores, pick[:, k], ALU.mult))
                seq(V.tensor_reduce(gate[:, k, :], prod, AX, ALU.add))
            V.tensor_tensor(took, pick[:, 0], pick[:, 1], ALU.add).then_inc(d_vec, 1)
            seq(V.tensor_tensor(gate_sum, gate[:, 0, :], gate[:, 1, :], ALU.add))
            seq(V.reciprocal(gate_sum, gate_sum))
            seq(V.tensor_tensor(gate, gate, under(gate_sum, 2), ALU.mult))
            dve.wait_ge(d_mm, 1)
            V.memset(base[:, 0, :], 0.0)
            V.tensor_copy(rank, r_prefix)
            seq(V.tensor_copy(total, r_total))
            for c in range(NC):
                seq(V.tensor_tensor(base[:, c + 1, :], base[:, c, :], total[:, c, :], ALU.add))
            seq(V.tensor_tensor(more, over(base[:, NC, :], NC), under(cst3("fills"), NE), ALU.is_gt))
            seq(V.tensor_reduce(nblk, more, AX, ALU.add))
            seq(V.tensor_tensor_scan(pend, cst3("one")[:, 0:NE], nblk, 0.0, ALU.mult, ALU.add))
            seq(V.tensor_tensor(pstart, pend, nblk, ALU.subtract))
            seq(V.tensor_scalar(pstart, pstart, float(P), None, ALU.mult))
            seq(V.tensor_tensor(rank, rank, base[:, 0:NC, :], ALU.add))
            seq(V.tensor_tensor(rank, rank, under(pstart, NC), ALU.add))
            for k in range(2):
                seq(V.tensor_tensor(prod, rank, pick[:, k], ALU.mult))
                seq(V.tensor_reduce(place_e[:, k, :], prod, AX, ALU.add))
            seq(V.tensor_tensor(blk_cmp, under(pend, NB), over(cst3("block"), NE), ALU.is_le))
            seq(V.tensor_reduce(blk_e, blk_cmp, AX, ALU.add))
            seq(V.tensor_scalar(blk_e, blk_e, float(NE - 1), None, ALU.min))
            V.tensor_scalar(done_f, pend, 2.0, 1.0, ALU.mult, ALU.add)
            seq(V.tensor_copy(blk_i, blk_e))
            V.tensor_copy(exp_done, done_f)
            seq(V.tensor_copy(dest_i, place_e.rearrange("p k c -> p (k c)")))
            V.tensor_scalar(q_i, dest_i, 7, None, ALU.logical_shift_right)
            seq(V.tensor_scalar(s_i, dest_i, P - 1, None, ALU.bitwise_and))
            V.tensor_copy(q_f, q_i)
            seq(V.tensor_copy(s_f, s_i))
            dve.wait_ge(c_x3st, 16 * NC)
            V.tensor_tensor(hot_s, under(cst3("place"), 2 * NC), over(s_f, P), ALU.is_equal)
            seq(V.tensor_tensor(hot_q[:, :, 0, :], under(cst3("block"), 2 * NC), over(q_f, NB), ALU.is_equal))
            seq(V.tensor_tensor(hot_q[:, :, 1, :], hot_q[:, :, 0, :], over(gate.rearrange("p k c -> p (k c)"), NB), ALU.mult))
            for k in range(2):
                ins = V.tensor_tensor(hot_q[:, k * NC:(k + 1) * NC, 0, :], hot_q[:, k * NC:(k + 1) * NC, 0, :],
                                      over(cst3("token"), NB), ALU.mult)
            ins.then_inc(d_vec, 1)
            dve.wait_ge(d_mm, 2)
            V.tensor_copy(src_i, r_src)
            V.tensor_copy(row_gate, r_gate).then_inc(d_vec, 1)

        def d_tensor(pe):
            pe.wait_ge(d_vec, 1)
            flat = took.rearrange("p c e -> p (c e)")
            nc.tensor.matmul(psum[:, 6, 0:NC * NE], cst3("before"), flat, start=True, stop=True)
            nc.tensor.matmul(psum[:, 7, 0:NC * NE], cst3("one"), flat, start=True, stop=True).then_inc(d_mm, 1)
            pe.wait_ge(d_vec, 2)
            for i in range(2 * NC):
                ins = nc.tensor.matmul(r_rows, hot_s[:, i, :], hot_q[:, i].rearrange("p a n -> p (a n)"),
                                       start=(i == 0), stop=(i == 2 * NC - 1))
            ins.then_inc(d_mm, 1)

        def load_expert(sp, e, slot):
            for dst, name in ((w_gu[:, slot, :, 0:FE], "w_gate_2"), (w_gu[:, slot, :, FE:2 * FE], "w_up_2"),
                              (w_dn[:, slot], "w_down_2")):
                src = t[name].rearrange("e (k p) n -> e p k n", p=P)
                src = src[e] if static(e) else src[bass.ds(e, 1)].rearrange("e p k n -> (e p) k n")
                sp.dma_start(dst, src).then_inc(e_w, 16)

        def e_sync_first(sp):
            sp.wait_ge(h_wl, C_TILE + 2 * KT)
            d_sync(sp)
            load_expert(sp, 0, 0)
            sp.wait_ge(e_w, 48)
            load_expert(sp, 1, 1)

        def e_sync(sp):

            def next_expert(e, slot):
                through = sp.value_load(exp_done[0:1, bass.ds(e - 2, 1)], min_val=1, max_val=2 * NB + 1)
                sp.wait_ge(e_pj, through)
                settled(sp)
                sp.wait_ge(e_w, e * 48)
                load_expert(sp, e, slot)

            sp.wait_ge(d_vec, 3)
            with sp.Fori(1, NE // 2) as i:
                next_expert(2 * i, 0)
                next_expert(2 * i + 1, 1)

        def e_tensor(pe):
            def front(b, par, at):
                pe.wait_ge(e_gath[par], done(b, par, 16))
                if not static(at) or at:
                    pe.wait_ge(e_tpf, at)
                for k in range(KT):
                    ins = nc.tensor.transpose(tp[:, k, :], xb[:, par, k * P:(k + 1) * P], ident)
                ins.then_inc(e_tp, 1)

            def expert(b):
                at = slice(b, b + 1) if static(b) else bass.ds(b, 1)
                return pe.value_load(blk_i[0:1, at], min_val=0, max_val=NE - 1)

            def buffer_of(e):
                return bass.ds(e & 1, 1)

            def gate_up(b, par, e):
                pe.wait_ge(e_w, e * 48 + 48)
                pe.wait_ge(e_tpf, b + 1)
                if not static(b) or b >= 2:
                    pe.wait_ge(e_hr, b - 1)
                for k in range(KT):
                    ins = nc.tensor.matmul(gu_ps[par], xbT[:, par, k, :], w_gu[:, buffer_of(e), k, :].rearrange("p a n -> p (a n)"),
                                           start=(k == 0), stop=(k == KT - 1))
                ins.then_inc(e_gu, 1)

            pe.sem_inc(e_pj, 1)
            pe.wait_ge(d_vec, 3)
            front(0, 0, 0)
            front(1, 1, 1)
            gate_up(0, 0, expert(0))

            def step(b, par):
                nxt = not static(b) or b + 1 < NB
                e = expert(b)
                pe.wait_ge(e_hr, b + 1)
                if not static(b) or b:
                    pe.wait_ge(e_htt, b)
                for k in range(2):
                    ins = nc.tensor.transpose(hT_ps[:, k, :], e_h[:, k * P:(k + 1) * P], ident)
                ins.then_inc(e_ht, 1)
                if nxt:
                    gate_up(b + 1, 1 - par, expert(b + 1))
                if not static(b) or b + 2 < NB:
                    front(b + 2, par, b + 2)
                pe.wait_ge(e_htt, b + 1)
                for j in range(2):
                    if not static(b) or b:
                        pe.wait_ge(e_pjf, b * 2 + (j - 1))
                    for k in range(2):
                        ins = nc.tensor.matmul(pj[j], e_hT[:, k, :],
                                               w_dn[:, buffer_of(e), k, j * 512:(j + 1) * 512].rearrange("p a n -> p (a n)"),
                                               start=(k == 0), stop=(k == 1))
                    ins.then_inc(e_pj, 1)

            run_chunks(pe, step, n=NB)

        def e_scalar(act):
            def copy(dst, src, scale=1.0):
                return nc.scalar.activation(dst, src, ACT.Copy, scale=scale)

            def take_x(b, par):
                act.wait_ge(e_tp, b + 1)
                copy(xbT[:, par, 0:4, :], tp[:, 0:4, :])
                copy(xbT[:, par, 4:8, :], tp[:, 4:8, :]).then_inc(e_tpf, 1)

            def tanh(b, par):
                act.wait_ge(e_gu, b + 1)
                if not static(b) or b:
                    act.wait_ge(e_hr, b)
                nc.scalar.activation(e_th, gu_ps[par][:, 0:FE], ACT.Tanh, scale=0.5).then_inc(e_tanh, 1)

            act.wait_ge(d_vec, 3)
            take_x(0, 0)
            take_x(1, 1)
            tanh(0, 0)

            def step(b, par):
                nxt = not static(b) or b + 1 < NB
                act.wait_ge(e_ht, b + 1)
                copy(e_hT, hT_ps).then_inc(e_htt, 1)
                if nxt:
                    tanh(b + 1, 1 - par)
                if not static(b) or b + 2 < NB:
                    take_x(b + 2, par)
                g = row_gate[:, b:b + 1] if static(b) else row_gate[:, bass.ds(b, 1)]
                for j in range(2):
                    act.wait_ge(e_pj, b * 2 + (j + 2))
                    settled(act)
                    copy(yb[:, par, j * 512:(j + 1) * 512], pj[j], g).then_inc(e_pjf, 1)
                act.wait_ge(e_pjf, b * 2 + 2)
                if not static(b) or b:
                    settled(act)
                    act.wait_ge(e_st, b * 16)
                act.dma_start(rows(yb_d, b), yb[:, par, :]).then_inc(e_st, 16)

            run_chunks(act, step, n=NB)
            act.wait_ge(e_st, 16 * NB)

        def e_vector(dve, ch):
            def index(b, par):
                src = src_i[:, b:b + 1] if static(b) else src_i[:, bass.ds(b, 1)]
                nc.vector.tensor_copy(xidx[:, par, :], src).then_inc(e_idx, 1)

            def hidden(b, par):
                dve.wait_ge(e_tanh, b + 1)
                if not static(b) or b:
                    dve.wait_ge(e_ht, b)
                ch.link(nc.vector.scalar_tensor_tensor(e_h, e_th, 1.0, gu_ps[par][:, 0:FE], ALU.add, ALU.mult))
                ch.wait()
                nc.vector.scalar_tensor_tensor(e_h, e_h, 0.5, gu_ps[par][:, FE:2 * FE], ALU.mult, ALU.mult).then_inc(e_hr, 1)

            dve.wait_ge(d_vec, 3)
            index(0, 0)
            index(1, 1)
            hidden(0, 0)

            def step(b, par):
                if not static(b) or b + 2 < NB:
                    dve.wait_ge(e_gath[par], done(b, par, 16))
                    index(b + 2, par)
                if not static(b) or b + 1 < NB:
                    hidden(b + 1, 1 - par)

            run_chunks(dve, step, ch, n=NB)

        def e_gpsimd(pool):
            def gather(b, par):
                pool.wait_ge(e_idx, b + 1)
                if not static(b) or b >= 2:
                    pool.wait_ge(e_tp, b - 1)
                settled(pool)
                nc.gpsimd.indirect_dma_start(out=xb[:, par, :], out_offset=None, in_=x3_d,
                                             in_offset=bass.IndirectOffsetOnAxis(ap=xidx[:, par, :], axis=0)).then_inc(e_gath[par], 16)

            pool.wait_ge(c_x3st, 16 * NC)
            gather(0, 0)
            gather(1, 1)

            def step(b, par):
                if not static(b) or b + 2 < NB:
                    gather(b + 2, par)

            run_chunks(pool, step, n=NB)

        def f_sync(sp):
            for c in range(3):
                sp.dma_start(f_x[:, c, :], rows(x3_d, c)).then_inc(f_xl, 16)
                sp.wait_ge(f_xl, 16 * (c + 1))

            def step(c, par, turn):
                sp.wait_ge(f_out, c + 1)
                sp.dma_start(rows(out, c), f_x[:, par, :]).then_inc(f_st, 16)
                if not static(c) or c + 3 < NC:
                    sp.wait_ge(f_st, c * 16 + 16)
                    settled(sp)
                    sp.wait_ge(f_xl, c * 16 + 48)
                    sp.dma_start(f_x[:, par, :], rows(x3_d, c + 3)).then_inc(f_xl, 16)

            run_thirds(sp, step)
            sp.wait_ge(f_st, 16 * NC)

        def f_gpsimd(pool):
            def gather(c, par):
                pool.wait_ge(f_idx, c + 1)
                if not static(c) or c >= 3:
                    pool.wait_ge(f_acc, c - 2)
                settled(pool)
                for k in range(2):
                    nc.gpsimd.indirect_dma_start(out=f_y[:, par, k, :], out_offset=None, in_=yb_d,
                                                 in_offset=bass.IndirectOffsetOnAxis(ap=yidx[:, par, k:k + 1], axis=0)).then_inc(f_g[par], 16)

            pool.wait_ge(e_st, 16 * NB)
            for c in range(3):
                gather(c, c)

            def step(c, par, turn):
                pool.wait_ge(f_rv, c + 1)
                nc.gpsimd.tensor_tensor(f_rstd, f_var, neg_half[:, 0:1], ALU.pow).then_inc(f_rr, 1)
                if not static(c) or c + 3 < NC:
                    gather(c + 3, par)

            run_thirds(pool, step)

        def f_vector(dve, ch):
            def seq(ins):
                ch.link(ins)
                ch.wait()

            both = dest_i.rearrange("p (k c) -> p c k", k=2)

            def index(c, par):
                src = both[:, c, :] if static(c) else both[:, bass.ds(c, 1), :].rearrange("p a k -> p (a k)")
                nc.vector.tensor_copy(yidx[:, par, :], src).then_inc(f_idx, 1)

            for c in range(3):
                index(c, c)

            def step(c, par, turn):
                x = f_x[:, par, :]
                dve.wait_ge(f_xl, c * 16 + 16)
                dve.wait_ge(f_g[par], turn * 32 + (f_g_from[par] + 32))
                seq(nc.vector.scalar_tensor_tensor(x, x, ALPHA, f_y[:, par, 0, :], ALU.mult, ALU.add))
                if not static(c) or c + 3 < NC:
                    index(c + 3, par)
                nc.vector.tensor_tensor(x, x, f_y[:, par, 1, :], ALU.add).then_inc(f_acc, 1)
                dve.wait_ge(f_acc, c + 1)
                for j in range(2):
                    ins = nc.vector.bn_stats(f_stats[:, j, :], x[:, j * 512:(j + 1) * 512])
                seq(ins)
                settled(dve)
                seq(nc.vector.bn_aggr(f_mv, f_stats.rearrange("p a b -> p (a b)")))
                nc.vector.tensor_scalar(f_var, f_mv[:, 1:2], LN_EPS, None, ALU.add).then_inc(f_rv, 1)
                seq(nc.vector.scalar_tensor_tensor(x, x, f_mv[:, 0:1], lnm_g, ALU.subtract, ALU.mult))
                dve.wait_ge(f_rr, c + 1)
                nc.vector.scalar_tensor_tensor(x, x, f_rstd, lnm_b, ALU.mult, ALU.add).then_inc(f_out, 1)

            run_thirds(dve, step, ch)

        block = ctx.enter_context(nc.Block())

        last = {"a": 1, "b": 2, "c": 3, "all": 4}[stop_after]

        @block.sync
        def _(sp):
            a_sync(sp, (lambda: b_sync(sp)) if last > 1 else None)
            a_sync_end(sp)
            if last > 1:
                b_sync_main(sp, (lambda: c_sync(sp)) if last > 2 else None)
                b_sync_end(sp)
            if last > 2:
                c_sync_main(sp, (lambda: e_sync_first(sp)) if last > 3 else None)
            if last > 3:
                e_sync(sp)
                f_sync(sp)

        @block.tensor
        def _(pe):
            for phase in (a_tensor, b_tensor, c_tensor, d_tensor, e_tensor)[:last if last < 4 else 5]:
                phase(pe)

        @block.scalar
        def _(act):
            for phase in (a_scalar, b_scalar, c_scalar, e_scalar)[:last]:
                phase(act)

        @block.vector
        def _(dve):
            ch = Chain(dve, s_dve)
            for phase in (a_vector, b_vector, c_vector, d_vector, e_vector, f_vector)[:last if last < 4 else 6]:
                phase(dve, ch)

        @block.gpsimd
        def _(pool):
            for phase in (a_gpsimd, b_gpsimd, c_gpsimd, e_gpsimd, f_gpsimd)[:last if last < 4 else 5]:
                phase(pool)


_SHAPES = {
    "x": (S, D), "mem": (MEM, D), "pre_norm_g": (D,), "post_norm_g": (D,), "mem_norm_g": (D,), "w_in": (D, IN1),
    "w_mem_kv": (D, 2 * MEM), "v_norm_g": (A_W,), "v_norm_b": (A_W,), "w_spatial": (4, P, P), "b_spatial": (4, P),
    "attn_sinks": (4,), "rel_bias": (SWA_BUCKETS, 4), "w_out": (D, D),
    "w_in_2": (D, IN2), "b_i_2": (LH,), "b_f_2": (LH,), "conv_qk_2": (CONV, D), "head_norm_g_2": (M_W,), "pool_w_2": (4, P, P),
    "pool_scale_2": (M_W,), "w_mix_out_2": (D, D), "ln_mix_g_2": (D,), "ln_mix_b_2": (D,),
    "mem_2": (MEM, D), "w_xq_2": (D, D), "w_xkv_2": (D, 2 * D), "w_xo_2": (D, D), "ln_x_g_2": (D,), "ln_x_b_2": (D,),
    "router_w_2": (D, NE), "router_bias_2": (NE,), "w_gate_2": (NE, D, FE), "w_up_2": (NE, D, FE), "w_down_2": (NE, FE, D),
    "ln_moe_g_2": (D,), "ln_moe_b_2": (D,),
}


def kernel(**inputs):
    import concourse.bacc as bacc
    from concourse.bass_utils import run_bass_kernel_spmd

    nc = bacc.Bacc("TRN2", target_bir_lowering=False, num_devices=1)
    arrays = {n: np.ascontiguousarray(np.asarray(inputs[n]).reshape(shape)) for n, shape in _SHAPES.items()}
    arrays["ident"] = np.eye(P, dtype=np.float32)
    for name, tables in (("tables", shape_constants()), ("tables2", mixer_constants()), ("tables3", routing_constants())):
        arrays[name] = np.ascontiguousarray(np.concatenate(list(tables.values()), 1))
    aps = {n: nc.dram_tensor(n, a.shape, mybir.dt.from_np(a.dtype), kind="ExternalInput").ap() for n, a in arrays.items()}
    out = nc.dram_tensor("result", (S, D), F32, kind="ExternalOutput").ap()
    build(nc, aps, out)
    r = run_bass_kernel_spmd(nc, [arrays], core_ids=[0])
    return r.results[0]["result"].reshape(1, S, D)
```
